# Optimizing a Trainium2 kernel written in Bass

```python
import jax, jax.numpy as jnp
from jax import lax
import numpy as np

D_MODEL = 2048
BATCH = 1
SEQ = 256
DEPTH = 2

CHUNK = 64
N_MIXERS = 3
N_RWKV = (DEPTH + 2) // N_MIXERS
N_RET = (DEPTH + 1) // N_MIXERS
N_MLSTM = DEPTH // N_MIXERS
NORM_EPS = 1e-6

RW_HEAD = 64
RW_HEADS = D_MODEL // RW_HEAD
RW_DECAY_LORA = max(32, int(round(1.8 * D_MODEL ** 0.5 / 32)) * 32)
RW_AAA_LORA = max(32, int(round(1.8 * D_MODEL ** 0.5 / 32)) * 32)
RW_MV_LORA = max(32, int(round(1.3 * D_MODEL ** 0.5 / 32)) * 32)
RW_GATE_LORA = max(32, int(round(0.6 * D_MODEL ** 0.8 / 32)) * 32)
RW_GN_EPS = 64e-5

RET_HEADS = 8
RET_DK = D_MODEL // RET_HEADS
RET_DV = 2 * D_MODEL // RET_HEADS
ROPE_BASE = 10000.0

ML_HEADS = 4
ML_DQK = D_MODEL // 2 // ML_HEADS
ML_DV = D_MODEL // ML_HEADS
ML_GATE_CAP = 15.0

D_FF = -(-8 * D_MODEL // (3 * 256)) * 256

kernel_name = 'hybrid_rwkv7_retention_mlstm_trunk'

F32 = jnp.float32

def _rms_norm(x, g):
    xf = x.astype(F32)
    y = xf * lax.rsqrt(jnp.mean(xf * xf, axis=-1, keepdims=True) + NORM_EPS)
    return (y * g.astype(F32)).astype(x.dtype)

def _head_layer_norm(y, eps):
    mean = jnp.mean(y, axis=-1, keepdims=True)
    yc = y - mean
    return yc * lax.rsqrt(jnp.mean(yc * yc, axis=-1, keepdims=True) + eps)

def _to_chunks(t):
    b, s = t.shape[:2]
    return jnp.moveaxis(t.reshape(b, s // CHUNK, CHUNK, *t.shape[2:]), 1, 0)

def _from_chunks(t):
    t = jnp.moveaxis(t, 0, 1)
    return t.reshape(t.shape[0], t.shape[1] * t.shape[2], *t.shape[3:])

def _rotary_tables(positions):
    inv_freq = 1.0 / (ROPE_BASE ** jnp.linspace(0.0, 1.0, RET_DK // 2, dtype=F32))
    ang = positions.astype(F32)[..., None] * inv_freq
    return jnp.cos(ang), jnp.sin(ang)

def _rotary(t, cos, sin):
    half = t.shape[-1] // 2
    t1, t2 = t[..., :half], t[..., half:]
    c = cos[:, :, None, :].astype(t.dtype)
    s = sin[:, :, None, :].astype(t.dtype)
    return jnp.concatenate([t1 * c - t2 * s, t1 * s + t2 * c], axis=-1)

def _rwkv7_scan(r, w, k, v, a, b):
    bsz, _, nh, n = r.shape

    def step(st, inp):
        r_t, w_t, k_t, v_t, a_t, b_t = inp
        sa = jnp.einsum('bhvk,bhk->bhv', st, a_t)
        st = st * w_t[:, :, None, :] + sa[..., None] * b_t[:, :, None, :] + v_t[..., None] * k_t[:, :, None, :]
        return st, jnp.einsum('bhvk,bhk->bhv', st, r_t)

    xs = tuple(jnp.moveaxis(t, 1, 0) for t in (r, w, k, v, a, b))
    _, ys = lax.scan(step, jnp.zeros((bsz, nh, n, n), F32), xs)
    return jnp.moveaxis(ys, 0, 1)

def _rwkv7_mix(h, v_first, mu, w_rkv, w0, w1, w2, a0, a1, a2, g1, g2, k_k, k_a, r_k, ln_w, ln_b, w_o, vres):
    b, s, d = h.shape
    xx = jnp.pad(h, ((0, 0), (1, 0), (0, 0)))[:, :-1] - h
    xr, xw, xk, xv, xa, xg = (h + xx * mu[j] for j in range(6))
    r = xr @ w_rkv[0]
    k = xk @ w_rkv[1]
    v = xv @ w_rkv[2]
    w_log = -jax.nn.softplus(-(w0 + jnp.tanh(xw @ w1) @ w2)) - 0.5
    decay = jnp.exp(-jnp.exp(w_log.astype(F32)))
    a = jax.nn.sigmoid(a0 + (xa @ a1) @ a2)
    if vres is not None:
        v0, v1, v2 = vres
        v = v + (v_first - v) * jax.nn.sigmoid(v0 + (xv @ v1) @ v2)
    g = jax.nn.sigmoid(xg @ g1) @ g2

    def heads(t):
        return t.reshape(b, s, RW_HEADS, RW_HEAD).astype(F32)

    kk = heads(k * k_k)
    kk = kk / jnp.maximum(jnp.sqrt(jnp.sum(kk * kk, axis=-1, keepdims=True)), 1e-12)
    k = k * (1 + (a - 1) * k_a)
    rh, kh, vh, ah = heads(r), heads(k), heads(v), heads(a)
    y = _rwkv7_scan(rh, heads(decay), kh, vh, -kk, kk * ah)
    yn = _head_layer_norm(y, RW_GN_EPS).reshape(b, s, d) * ln_w.astype(F32) + ln_b.astype(F32)
    bonus = (jnp.sum(rh * kh * r_k.astype(F32), axis=-1, keepdims=True) * vh).reshape(b, s, d)
    out = ((yn + bonus).astype(h.dtype) * g) @ w_o
    return out, v

def _retention_scan(q, k, v, log_gamma):
    bsz, _, nh, dk = q.shape
    dv = v.shape[-1]
    idx = jnp.arange(CHUNK, dtype=F32)
    diff = idx[:, None] - idx[None, :]
    causal = diff >= 0
    intra = jnp.where(causal, jnp.exp(log_gamma[:, None, None] * jnp.where(causal, diff, 0.0)), 0.0)
    xi = jnp.exp(log_gamma[:, None] * (idx + 1.0)).T[None, :, :, None]
    zeta = jnp.exp(log_gamma[:, None] * (CHUNK - 1.0 - idx)).T[None, :, :, None]
    g_chunk = jnp.exp(log_gamma * CHUNK)[None, :, None, None]

    def step(r_st, inp):
        qc, kc, vc = inp
        sc = jnp.einsum('bihd,bjhd->bhij', qc, kc) * intra
        inner = jnp.einsum('bhij,bjhe->bihe', sc, vc)
        cross = jnp.einsum('bihd,bhde->bihe', qc, r_st) * xi
        r_st = g_chunk * r_st + jnp.einsum('bjhd,bjhe->bhde', kc * zeta, vc)
        return r_st, inner + cross

    xs = (_to_chunks(q), _to_chunks(k), _to_chunks(v))
    _, ys = lax.scan(step, jnp.zeros((bsz, nh, dk, dv), F32), xs)
    return _from_chunks(ys)

def _retention_mix(h, cos, sin, w_in, gn_w, w_out):
    b, s, d = h.shape
    proj = h @ w_in
    q = proj[..., :d].reshape(b, s, RET_HEADS, RET_DK)
    k = proj[..., d:2 * d].reshape(b, s, RET_HEADS, RET_DK)
    v = proj[..., 2 * d:4 * d].reshape(b, s, RET_HEADS, RET_DV)
    g = proj[..., 4 * d:]
    q = _rotary(q, cos, sin)
    k = _rotary(k, cos, sin) * (RET_DK ** -0.5)
    log_gamma = jnp.log1p(-jnp.exp2(-5.0 - jnp.arange(RET_HEADS, dtype=F32)))
    y = _retention_scan(q.astype(F32), k.astype(F32), v.astype(F32), log_gamma)
    yn = _head_layer_norm(y, NORM_EPS).reshape(b, s, 2 * d) * gn_w.astype(F32)
    return (jax.nn.silu(g) * yn.astype(h.dtype)) @ w_out

def _mlstm_scan(q, k, v, i_pre, log_f):
    bsz, _, nh, dk = q.shape
    dv = v.shape[-1]
    causal = jnp.tril(jnp.ones((CHUNK, CHUNK), dtype=bool))

    def step(carry, inp):
        c_st, n_st, m_st = carry
        qc, kc, vc, ic, fc = inp
        bcum = jnp.moveaxis(jnp.cumsum(fc, axis=1), 1, 2)
        ig = jnp.moveaxis(ic, 1, 2)
        log_d = jnp.where(causal, bcum[..., :, None] - bcum[..., None, :] + ig[..., None, :], -jnp.inf)
        log_inter = bcum + m_st[..., None]
        m_t = jnp.maximum(log_inter, jnp.max(log_d, axis=-1))
        dmat = jnp.exp(log_d - m_t[..., None])
        w_inter = jnp.exp(log_inter - m_t)
        sc = jnp.einsum('blhd,bshd->bhls', qc, kc) * dmat
        num = jnp.einsum('bhls,bshe->bhle', sc, vc) + w_inter[..., None] * jnp.einsum('blhd,bhde->bhle', qc, c_st)
        dot = jnp.sum(sc, axis=-1) + w_inter * jnp.einsum('blhd,bhd->bhl', qc, n_st)
        hc = num / jnp.maximum(jnp.abs(dot), jnp.exp(-m_t))[..., None]
        m_new = m_t[..., -1]
        w_s = jnp.exp(bcum[..., -1:] - bcum + ig - m_new[..., None])
        dec = jnp.exp(bcum[..., -1] + m_st - m_new)
        c_st = dec[..., None, None] * c_st + jnp.einsum('bhs,bshd,bshe->bhde', w_s, kc, vc)
        n_st = dec[..., None] * n_st + jnp.einsum('bhs,bshd->bhd', w_s, kc)
        return (c_st, n_st, m_new), jnp.moveaxis(hc, 1, 2)

    init = (jnp.zeros((bsz, nh, dk, dv), F32), jnp.zeros((bsz, nh, dk), F32), jnp.zeros((bsz, nh), F32))
    xs = tuple(_to_chunks(t) for t in (q, k, v, i_pre, log_f))
    _, ys = lax.scan(step, init, xs)
    return _from_chunks(ys)

def _mlstm_mix(h, w_in, b_if, hn_w, w_out):
    b, s, d = h.shape
    dq = ML_HEADS * ML_DQK
    proj = h @ w_in
    q = proj[..., :dq].reshape(b, s, ML_HEADS, ML_DQK)
    k = proj[..., dq:2 * dq].reshape(b, s, ML_HEADS, ML_DQK) * (ML_DQK ** -0.5)
    v = proj[..., 2 * dq:2 * dq + d].reshape(b, s, ML_HEADS, ML_DV)
    o = proj[..., 2 * dq + d:2 * dq + 2 * d]
    gates = proj[..., 2 * dq + 2 * d:].astype(F32) + b_if.astype(F32)
    gates = ML_GATE_CAP * jnp.tanh(gates / ML_GATE_CAP)
    i_pre = gates[..., :ML_HEADS]
    log_f = jax.nn.log_sigmoid(gates[..., ML_HEADS:])
    y = _mlstm_scan(q.astype(F32), k.astype(F32), v.astype(F32), i_pre, log_f)
    yf = y * lax.rsqrt(jnp.mean(y * y, axis=-1, keepdims=True) + NORM_EPS)
    yn = yf.reshape(b, s, d) * hn_w.astype(F32)
    return (jax.nn.sigmoid(o) * yn.astype(h.dtype)) @ w_out

def _swiglu(h, w1, w3, w2):
    return (jax.nn.silu(h @ w1) * (h @ w3)) @ w2

def setup_inputs(seed: int = 0) -> dict:
    key = jax.random.key(seed)
    keys = iter(jax.random.split(key, 40))
    D = D_MODEL

    def nrm(shape, scale):
        return jax.random.normal(next(keys), shape, F32) * scale

    def gain(shape):
        return 1.0 + nrm(shape, 0.02)

    x = nrm((BATCH, SEQ, D), 1.0)
    offs = CHUNK * jax.random.randint(next(keys), (BATCH,), 0, 64, dtype=jnp.int32)
    positions = offs[:, None] + jnp.arange(SEQ, dtype=jnp.int32)[None, :]
    nr, nv = N_RWKV, max(N_RWKV - 1, 1)
    inp = {
        'x': x,
        'positions': positions,
        'norm_mix': gain((DEPTH, D)),
        'norm_ffn': gain((DEPTH, D)),
        'norm_final': gain((D,)),
        'rw_mu': jax.random.uniform(next(keys), (nr, 6, D), F32),
        'rw_w_rkv': nrm((nr, 3, D, D), D ** -0.5),
        'rw_w0': jax.random.uniform(next(keys), (nr, D), F32, -6.0, -1.0),
        'rw_w1': nrm((nr, D, RW_DECAY_LORA), D ** -0.5),
        'rw_w2': nrm((nr, RW_DECAY_LORA, D), 0.1 * RW_DECAY_LORA ** -0.5),
        'rw_a0': nrm((nr, D), 0.1),
        'rw_a1': nrm((nr, D, RW_AAA_LORA), D ** -0.5),
        'rw_a2': nrm((nr, RW_AAA_LORA, D), 0.5 * RW_AAA_LORA ** -0.5),
        'rw_g1': nrm((nr, D, RW_GATE_LORA), D ** -0.5),
        'rw_g2': nrm((nr, RW_GATE_LORA, D), RW_GATE_LORA ** -0.5),
        'rw_k_k': 0.85 + nrm((nr, D), 0.02),
        'rw_k_a': gain((nr, D)),
        'rw_r_k': nrm((nr, RW_HEADS, RW_HEAD), 0.1),
        'rw_ln_w': gain((nr, D)),
        'rw_ln_b': nrm((nr, D), 0.02),
        'rw_w_o': nrm((nr, D, D), D ** -0.5),
        'rw_v0': gain((nv, D)),
        'rw_v1': nrm((nv, D, RW_MV_LORA), D ** -0.5),
        'rw_v2': nrm((nv, RW_MV_LORA, D), 0.5 * RW_MV_LORA ** -0.5),
        'ret_w_in': nrm((N_RET, D, 6 * D), D ** -0.5),
        'ret_gn_w': gain((N_RET, 2 * D)),
        'ret_w_out': nrm((N_RET, 2 * D, D), (2 * D) ** -0.5),
        'ml_w_in': nrm((N_MLSTM, D, 3 * D + 2 * ML_HEADS), D ** -0.5),
        'ml_b_if': jnp.concatenate([nrm((N_MLSTM, ML_HEADS), 0.5), 3.0 + nrm((N_MLSTM, ML_HEADS), 0.5)], axis=-1),
        'ml_hn_w': gain((N_MLSTM, D)),
        'ml_w_out': nrm((N_MLSTM, D, D), D ** -0.5),
        'ffn_w1': nrm((DEPTH, D, D_FF), D ** -0.5),
        'ffn_w3': nrm((DEPTH, D, D_FF), D ** -0.5),
        'ffn_w2': nrm((DEPTH, D_FF, D), D_FF ** -0.5),
    }
    return inp

def reference(x, positions, norm_mix, norm_ffn, norm_final, rw_mu, rw_w_rkv, rw_w0, rw_w1, rw_w2,
              rw_a0, rw_a1, rw_a2, rw_g1, rw_g2, rw_k_k, rw_k_a, rw_r_k, rw_ln_w, rw_ln_b, rw_w_o,
              rw_v0, rw_v1, rw_v2, ret_w_in, ret_gn_w, ret_w_out, ml_w_in, ml_b_if, ml_hn_w, ml_w_out,
              ffn_w1, ffn_w3, ffn_w2):
    cos, sin = _rotary_tables(positions)
    v_first = None
    for i in range(DEPTH):
        kind, j = i % N_MIXERS, i // N_MIXERS
        h = _rms_norm(x, norm_mix[i])
        if kind == 0:
            vres = None if j == 0 else (rw_v0[j - 1], rw_v1[j - 1], rw_v2[j - 1])
            y, v = _rwkv7_mix(h, v_first, rw_mu[j], rw_w_rkv[j], rw_w0[j], rw_w1[j], rw_w2[j],
                              rw_a0[j], rw_a1[j], rw_a2[j], rw_g1[j], rw_g2[j], rw_k_k[j], rw_k_a[j],
                              rw_r_k[j], rw_ln_w[j], rw_ln_b[j], rw_w_o[j], vres)
            if j == 0:
                v_first = v
        elif kind == 1:
            y = _retention_mix(h, cos, sin, ret_w_in[j], ret_gn_w[j], ret_w_out[j])
        else:
            y = _mlstm_mix(h, ml_w_in[j], ml_b_if[j], ml_hn_w[j], ml_w_out[j])
        x = x + y
        x = x + _swiglu(_rms_norm(x, norm_ffn[i]), ffn_w1[i], ffn_w3[i], ffn_w2[i])
    return _rms_norm(x, norm_final)


_drawn_inputs = setup_inputs


def setup_inputs(seed=0):
    import zlib

    import numpy as np

    out = dict(_drawn_inputs(seed))
    spreads = {}
    factors = {'norm_ffn': 2.692,
     'norm_final': 2.862,
     'rw_w1': 8.0,
     'rw_w2': 8.0,
     'rw_k_k': 5.242,
     'rw_k_a': 3.575,
     'rw_ln_w': 4.056,
     'rw_ln_b': 4.342,
     'ret_gn_w': 6.132}
    for name, (base, spread) in spreads.items():
        noise = np.random.default_rng([zlib.crc32(name.encode()), seed]).standard_normal(out[name].shape)
        drawn = base * np.exp(spread * noise) if base else spread * noise
        out[name] = __import__('jax').numpy.asarray(drawn.astype(out[name].dtype))
    for name, factor in factors.items():
        out[name] = (out[name] * factor).astype(out[name].dtype)
    return out
```

```python
from contextlib import ExitStack

import numpy as np

import concourse.bass as bass
from concourse import mybir

ALU = mybir.AluOpType
ACT = mybir.ActivationFunctionType
AX_X = mybir.AxisListType.X
F32 = mybir.dt.float32
F32R = mybir.dt.float32r
I32 = mybir.dt.int32

P = 128
T = 256
D = 2048
DT = D // P
F = 5632
FT = F // P
CHUNK = 64
NC = T // CHUNK
LORA = 96
GLORA = 256
RET_HEADS = 8
RET_DK = D // RET_HEADS
RET_DV = 2 * D // RET_HEADS
ROPE_BASE = 10000.0
NORM_EPS = 1e-6
RW_GN_EPS = 64e-5
RW_HEAD = 64
PAIRS = D // P
UNIT = 2048
UP_BLOCKS = F // 512

PARAM_ROWS = {}
_row = 0
for _name, _n in (("norm_mix", 2 * DT), ("norm_ffn", 2 * DT), ("norm_final", DT), ("rw_mu", 6 * DT), ("rw_w0", DT),
                  ("rw_a0", DT), ("rw_k_k", DT), ("rw_k_a", DT), ("rw_r_k", DT), ("rw_ln_w", DT), ("rw_ln_b", DT),
                  ("ret_gn_w", 2 * DT)):
    PARAM_ROWS[_name] = (_row, _n)
    _row += _n
PARAM_BLOCKS = -(-_row // P)

TABLE_COLS = {}
_col = 0
for _name, _n in (("ident", P), ("ones", P), ("head_ones", P), ("ident2", 64), ("pair_mask", 2), ("strict_mask", 64),
                  ("chunk_mask", 2 * 2 * 64), ("scan_mask", T), ("inv_freq", 1), ("ret_decay", RET_HEADS * T)):
    TABLE_COLS[_name] = (_col, _n)
    _col += _n
TABLE_WIDTH = _col


def shape_table():
    t = np.zeros((P, TABLE_WIDTH), np.float32)

    def put(name, value):
        c, n = TABLE_COLS[name]
        t[:, c:c + n] = np.asarray(value, np.float32).reshape(P, n)

    p = np.arange(P)
    half, s = p // 64, p % 64
    tt = np.arange(64)
    put("ident", np.eye(P))
    put("ones", np.ones((P, P)))
    put("head_ones", half[:, None] == half[None, :])
    put("ident2", s[:, None] == tt[None, :])
    pair = half[:, None] == np.arange(2)[None, :]
    put("pair_mask", pair)
    causal = np.stack([s[:, None] < tt[None, :], s[:, None] <= tt[None, :]], 1)
    put("strict_mask", causal[:, 0])
    put("chunk_mask", causal[:, :, None, :] * pair[:, None, :, None])
    put("scan_mask", np.broadcast_to((np.arange(T) % CHUNK != 0)[None, :], (P, T)))
    put("inv_freq", 1.0 / ROPE_BASE ** (np.arange(P) / (RET_DK // 2 - 1)))
    gamma = 1.0 - 2.0 ** (-5.0 - np.arange(RET_HEADS))
    dist = np.arange(T)[None, :] - p[:, None]
    decay = np.where(dist[:, None, :] >= 0, gamma[None, :, None] ** np.maximum(dist, 0)[:, None, :], 0.0)
    put("ret_decay", decay * RET_DK ** -0.5)
    return t


def trunk_program(nc, x, positions, norm_mix, norm_ffn, norm_final, rw_mu, rw_w_rkv, rw_w0, rw_w1, rw_w2,
                  rw_a0, rw_a1, rw_a2, rw_g1, rw_g2, rw_k_k, rw_k_a, rw_r_k, rw_ln_w, rw_ln_b, rw_w_o,
                  ret_w_in, ret_gn_w, ret_w_out, ffn_w1, ffn_w3, ffn_w2, table, out):
    units = {}
    total = 0
    for name, n in (("decay", 2), ("rate", 2), ("key", 16), ("rec", 16), ("val", 16), ("gate", 4), ("rw_out", DT),
                    ("up0", 8 * UP_BLOCKS), ("down0", FT), ("ret", 12 * RET_HEADS), ("ret_out", 2 * DT),
                    ("up1", 8 * UP_BLOCKS), ("down1", FT)):
        units[name] = total
        total += n

    w1s = [ffn_w1[l].rearrange("(kt p) n -> p kt n", p=P) for l in range(2)]
    w3s = [ffn_w3[l].rearrange("(kt p) n -> p kt n", p=P) for l in range(2)]
    w2s = [ffn_w2[l].rearrange("(kt p) n -> p kt n", p=P) for l in range(2)]
    ret_in = ret_w_in[0].rearrange("(kt p) n -> p kt n", p=P)
    ret_out = ret_w_out[0].rearrange("(kt p) n -> p kt n", p=P)
    x_dram = x[0].rearrange("(tt p) n -> p tt n", p=P)
    out_dram = out[0].rearrange("(tt p) n -> p tt n", p=P)

    base = 16512
    KB = 1024

    def place(name, shape, offset, dtype=F32):
        return nc.alloc_sbuf_tensor_at(name, shape, dtype, offset=base + offset)

    x_res = place("x_res", [P, DT, T], 0)
    raw = place("raw", [P, 2, UNIT], 16 * KB)
    w_hi = place("w_hi", [P, 2, UNIT], 32 * KB, F32R)
    w_lo = place("w_lo", [P, 2, UNIT], 48 * KB, F32R)
    x_hi = place("x_hi", [P, DT, T], 64 * KB, F32R)
    x_lo = place("x_lo", [P, DT, T], 80 * KB, F32R)
    work = place("work", [P, 2, 4, T], 96 * KB)
    small = 104 * KB
    tab_cols = TABLE_COLS["ret_decay"][0]
    tab = place("tab", [P, tab_cols], small)
    small += 4 * tab_cols + 28
    small -= small % 32
    prm = place("prm", [P, PARAM_BLOCKS * P], small)
    small += 4 * PARAM_BLOCKS * P
    rstd = place("rstd", [P, T], small)
    rvar = place("rvar", [P, T], small + KB)
    rvar_at = small + KB
    small += 2 * KB
    zone = small + (-small) % 32
    hid_hi = place("hid_hi", [P, FT, T], zone, F32R)
    hid_lo = place("hid_lo", [P, FT, T], zone + 44 * KB, F32R)
    x_rows = place("x_rows", [P, 2, D], zone)
    param_rows = place("param_rows", [P, PARAM_BLOCKS, P], zone + 16 * KB)
    out_rows = place("out_rows", [P, 2, D], zone)
    ret_hi = place("ret_hi", [P, 2 * DT, T], zone, F32R)
    ret_lo = place("ret_lo", [P, 2 * DT, T], zone + 32 * KB, F32R)
    z = zone + 64 * KB
    ret_decay = place("ret_decay", [P, RET_HEADS, T], z)
    cos = place("cos", [P, T], z + 8 * KB)
    sin = place("sin", [P, T], z + 9 * KB)
    qk_rot = place("qk_rot", [P, 2, 2, T], z + 10 * KB)
    v_rows = place("v_rows", [P, 2, RET_DV], z + 14 * KB)
    probs = place("probs", [P, 3 * P], z + 18 * KB)
    silu_g = place("silu_g", [P, 4, T], z + 20 * KB)
    y_head = place("y_head", [P, 4, T], z + 24 * KB)
    assert base + z + 28 * KB <= nc.sbuf_usable_end and base + zone + 88 * KB <= nc.sbuf_usable_end
    pos_i = place("pos_i", [P, T], z + 14 * KB, I32)
    rot_a, rot_b, rot_c, rot_d = (work[:, k // 2, 2 * (k % 2):2 * (k % 2) + 2] for k in range(4))

    h_in = place("h_in", [P, DT, T + 1], zone)
    out_gate = place("out_gate", [P, DT, T], zone)
    quad_at = zone + 4 * DT * (T + 1)
    quad = place("quad", [P, 4, DT, T], quad_at)
    att_hi = place("att_hi", [P, DT, T], quad_at, F32R)
    att_lo = place("att_lo", [P, DT, T], quad_at + 16 * KB, F32R)
    solve_t = place("solve_t", [P, 1024], quad_at + 32 * KB)
    bonus = place("bonus", [P, DT, T], quad_at + 32 * KB)
    inv_at = quad_at + 64 * KB
    assert base + inv_at + 16 * KB <= nc.sbuf_usable_end
    prep_t = place("prep_t", [P, 4, T], inv_at)
    b_wide = place("b_wide", [P, 2, NC, 2, 64], inv_at + 4 * KB)
    tri_rows = place("tri_rows", [P, 2, NC, 64], inv_at + 8 * KB)
    tri = place("tri", [P, 64, 64], inv_at)
    inv_t = place("inv_t", [P, PAIRS * NC, 64], inv_at)
    lora_hi = place("lora_hi", [P, 1, T], inv_at + 12 * KB, F32R)
    lora_lo = place("lora_lo", [P, 1, T], inv_at + 13 * KB, F32R)
    glora_hi = place("glora_hi", [P, 2, T], 96 * KB, F32R)
    glora_lo = place("glora_lo", [P, 2, T], 98 * KB, F32R)
    chunk_decay = place("chunk_decay", [P, PAIRS, NC], rvar_at)
    v_feat = place("v_feat", [P, DT, T], 64 * KB)
    y_all = place("y_all", [P, PAIRS, NC, 64], 80 * KB)
    scan_at = 32 * KB
    quad_wide = place("quad_wide", [P, 4, 4, 2, 64], scan_at)
    v_wide = place("v_wide", [P, 4, 2, 64], scan_at + 8 * KB)
    inv_wide = place("inv_wide", [P, 4, 2, 64], scan_at + 10 * KB)
    mix_wide = place("mix_wide", [P, 4, 3, 2, 64], scan_at + 12 * KB)
    kbv_rows = place("kbv_rows", [P, 4, 2 * P + 64], scan_at + 18 * KB)
    x_stack = place("x_stack", [P, 4, 64], scan_at + 23 * KB)
    u_stack = place("u_stack", [P, 4, 64], scan_at + 24 * KB)
    state = place("state", [P, PAIRS, 64], scan_at + 25 * KB)
    state_dec = place("state_dec", [P, 4, 64], scan_at + 29 * KB)
    y_wide = place("y_wide", [P, 2, NC, 2, 64], scan_at)
    y_mean = place("y_mean", [P, 64], scan_at + 8 * KB)
    y_inv = place("y_inv", [P, 64], scan_at + 9 * KB)
    y_scale = place("y_scale", [P, 64, 2], scan_at + 10 * KB)

    def const(name):
        c, n = TABLE_COLS[name]
        return tab[:, c:c + n]

    def param(name, tile):
        r, _ = PARAM_ROWS[name]
        return prm[:, r + tile:r + tile + 1]

    ident, ones = const("ident"), const("ones")

    with ExitStack() as ctx:
        def sem(name):
            return ctx.enter_context(nc.semaphore(name))

        acc = ctx.enter_context(nc.psum_tensor("acc", [P, 8, 512], F32))

        w_loaded = [sem("w_loaded0"), sem("w_loaded1")]
        hi_done = sem("hi_done")
        lo_done = sem("lo_done")
        unit_used = sem("unit_used")
        tables_in = sem("tables_in")
        rows_in = sem("rows_in")
        params_t = sem("params_t")
        params_ready = sem("params_ready")
        x_turned = sem("x_turned")
        x_ready = sem("x_ready")
        norm_sq = sem("norm_sq")
        norm_stat = sem("norm_stat")
        norm_var = sem("norm_var")
        norm_eps_added = sem("norm_eps_added")
        norm_rstd = sem("norm_rstd")
        hn_ready = sem("hn_ready")
        hn_hi = sem("hn_hi")
        hn_lo = sem("hn_lo")
        up_free = sem("up_free")
        silu_done = sem("silu_done")
        hid_hi_done = sem("hid_hi_done")
        hid_lo_done = sem("hid_lo_done")
        out_turned = sem("out_turned")
        out_ready = sem("out_ready")
        out_stored = sem("out_stored")
        pos_in = sem("pos_in")
        decay_in = sem("decay_in")
        rope_step = sem("rope_step")
        rope_sin = sem("rope_sin")
        rope_ready = sem("rope_ready")
        rot_mul = sem("rot_mul")
        rot_done = sem("rot_done")
        v_evac = sem("v_evac")
        silu_g_done = sem("silu_g_done")
        scores_done = sem("scores_done")
        probs_done = sem("probs_done")
        y_done = sem("y_done")
        y_evac = sem("y_evac")
        mean_done = sem("mean_done")
        centred = sem("centred")
        y_sq = sem("y_sq")
        var_done = sem("var_done")
        y_eps_added = sem("y_eps_added")
        y_var = sem("y_var")
        y_rstd = sem("y_rstd")
        y_scaled = sem("y_scaled")
        gated = sem("gated")
        ret_hi_done = sem("ret_hi_done")
        ret_lo_done = sem("ret_lo_done")

        def load_unit(sp, n, src, shape, off=0, parts=P):
            if n >= 2:
                sp.wait_ge(lo_done, n - 1 + off)
            dst = raw[0:parts, n % 2, 0:shape[0] * shape[1]].rearrange("p (k n) -> p k n", k=shape[0])
            sp.dma_start(dst, src).then_inc(w_loaded[n % 2], 16)

        def split_hi(act, n, off=0, parts=P, width=UNIT):
            act.wait_ge(w_loaded[n % 2], 16 * (n // 2 + 1) + 8 * off)
            if n >= 2:
                act.wait_ge(unit_used, n - 1 + off)
            nc.scalar.activation(w_hi[0:parts, n % 2, 0:width], raw[0:parts, n % 2, 0:width],
                                 ACT.Copy).then_inc(hi_done, 1)

        def split_lo(dve, n, off=0, parts=P, width=UNIT):
            dve.wait_ge(hi_done, n + 1 + off)
            nc.vector.tensor_tensor(w_lo[0:parts, n % 2, 0:width], raw[0:parts, n % 2, 0:width],
                                    w_hi[0:parts, n % 2, 0:width].bitcast(F32), ALU.subtract).then_inc(lo_done, 1)

        def unit_product(pe, n, shape, xs, tile_out, first, last, off=0, parts=P):
            pe.wait_ge(lo_done, n + 1 + off)
            rows, cols = shape
            hi = w_hi[0:parts, n % 2, 0:rows * cols].rearrange("p (k n) -> p k n", k=rows)
            lo = w_lo[0:parts, n % 2, 0:rows * cols].rearrange("p (k n) -> p k n", k=rows)
            for k in range(rows):
                a_hi, a_lo = xs(k)
                for f in range(-(-cols // P)):
                    c = slice(f * P, min((f + 1) * P, cols))
                    for m, (w, a) in enumerate(((hi, a_hi), (hi, a_lo), (lo, a_hi))):
                        mm = nc.tensor.matmul(tile_out(f), w[:, k, c], a,
                                              start=(first and k == 0 and m == 0 and f % 2 == 0),
                                              stop=(last and k == rows - 1 and m == 2), skip_group_check=True)
            mm.then_inc(unit_used, 1)

        def x_tiles(k0):
            return lambda k: (x_hi[:, k0 + k, :], x_lo[:, k0 + k, :])

        def bank_tile(b, f):
            if isinstance(b, int):
                return acc[:, b + f // 2, T * (f % 2):T * (f % 2) + T]
            return acc[:, bass.ds(b + f // 2, 1), T * (f % 2):T * (f % 2) + T].rearrange("p a t -> p (a t)")

        def norm_act(act, q):
            for j in range(4):
                act.wait_ge(x_ready, 4 * q + j + 1)
                if j >= 2:
                    act.wait_ge(norm_stat, 4 * q + j - 1)
                nc.scalar.activation(work[:, j % 2], x_res[:, 4 * j:4 * j + 4], ACT.Square).then_inc(norm_sq, 1)
            act.wait_ge(norm_var, q + 1)
            nc.scalar.activation(rstd[:], rvar[:], ACT.Sqrt).then_inc(norm_rstd, 1)

        def norm_pe(pe, q):
            for j in range(4):
                pe.wait_ge(norm_sq, 4 * q + j + 1)
                for k in range(4):
                    mm = nc.tensor.matmul(acc[:, 7, 0:T], ones, work[:, j % 2, k], start=(j == 0 and k == 0),
                                          stop=(j == 3 and k == 3))
                mm.then_inc(norm_stat, 1)

        def norm_dve(dve, q):
            dve.wait_ge(norm_stat, 4 * q + 4)
            nc.vector.tensor_scalar(rvar[:], acc[:, 7, 0:T], 1.0 / D, NORM_EPS, ALU.mult,
                                    ALU.add).then_inc(norm_eps_added, 1)
            dve.wait_ge(norm_eps_added, q + 1)
            nc.vector.reciprocal(rvar[:], rvar[:]).then_inc(norm_var, 1)
            dve.wait_ge(norm_rstd, q + 1)

        def norm_group(j, gain, gain_tile):
            for k in range(4):
                last = nc.vector.scalar_tensor_tensor(out=work[:, j % 2, k], in0=x_res[:, 4 * j + k],
                                                      scalar=param(gain, gain_tile + 4 * j + k), in1=rstd[:],
                                                      op0=ALU.mult, op1=ALU.mult)
            return last

        def fill_act(act, i):
            for j in range(4):
                act.wait_ge(hn_ready, 4 * i + j + 1)
                nc.scalar.activation(x_hi[:, 4 * j:4 * j + 4], work[:, j % 2], ACT.Copy).then_inc(hn_hi, 1)

        def fill_dve(dve, i, group):
            def low(j):
                dve.wait_ge(hn_hi, 4 * i + j + 1)
                nc.vector.tensor_tensor(x_lo[:, 4 * j:4 * j + 4], work[:, j % 2],
                                        x_hi[:, 4 * j:4 * j + 4].bitcast(F32), ALU.subtract).then_inc(hn_lo, 1)

            for j in range(4):
                if j >= 2:
                    low(j - 2)
                    dve.wait_ge(hn_lo, 4 * i + j - 1)
                group(j).then_inc(hn_ready, 1)
            low(2)
            low(3)
            dve.wait_ge(hn_lo, 4 * i + 4)

        def up_sp(sp, l):
            n0 = units[f"up{l}"]
            with sp.Fori(0, UP_BLOCKS) as i:
                for u in range(8):
                    w = (w1s, w3s)[u // 4][l]
                    load_unit(sp, n0 + u, w[:, 4 * (u % 4):4 * (u % 4) + 4, bass.ds(i * 512, 512)], (4, 512), off=8 * i)

        def up_act(act, l):
            n0 = units[f"up{l}"]

            def block(i, behind):
                off = 8 * i
                split_hi(act, n0, off)
                split_hi(act, n0 + 1, off)
                if behind:
                    silu(i - 1)
                split_hi(act, n0 + 2, off)
                split_hi(act, n0 + 3, off)
                split_hi(act, n0 + 4, off)
                split_hi(act, n0 + 5, off)
                if behind:
                    hidden_hi(i - 1)
                split_hi(act, n0 + 6, off)
                split_hi(act, n0 + 7, off)

            def silu(i):
                act.wait_ge(unit_used, 8 * i + n0 + 8)
                nc.scalar.activation(work[:, 0].rearrange("p a t -> p (a t)").rearrange("p (b s) -> p b s", b=2),
                                     acc[:, bass.ds((i % 2) * 4, 2), :], ACT.Silu).then_inc(silu_done, 1)

            def hidden_hi(i):
                act.wait_ge(up_free, UP_BLOCKS * l + 2 + i)
                nc.scalar.activation(hid_hi[:, bass.ds(4 * i, 4), :], work[:, 1], ACT.Copy).then_inc(hid_hi_done, 1)

            block(0, False)
            with act.Fori(1, UP_BLOCKS) as i:
                block(i, True)
            silu(UP_BLOCKS - 1)
            hidden_hi(UP_BLOCKS - 1)

        def up_dve(dve, l):
            n0 = units[f"up{l}"]

            def block(i, behind):
                off = 8 * i
                for u in range(3):
                    split_lo(dve, n0 + u, off)
                if behind:
                    glu(i - 1)
                for u in range(3, 7):
                    split_lo(dve, n0 + u, off)
                if behind:
                    hidden_lo(i - 1)
                split_lo(dve, n0 + 7, off)

            def glu(i):
                dve.wait_ge(silu_done, UP_BLOCKS * l + 1 + i)
                dve.wait_ge(hid_lo_done, UP_BLOCKS * l + i)
                nc.vector.tensor_tensor(work[:, 1].rearrange("p a t -> p (a t)").rearrange("p (b s) -> p b s", b=2),
                                        acc[:, bass.ds((i % 2) * 4 + 2, 2), :],
                                        work[:, 0].rearrange("p a t -> p (a t)").rearrange("p (b s) -> p b s", b=2),
                                        ALU.mult).then_inc(up_free, 1)

            def hidden_lo(i):
                dve.wait_ge(hid_hi_done, UP_BLOCKS * l + 1 + i)
                nc.vector.tensor_tensor(hid_lo[:, bass.ds(4 * i, 4), :], work[:, 1],
                                        hid_hi[:, bass.ds(4 * i, 4), :].bitcast(F32),
                                        ALU.subtract).then_inc(hid_lo_done, 1)

            block(0, False)
            with dve.Fori(1, UP_BLOCKS) as i:
                block(i, True)
            glu(UP_BLOCKS - 1)
            hidden_lo(UP_BLOCKS - 1)

        def up_pe(pe, l, fill):
            n0 = units[f"up{l}"]
            with pe.Fori(0, UP_BLOCKS) as i:
                pe.wait_ge(up_free, UP_BLOCKS * l + i)
                for u in range(8):
                    pe.wait_ge(hn_lo, 4 * fill + u % 4 + 1)
                    bank = (i % 2) * 4 + 2 * (u // 4)
                    unit_product(pe, n0 + u, (4, 512), x_tiles(4 * (u % 4)), lambda f: bank_tile(bank, f),
                                 u % 4 == 0, u % 4 == 3, off=8 * i)

        def out_sp(sp, stage, w, kt):
            for b in range(2):
                n0 = units[stage] + b * kt // 2
                with sp.Fori(0, kt // 4) as j:
                    for u in range(2):
                        load_unit(sp, n0 + u, w[:, bass.ds(4 * j + 2 * u, 2), 1024 * b:1024 * b + 1024], (2, 1024),
                                  off=2 * j)

        def out_act(act, stage, kt):
            for b in range(2):
                n0 = units[stage] + b * kt // 2
                with act.Fori(0, kt // 4) as j:
                    for u in range(2):
                        split_hi(act, n0 + u, off=2 * j)

        def out_dve(dve, stage, kt):
            n0 = units[stage]

            def add(b):
                for g in range(2):
                    dve.wait_ge(unit_used, n0 + (b + 1) * kt // 2)
                    o = x_res[:, 8 * b + 4 * g:8 * b + 4 * g + 4].rearrange("p a t -> p (a t)")
                    o = o.rearrange("p (c s) -> p c s", c=2)
                    bank = 4 * (1 - b) + 2 * g
                    nc.vector.tensor_tensor(o, acc[:, bank:bank + 2], o, ALU.add).then_inc(x_ready, 1)

            with dve.Fori(0, kt // 4) as j:
                for u in range(2):
                    split_lo(dve, n0 + u, off=2 * j)
            n1 = n0 + kt // 2
            split_lo(dve, n1)
            split_lo(dve, n1 + 1)
            add(0)
            with dve.Fori(1, kt // 4) as j:
                for u in range(2):
                    split_lo(dve, n1 + u, off=2 * j)
            add(1)

        def out_pe(pe, stage, hi, lo, kt, before_block, before_last):
            for b in range(2):
                n0 = units[stage] + b * kt // 2
                bank = 4 * (1 - b)

                def pair(j, first, last):
                    for u in range(2):
                        def xs(k):
                            if isinstance(j, int):
                                return hi[:, 4 * j + 2 * u + k, :], lo[:, 4 * j + 2 * u + k, :]
                            at = bass.ds(4 * j + 2 * u + k, 1)
                            return (hi[:, at, :].rearrange("p a t -> p (a t)"), lo[:, at, :].rearrange("p a t -> p (a t)"))
                        off, n = (0, n0 + 2 * j + u) if isinstance(j, int) else (2 * j, n0 + u)
                        unit_product(pe, n, (2, 1024), xs, lambda f: bank_tile(bank, f), first and u == 0,
                                     last and u == 1, off=off)

                before_block(b)
                pair(0, True, False)
                with pe.Fori(1, kt // 4 - 1) as j:
                    pair(j, False, False)
                if b == 0:
                    before_last()
                pair(kt // 4 - 1, False, True)

        def down_pe(pe, l):
            def before_block(b):
                pe.wait_ge(up_free, UP_BLOCKS * (l + 1) + b)
                if b == 0:
                    pe.wait_ge(hid_lo_done, UP_BLOCKS * (l + 1) - 1)

            out_pe(pe, f"down{l}", hid_hi, hid_lo, FT, before_block,
                   lambda: pe.wait_ge(hid_lo_done, UP_BLOCKS * (l + 1)))

        TWO_PI = 2.0 * np.pi
        parts_2pi = []
        rest = TWO_PI
        for _ in range(3):
            e = 2.0 ** (7 - int(np.floor(np.log2(rest))))
            parts_2pi.append(float(np.floor(rest * e) / e))
            rest -= parts_2pi[-1]
        parts_2pi.append(float(np.float32(rest)))

        def rope_dve(dve):
            step = 0

            def then(ins):
                nonlocal step
                step += 1
                ins.then_inc(rope_step, 1)
                dve.wait_ge(rope_step, step)

            ang, turns, half = rot_b[:, 0], rot_b[:, 1], rot_c[:, 0]
            dve.wait_ge(pos_in, 16)
            then(nc.vector.tensor_copy(ang, pos_i[:]))
            then(nc.vector.tensor_scalar(ang, ang, const("inv_freq"), None, ALU.mult))
            then(nc.vector.tensor_scalar(turns, ang, 1.0 / TWO_PI, 1.5 * 2.0 ** 23, ALU.mult, ALU.add))
            then(nc.vector.tensor_scalar(turns, turns, 1.5 * 2.0 ** 23, None, ALU.subtract))
            for c in parts_2pi:
                then(nc.vector.scalar_tensor_tensor(out=ang, in0=turns, scalar=-c, in1=ang, op0=ALU.mult, op1=ALU.add))
            pi_below = 3.1415925
            then(nc.vector.tensor_scalar(ang, ang, pi_below, -pi_below, ALU.min, ALU.max))
            dve.wait_ge(rope_sin, 2)
            then(nc.vector.tensor_tensor(half, half, half, ALU.mult))
            nc.vector.tensor_scalar(cos[:], half, -2.0, 1.0, ALU.mult, ALU.add).then_inc(rope_ready, 1)

        rope_steps = 5 + len(parts_2pi)

        def rope_act(act):
            act.wait_ge(x_ready, 4 * (norm_of["ret"] + 1))
            act.dma_start(pos_i[:], positions.to_broadcast([P, T])).then_inc(pos_in, 16)
            c, n = TABLE_COLS["ret_decay"]
            act.dma_start(ret_decay[:], table[:, c:c + n].rearrange("p (h t) -> p h t", h=RET_HEADS)).then_inc(decay_in, 16)
            act.wait_ge(rope_step, rope_steps)
            nc.scalar.activation(sin[:], rot_b[:, 0], ACT.Sin).then_inc(rope_sin, 1)
            nc.scalar.activation(rot_c[:, 0], rot_b[:, 0], ACT.Sin, scale=0.5).then_inc(rope_sin, 1)

        n_ret = units["ret"]

        def ret_sp(sp):
            with sp.Fori(0, RET_HEADS) as h:
                off = 12 * h
                for u in range(4):
                    src = ret_in[:, 8 * (u % 2):8 * (u % 2) + 8, bass.ds(D * (u // 2) + RET_DK * h, RET_DK)]
                    load_unit(sp, n_ret + u, src, (8, RET_DK), off=off)
                for u in range(8):
                    src = ret_in[:, 4 * (u % 4):4 * (u % 4) + 4, bass.ds(2 * D * (1 + u // 4) + RET_DV * h, RET_DV)]
                    load_unit(sp, n_ret + 4 + u, src, (4, RET_DV), off=off)

        def ret_pe(pe, fill):
            def values_unit(u, off):
                n = n_ret + 4 + u
                pe.wait_ge(lo_done, n + 1 + off)
                hi = w_hi[:, n % 2, :].rearrange("p (k n) -> p k n", k=4)
                lo = w_lo[:, n % 2, :].rearrange("p (k n) -> p k n", k=4)
                for k in range(4):
                    for tt in range(2):
                        c = slice(P * tt, P * tt + P)
                        for m, (a, w) in enumerate(((x_hi, hi), (x_lo, hi), (x_hi, lo))):
                            mm = nc.tensor.matmul(acc[:, 2 + tt, :], a[:, 4 * u + k, c], w[:, k, :],
                                                  start=(u == 0 and k == 0 and m == 0),
                                                  stop=(u == 3 and k == 3 and m == 2), skip_group_check=True)
                mm.then_inc(unit_used, 1)

            def outputs(h):
                pe.wait_ge(probs_done, 1 + h)
                pe.wait_ge(v_evac, 1 + h)
                pe.wait_ge(y_var, h)
                for f in range(4):
                    c = slice(P * f, P * f + P)
                    nc.tensor.matmul(bank_tile(6, f), v_rows[:, 0, c], probs[:, 0:T], start=(f % 2 == 0), stop=False,
                                     skip_group_check=True)
                    mm = nc.tensor.matmul(bank_tile(6, f)[:, P:T], v_rows[:, 1, c], probs[:, T:T + P], start=False,
                                          stop=True, skip_group_check=True)
                mm.then_inc(y_done, 1)

            def head_sum(h, ready, src, col, done):
                pe.wait_ge(ready, 1 + h)
                for f in range(4):
                    mm = nc.tensor.matmul(acc[:, 6, col:col + T], ones, src[:, f], start=(f == 0), stop=(f == 3),
                                          skip_group_check=True)
                mm.then_inc(done, 1)

            def scores(h):
                pe.wait_ge(rot_done, 1 + h)
                for jt in range(2):
                    for d in range(2):
                        mm = nc.tensor.matmul(acc[:, 7, T * jt:T + P * jt], qk_rot[:, 1, d, P * jt:P * jt + P],
                                              qk_rot[:, 0, d, P * jt:T], start=(jt == 0 and d == 0), stop=(d == 1),
                                              skip_group_check=True)
                mm.then_inc(scores_done, 1)

            def head(h, behind):
                off = 12 * h
                if behind:
                    pe.wait_ge(rot_done, h)
                for u in range(4):
                    if not behind:
                        pe.wait_ge(hn_lo, 4 * fill + 2 * (u % 2) + 2)
                    unit_product(pe, n_ret + u, (8, RET_DK), x_tiles(8 * (u % 2)), lambda f: bank_tile(u // 2, f),
                                 u % 2 == 0, u % 2 == 1, off=off)
                if behind:
                    outputs(h - 1)
                values_unit(0, off)
                values_unit(1, off)
                if behind:
                    head_sum(h - 1, y_evac, y_head, 0, mean_done)
                values_unit(2, off)
                values_unit(3, off)
                if behind:
                    head_sum(h - 1, y_sq, work[:, 0], T, var_done)
                scores(h)
                if behind:
                    pe.wait_ge(silu_g_done, h)
                for u in range(4):
                    unit_product(pe, n_ret + 8 + u, (4, 512), x_tiles(4 * u), lambda f: bank_tile(4, f), u == 0,
                                 u == 3, off=off)

            head(0, False)
            with pe.Fori(1, RET_HEADS) as h:
                head(h, True)
            h = RET_HEADS - 1
            outputs(h)
            head_sum(h, y_evac, y_head, 0, mean_done)
            head_sum(h, y_sq, work[:, 0], T, var_done)

        def two_banks(ap):
            return ap.rearrange("p a t -> p (a t)").rearrange("p (b s) -> p b s", b=2)

        def ret_act(act):
            def silu(h):
                act.wait_ge(unit_used, n_ret + 12 + 12 * h)
                act.wait_ge(gated, h)
                nc.scalar.activation(two_banks(silu_g[:]), acc[:, 4:6], ACT.Silu).then_inc(silu_g_done, 1)

            def take_y(h):
                act.wait_ge(y_done, 1 + h)
                act.wait_ge(gated, h)
                nc.scalar.activation(two_banks(y_head[:]), acc[:, 6:8], ACT.Copy).then_inc(y_evac, 1)

            def square(h):
                act.wait_ge(centred, 1 + h)
                nc.scalar.activation(work[:, 0], y_head[:], ACT.Square).then_inc(y_sq, 1)

            def root(h):
                act.wait_ge(y_var, 1 + h)
                nc.scalar.activation(rstd[:], rvar[:], ACT.Sqrt).then_inc(y_rstd, 1)

            def take_v(h):
                act.wait_ge(unit_used, n_ret + 8 + 12 * h)
                act.wait_ge(y_done, h)
                nc.scalar.activation(v_rows[:], acc[:, 2:4], ACT.Copy).then_inc(v_evac, 1)

            def high(h):
                act.wait_ge(gated, 1 + h)
                nc.scalar.activation(ret_hi[:, bass.ds(4 * h, 4), :], work[:, 1], ACT.Copy).then_inc(ret_hi_done, 1)

            def head(h, behind):
                off = 12 * h
                split_hi(act, n_ret, off)
                split_hi(act, n_ret + 1, off)
                if behind:
                    silu(h - 1)
                split_hi(act, n_ret + 2, off)
                split_hi(act, n_ret + 3, off)
                split_hi(act, n_ret + 4, off)
                split_hi(act, n_ret + 5, off)
                if behind:
                    take_y(h - 1)
                split_hi(act, n_ret + 6, off)
                split_hi(act, n_ret + 7, off)
                if behind:
                    square(h - 1)
                split_hi(act, n_ret + 8, off)
                split_hi(act, n_ret + 9, off)
                if behind:
                    root(h - 1)
                take_v(h)
                split_hi(act, n_ret + 10, off)
                if behind:
                    high(h - 1)
                split_hi(act, n_ret + 11, off)

            head(0, False)
            with act.Fori(1, RET_HEADS) as h:
                head(h, True)
            h = RET_HEADS - 1
            silu(h)
            take_y(h)
            square(h)
            root(h)
            high(h)

        def ret_dve(dve):
            def rotate(h, behind):
                dve.wait_ge(unit_used, n_ret + 4 + 12 * h)
                dve.wait_ge(scores_done, h)
                dve.wait_ge(rot_done, h)
                if behind:
                    dve.wait_ge(ret_lo_done, h - 1)
                first, second = acc[:, 0:2, 0:T], acc[:, 0:2, T:2 * T]
                c2 = cos[:].rearrange("p (a t) -> p a t", a=1).to_broadcast([P, 2, T])
                s2 = sin[:].rearrange("p (a t) -> p a t", a=1).to_broadcast([P, 2, T])
                nc.vector.tensor_tensor(rot_a, first, c2, ALU.mult)
                nc.vector.tensor_tensor(rot_b, second, s2, ALU.mult)
                nc.vector.tensor_tensor(rot_c, first, s2, ALU.mult)
                nc.vector.tensor_tensor(rot_d, second, c2, ALU.mult).then_inc(rot_mul, 1)
                dve.wait_ge(rot_mul, 1 + h)
                nc.vector.tensor_tensor(qk_rot[:, :, 0, :], rot_a, rot_b, ALU.subtract)
                nc.vector.tensor_tensor(qk_rot[:, :, 1, :], rot_c, rot_d, ALU.add).then_inc(rot_done, 1)

            def decay_scores(h):
                dve.wait_ge(scores_done, 1 + h)
                dve.wait_ge(y_done, h)
                d = ret_decay[:, bass.ds(h, 1), :].rearrange("p a t -> p (a t)")
                nc.vector.tensor_tensor(probs[:, 0:T], acc[:, 7, 0:T], d, ALU.mult)
                nc.vector.tensor_tensor(probs[:, T:T + P], acc[:, 7, T:T + P], d[:, 0:P], ALU.mult).then_inc(probs_done, 1)

            def centre(h):
                dve.wait_ge(mean_done, 1 + h)
                mean = acc[:, 6, 0:T]
                for f in range(4):
                    last = nc.vector.scalar_tensor_tensor(out=y_head[:, f], in0=mean, scalar=-1.0 / RET_DV,
                                                          in1=y_head[:, f], op0=ALU.mult, op1=ALU.add)
                last.then_inc(centred, 1)

            def variance(h):
                dve.wait_ge(var_done, 1 + h)
                dve.wait_ge(y_rstd, h)
                nc.vector.tensor_scalar(rvar[:], acc[:, 6, T:2 * T], 1.0 / RET_DV, NORM_EPS, ALU.mult,
                                        ALU.add).then_inc(y_eps_added, 1)
                dve.wait_ge(y_eps_added, 1 + h)
                nc.vector.reciprocal(rvar[:], rvar[:]).then_inc(y_var, 1)

            def gate(h):
                dve.wait_ge(y_rstd, 1 + h)
                r0, _ = PARAM_ROWS["ret_gn_w"]
                for f in range(4):
                    gain = prm[:, r0 + 4 * h + f:r0 + 4 * h + f + 1] if isinstance(h, int) else prm[:, bass.ds(4 * h + (r0 + f), 1)]
                    last = nc.vector.scalar_tensor_tensor(out=y_head[:, f], in0=y_head[:, f], scalar=gain, in1=rstd[:],
                                                          op0=ALU.mult, op1=ALU.mult)
                last.then_inc(y_scaled, 1)
                dve.wait_ge(y_scaled, 1 + h)
                dve.wait_ge(silu_g_done, 1 + h)
                dve.wait_ge(ret_lo_done, h)
                nc.vector.tensor_tensor(work[:, 1], y_head[:], silu_g[:], ALU.mult).then_inc(gated, 1)

            def low(h):
                dve.wait_ge(ret_hi_done, 1 + h)
                nc.vector.tensor_tensor(ret_lo[:, bass.ds(4 * h, 4), :], work[:, 1],
                                        ret_hi[:, bass.ds(4 * h, 4), :].bitcast(F32), ALU.subtract).then_inc(ret_lo_done, 1)

            def head(h, behind):
                off = 12 * h
                for u in range(6):
                    split_lo(dve, n_ret + u, off)
                rotate(h, behind)
                split_lo(dve, n_ret + 6, off)
                if behind:
                    centre(h - 1)
                split_lo(dve, n_ret + 7, off)
                split_lo(dve, n_ret + 8, off)
                if behind:
                    variance(h - 1)
                split_lo(dve, n_ret + 9, off)
                decay_scores(h)
                if behind:
                    gate(h - 1)
                split_lo(dve, n_ret + 10, off)
                split_lo(dve, n_ret + 11, off)
                if behind:
                    low(h - 1)

            dve.wait_ge(rope_ready, 1)
            dve.wait_ge(decay_in, 16)
            head(0, False)
            with dve.Fori(1, RET_HEADS) as h:
                head(h, True)
            h = RET_HEADS - 1
            centre(h)
            variance(h)
            gate(h)
            low(h)

        SLOT_K, SLOT_B, SLOT_A, SLOT_R = range(4)
        DECAY_SCALE = float(np.exp(-0.5))
        GROUPS = PAIRS * NC
        n_dec, n_rate, n_gate = (units[k] for k in ("decay", "rate", "gate"))
        MU = {"rec": 0, "decay": 1, "key": 2, "val": 3, "rate": 4, "gate": 5}
        BLOCKS_BEFORE = {"key": 0, "rec": 4, "val": 8}
        W_ROW = {"rec": 0, "key": 1, "val": 2}

        h_ready = sem("h_ready")
        h_zero = sem("h_zero")
        mix_diff = sem("mix_diff")
        lora_act = sem("lora_act")
        lora_hi_done = sem("lora_hi_done")
        lora_lo_done = sem("lora_lo_done")
        sig_done = sem("sig_done")
        cum_done = sem("cum_done")
        block_free = sem("block_free")
        kk_raw = sem("kk_raw")
        kk_sq = sem("kk_sq")
        kk_sum = sem("kk_sum")
        kk_root = sem("kk_root")
        kk_step = sem("kk_step")
        cum_gap = sem("cum_gap")
        decayed = sem("decayed")
        prep_step = sem("prep_step")
        prep_done = sem("prep_done")
        b_wide_done = sem("b_wide_done")
        tri_mm = sem("tri_mm")
        tri_masked = sem("tri_masked")
        tri_stored = [sem("tri_stored0"), sem("tri_stored1")]
        tri_loaded = sem("tri_loaded")
        solve_step = sem("solve_step")
        inv_stored = sem("inv_stored")
        inv_loaded = sem("inv_loaded")
        val_out = sem("val_out")
        rk_done = sem("rk_done")
        rk_sum = sem("rk_sum")
        bonus_done = sem("bonus_done")
        val_stored = sem("val_stored")
        bonus_stored = sem("bonus_stored")
        gate_out = sem("gate_out")
        v_loaded = sem("v_loaded")
        bonus_loaded = sem("bonus_loaded")
        wide_done = sem("wide_done")
        state_zero = sem("state_zero")
        m_mm = sem("m_mm")
        m_done = sem("m_done")
        kbv_done = sem("kbv_done")
        x_mm = sem("x_mm")
        x_done = sem("x_done")
        u_mm = sem("u_mm")
        u_done = sem("u_done")
        y_mm = sem("y_mm")
        y_taken = sem("y_taken")
        s_mm = sem("s_mm")
        dec_done = sem("dec_done")
        s_done = sem("s_done")
        ln_step = sem("ln_step")
        ln_sq = sem("ln_sq")
        ln_root = sem("ln_root")
        y_wide_done = sem("y_wide_done")
        yt_mm = sem("yt_mm")
        att_ready = sem("att_ready")
        att_hi_done = sem("att_hi_done")
        att_lo_done = sem("att_lo_done")

        tri_dram = nc.dram_tensor("tri_dram", (P, 64 * 64), F32, kind="Internal").ap()
        inv_dram = nc.dram_tensor("inv_dram", (P, 64 * 64), F32, kind="Internal").ap()
        a_dram = nc.dram_tensor("a_dram", (P, DT * T), F32, kind="Internal").ap()
        v_dram = nc.dram_tensor("v_dram", (P, DT, T), F32, kind="Internal").ap()
        bonus_dram = nc.dram_tensor("bonus_dram", (P, DT, T), F32, kind="Internal").ap()

        def stacked(dram, g0, n):
            return dram[2 * g0:2 * (g0 + n), :].rearrange("(g h) (s t) -> g (h s) t", h=2, s=64).rearrange("g r t -> r g t")

        def flat(ap):
            return ap.rearrange("p a t -> p (a t)")

        def param4(name, i, k):
            r, _ = PARAM_ROWS[name]
            if isinstance(i, int):
                return prm[:, r + 4 * i + k:r + 4 * i + k + 1]
            return prm[:, bass.ds(4 * i + (r + k), 1)]

        def lora_sp(sp, n, down, up):
            k = down.shape[1]
            load_unit(sp, n, down.rearrange("(kt p) n -> p kt n", p=P), (DT, k))
            load_unit(sp, n + 1, up.rearrange("p (a n) -> p a n", a=1), (1, D), parts=k)

        def rwkv_sp(sp):
            lora_sp(sp, n_dec, rw_w1[0], rw_w2[0])
            lora_sp(sp, n_rate, rw_a1[0], rw_a2[0])
            for name in ("key", "rec", "val"):
                w = rw_w_rkv[0, W_ROW[name]].rearrange("(kt p) n -> p kt n", p=P)
                with sp.Fori(0, 4) as i:
                    for u in range(4):
                        load_unit(sp, units[name] + u, w[:, 4 * u:4 * u + 4, bass.ds(i * 512, 512)], (4, 512), off=4 * i)
            g1 = rw_g1[0].rearrange("(kt p) n -> p kt n", p=P)
            g2 = rw_g2[0].rearrange("(kt p) n -> p kt n", p=P)
            for u in range(2):
                load_unit(sp, n_gate + u, g1[:, 8 * u:8 * u + 8, :], (8, GLORA))
            for u in range(2):
                load_unit(sp, n_gate + 2 + u, g2[:, u:u + 1, :], (1, D))
            out_sp(sp, "rw_out", rw_w_o[0].rearrange("(kt p) n -> p kt n", p=P), DT)

        def mix_group(dve, name):
            i, mu = fill_of[name], MU[name]

            def group(j):
                nc.vector.tensor_tensor(work[:, j % 2], h_in[:, 4 * j:4 * j + 4, 0:T], h_in[:, 4 * j:4 * j + 4, 1:T + 1],
                                        ALU.subtract).then_inc(mix_diff, 1)
                dve.wait_ge(mix_diff, 4 * i + j + 1)
                for k in range(4):
                    last = nc.vector.scalar_tensor_tensor(out=work[:, j % 2, k], in0=work[:, j % 2, k],
                                                          scalar=param("rw_mu", DT * mu + 4 * j + k),
                                                          in1=h_in[:, 4 * j + k, 1:T + 1], op0=ALU.mult, op1=ALU.add)
                return last
            return group

        def mixed_dve(dve, name):
            fill_dve(dve, fill_of[name], mix_group(dve, name))

        def mixed_act(act, name, used):
            if used:
                act.wait_ge(unit_used, used)
            fill_act(act, fill_of[name])

        def lora_pe(pe, name, n, which):
            pe.wait_ge(hn_lo, 4 * fill_of[name] + 4)
            if which:
                pe.wait_ge(sig_done, 4 * which)
            unit_product(pe, n, (DT, LORA), x_tiles(0), lambda f: acc[0:LORA, 0, 0:T], True, True)
            pe.wait_ge(lora_lo_done, which + 1)
            unit_product(pe, n + 1, (1, D), lambda k: (lora_hi[0:LORA, 0, :], lora_lo[0:LORA, 0, :]),
                         lambda f: bank_tile(0, f), True, True, parts=LORA)

        def lora_split_act(act, dst, src, which):
            act.wait_ge(lora_act, which + 1)
            nc.scalar.activation(dst, src, ACT.Copy).then_inc(lora_hi_done, 1)

        def lora_act_stage(act, n, which, first_func, bias_name, slot):
            split_hi(act, n, width=DT * LORA)
            split_hi(act, n + 1, parts=LORA)
            act.wait_ge(unit_used, n + 1)
            src = work[0:LORA, 1, 0:1]
            nc.scalar.activation(flat(src), acc[0:LORA, 0, 0:T], first_func).then_inc(lora_act, 1)
            lora_split_act(act, lora_hi[0:LORA], src, which)
            act.wait_ge(unit_used, n + 2)
            for kt in range(DT):
                ins = nc.scalar.activation(quad[:, slot, kt, :], bank_tile(0, kt), ACT.Sigmoid, bias=param(bias_name, kt))
                if kt % 4 == 3:
                    ins.then_inc(sig_done, 1)

        def lora_split_dve(dve, lo, hi, src, which):
            dve.wait_ge(lora_hi_done, which + 1)
            nc.vector.tensor_tensor(lo, src, hi.bitcast(F32), ALU.subtract).then_inc(lora_lo_done, 1)

        def blocks_pe(pe, name, behind_unit=None):
            n0 = units[name]
            with pe.Fori(0, 4) as i:
                pe.wait_ge(block_free, BLOCKS_BEFORE[name] + i)
                for u in range(4):
                    pe.wait_ge(hn_lo, 4 * fill_of[name] + u + 1)
                    bank = (i % 2) * 2
                    unit_product(pe, n0 + u, (4, 512), x_tiles(4 * u), lambda f: bank_tile(bank, f), u == 0, u == 3,
                                 off=4 * i)
                    if u == 2 and behind_unit:
                        behind_unit(i)

        def block_banks(i):
            return acc[:, bass.ds((i % 2) * 2, 2), :]

        def prep_act(act, i, part):
            tiles = bass.ds(4 * i, 4)
            if part == 0:
                act.wait_ge(kk_raw, 1 + i)
                nc.scalar.activation(work[:, 1], work[:, 0], ACT.Square).then_inc(kk_sq, 1)
            elif part == 1:
                act.wait_ge(kk_sum, 1 + i)
                nc.scalar.activation(two_banks(work[:, 1]), acc[:, 4:6], ACT.Sqrt).then_inc(kk_root, 1)
            else:
                act.wait_ge(kk_step, 3 * i + 3)
                nc.scalar.activation(work[:, 1], quad[:, SLOT_R, tiles, :], ACT.Exp, scale=DECAY_SCALE).then_inc(decayed, 1)
                act.wait_ge(cum_gap, 1 + i)
                act.wait_ge(decayed, 3 * i + 1)
                nc.scalar.activation(prep_t[:], prep_t[:], ACT.Exp, scale=-DECAY_SCALE).then_inc(decayed, 1)
                nc.scalar.activation(quad[:, SLOT_R, tiles, :], quad[:, SLOT_R, tiles, :], ACT.Exp,
                                     scale=-DECAY_SCALE).then_inc(decayed, 1)

        def prep_pe(pe, i):
            pe.wait_ge(kk_sq, 1 + i)
            for b in range(2):
                mm = nc.tensor.matmul(acc[:, 4 + b, :], const("head_ones"), flat(work[:, 1, 2 * b:2 * b + 2]))
            mm.then_inc(kk_sum, 1)

        def prep_dve(dve, i, part):
            tiles = bass.ds(4 * i, 4)
            k_t, b_t, a_t, p_t = (quad[:, s, tiles, :] for s in (SLOT_K, SLOT_B, SLOT_A, SLOT_R))
            if part == 0:
                dve.wait_ge(prep_done, i)
                for k in range(4):
                    last = nc.vector.tensor_scalar(work[:, 0, k], flat(quad[:, SLOT_K, bass.ds(4 * i + k, 1), :]),
                                                   param4("rw_k_k", i, k), None, ALU.mult)
                last.then_inc(kk_raw, 1)
            elif part == 1:
                dve.wait_ge(kk_root, 1 + i)
                nc.vector.tensor_scalar(work[:, 1], work[:, 1], 1e-12, None, ALU.max).then_inc(kk_step, 1)
                nc.vector.tensor_tensor(prep_t[:], p_t, a_t, ALU.subtract).then_inc(cum_gap, 1)
                dve.wait_ge(kk_step, 3 * i + 1)
                nc.vector.reciprocal(work[:, 1], work[:, 1]).then_inc(kk_step, 1)
                dve.wait_ge(kk_step, 3 * i + 2)
                nc.vector.tensor_tensor(work[:, 0], work[:, 0], work[:, 1], ALU.mult).then_inc(kk_step, 1)
            else:
                dve.wait_ge(kk_step, 3 * i + 3)
                dve.wait_ge(decayed, 3 * i + 2)
                nc.vector.scalar_tensor_tensor(out=a_t, in0=work[:, 0], scalar=-1.0, in1=prep_t[:], op0=ALU.mult,
                                               op1=ALU.mult).then_inc(prep_step, 1)
                dve.wait_ge(prep_step, 5 * i + 1)
                nc.vector.tensor_tensor(work[:, 0], work[:, 0], b_t, ALU.mult).then_inc(prep_step, 1)
                for k in range(4):
                    last = nc.vector.tensor_scalar(prep_t[:, k], flat(quad[:, SLOT_B, bass.ds(4 * i + k, 1), :]), -1.0,
                                                   param4("rw_k_a", i, k), ALU.add, ALU.mult)
                last.then_inc(prep_step, 1)
                dve.wait_ge(prep_step, 5 * i + 3)
                nc.vector.tensor_tensor(b_t, work[:, 0], work[:, 1], ALU.mult)
                nc.vector.scalar_tensor_tensor(out=prep_t[:], in0=prep_t[:], scalar=1.0, in1=k_t, op0=ALU.add,
                                               op1=ALU.mult).then_inc(prep_step, 1)
                dve.wait_ge(decayed, 3 * i + 3)
                dve.wait_ge(prep_step, 5 * i + 4)
                nc.vector.tensor_copy(chunk_decay[:, tiles, :], quad[:, SLOT_R, tiles, CHUNK - 1:T:CHUNK])
                nc.vector.tensor_tensor(k_t, prep_t[:], work[:, 1], ALU.mult).then_inc(prep_step, 1)
                dve.wait_ge(prep_step, 5 * i + 5)
                dve.sem_inc(prep_done, 1)

        def rk_pe(pe, i):
            pe.wait_ge(rk_done, 1 + i)
            for b in range(2):
                mm = nc.tensor.matmul(acc[:, 4 + b, :], const("head_ones"), flat(work[:, 1, 2 * b:2 * b + 2]))
            mm.then_inc(rk_sum, 1)

        def tri_pool(pool):
            pool.wait_ge(tables_in, table_loads)
            mask = const("pair_mask").rearrange("p (a h b) -> p a h b", a=1, b=1).to_broadcast([P, NC, 2, 64])
            for p in range(PAIRS):
                if p == 0:
                    pool.wait_ge(prep_done, 4)
                if p >= 2:
                    pool.wait_ge(tri_mm, p - 1)
                src = quad[:, SLOT_B, p, :].rearrange("p (c a t) -> p c a t", c=NC, a=1).to_broadcast([P, NC, 2, 64])
                nc.gpsimd.tensor_tensor(b_wide[:, p % 2], src, mask, ALU.mult).then_inc(b_wide_done, 1)
                if p >= 1:
                    store(pool, p - 1)
            store(pool, PAIRS - 1)

        def store(pool, p):
            pool.wait_ge(tri_masked, p + 1)
            pool.dma_start(stacked(tri_dram, NC * p, NC), tri_rows[:, p % 2]).then_inc(tri_stored[p % 2], 16)

        def tri_pe(pe):
            for p in range(PAIRS):
                pe.wait_ge(b_wide_done, p + 1)
                if p >= 2:
                    pe.wait_ge(tri_masked, p - 1)
                for c in range(NC):
                    mm = nc.tensor.matmul(acc[:, 4 + p % 2, 64 * c:64 * c + 64], b_wide[:, p % 2, c],
                                          quad[:, SLOT_A, p, 64 * c:64 * c + 64])
                mm.then_inc(tri_mm, 1)

        def tri_dve(dve):
            mask = const("strict_mask").rearrange("p (a t) -> p a t", a=1).to_broadcast([P, NC, 64])
            for p in range(PAIRS):
                dve.wait_ge(tri_mm, p + 1)
                if p >= 2:
                    dve.wait_ge(tri_stored[p % 2], 16 * (p // 2))
                nc.vector.tensor_tensor(tri_rows[:, p % 2],
                                        acc[:, 4 + p % 2, 0:NC * 64].rearrange("p (c t) -> p c t", c=NC), mask,
                                        ALU.mult).then_inc(tri_masked, 1)

        def solve_pool(pool):
            for stored in tri_stored:
                pool.wait_ge(stored, 8 * PAIRS)
            pool.dma_start(flat(tri[:]), tri_dram).then_inc(tri_loaded, 16)
            pool.dma_start(a_dram, flat(quad[:, SLOT_A])).then_inc(tri_loaded, 16)
            pool.wait_ge(tri_loaded, 32)
            step = 0
            for u in range(1, 63):
                w = 63 - u
                t = solve_t[:, 0:u * w].rearrange("p (a b) -> p a b", a=u)
                nc.gpsimd.tensor_tensor(t, tri[:, 0:u, u:u + 1].to_broadcast([P, u, w]),
                                        tri[:, u:u + 1, u + 1:64].to_broadcast([P, u, w]), ALU.mult).then_inc(solve_step, 1)
                pool.wait_ge(solve_step, step + 1)
                nc.gpsimd.tensor_tensor(tri[:, 0:u, u + 1:64], tri[:, 0:u, u + 1:64], t, ALU.add).then_inc(solve_step, 1)
                step += 2
                pool.wait_ge(solve_step, step)
            nc.gpsimd.memset(flat(tri[:])[:, 0:4096:65], 1.0).then_inc(solve_step, 1)
            pool.wait_ge(solve_step, step + 1)
            pool.dma_start(inv_dram, flat(tri[:])).then_inc(inv_stored, 16)
            pool.dma_start(flat(quad[:, SLOT_A]), a_dram).then_inc(inv_loaded, 16)
            pool.wait_ge(inv_stored, 16)
            pool.dma_start(inv_t[:], stacked(inv_dram, 0, GROUPS)).then_inc(inv_loaded, 16)
            pool.wait_ge(inv_loaded, 32)

        def at(g, k):
            if isinstance(g, int):
                return (g + k) % PAIRS, (g + k) // PAIRS * CHUNK
            return (g + (PAIRS + k)) % PAIRS, (g + k) // PAIRS * CHUNK

        def part(ap3, pair, t0, n=CHUNK):
            if isinstance(pair, int):
                return ap3[:, pair, t0:t0 + n]
            return flat(ap3[:, bass.ds(pair, 1), bass.ds(t0, n)])

        def turns(eng, step):
            for g in range(4):
                step(g, 0, g)
            with eng.Fori(1, GROUPS // 4) as it:
                for k in range(4):
                    step(4 * it, k, 4)
            for k in range(3):
                step(GROUPS, k, GROUPS + k)

        def scan_pool(pool):
            pool.wait_ge(v_loaded, 16)
            pool.wait_ge(gate_out, 2)
            four = const("pair_mask").rearrange("p (a h b) -> p a h b", a=1, b=1).to_broadcast([P, 4, 2, 64])
            one = const("pair_mask").rearrange("p (h b) -> p h b", b=1).to_broadcast([P, 2, 64])

            def step(g, k, least):
                if isinstance(g, int) and g + k >= GROUPS:
                    return
                pair, t0 = at(g, k)
                slot = k if not isinstance(g, int) else (g + k) % 4
                if least >= 4:
                    pool.wait_ge(s_mm, g + (k - 3))
                if isinstance(pair, int):
                    src = quad[:, :, pair, t0:t0 + CHUNK].rearrange("p q (a t) -> p q a t", a=1)
                    v_src, i_src = v_feat[:, pair, t0:t0 + CHUNK], inv_t[:, pair * NC + t0 // CHUNK, :]
                else:
                    src = quad[:, :, bass.ds(pair, 1), bass.ds(t0, CHUNK)]
                    v_src = part(v_feat, pair, t0)
                    i_src = flat(inv_t[:, bass.ds(pair * NC + (g + k) // PAIRS, 1), :])
                nc.gpsimd.tensor_tensor(quad_wide[:, slot], src.to_broadcast([P, 4, 2, 64]), four, ALU.mult)
                nc.gpsimd.tensor_tensor(v_wide[:, slot], v_src.rearrange("p (a t) -> p a t", a=1).to_broadcast([P, 2, 64]),
                                        one, ALU.mult)
                nc.gpsimd.tensor_tensor(inv_wide[:, slot], i_src.rearrange("p (a t) -> p a t", a=1).to_broadcast([P, 2, 64]),
                                        one, ALU.mult).then_inc(wide_done, 1)

            turns(pool, step)

        def scan_parts(g, k, least):
            out = []
            for lag in range(4):
                if isinstance(g, int):
                    here = 0 <= g + k - lag < GROUPS
                    out.append((k - lag, (g + k - lag) % 4, here))
                else:
                    out.append((k - lag, (k - lag) % 4, True))
            return out

        def scan_pe(pe):
            pe.wait_ge(state_zero, 1)
            pe.wait_ge(gate_out, 2)
            ident2 = const("ident2")

            def step(g, k, least):
                (k0, s0, on0), (k1, s1, on1), (k2, s2, on2), (k3, s3, on3) = scan_parts(g, k, least)
                if on0:
                    pair, t0 = at(g, k0)
                    bank = s0 % 2
                    pe.wait_ge(wide_done, g + k0 + 1)
                    if least >= 2:
                        pe.wait_ge(m_done, g + k0 - 1)
                        pe.wait_ge(kbv_done, g + k0 - 1)
                    if isinstance(pair, int):
                        ar = quad[:, SLOT_A:SLOT_R + 1, pair, t0:t0 + CHUNK]
                    else:
                        ar = quad[:, SLOT_A:SLOT_R + 1, bass.ds(pair, 1), bass.ds(t0, CHUNK)].rearrange("p q a t -> p q (a t)")
                    for n in (SLOT_K, SLOT_B):
                        nc.tensor.matmul(acc[:, bank, P * n:P * n + P].rearrange("p (q t) -> p q t", q=2),
                                         quad_wide[:, s0, n], ar, skip_group_check=True)
                    for n in (SLOT_K, SLOT_B):
                        nc.tensor.transpose(acc[:, 2 + bank, P * n:P * n + P], flat(quad_wide[:, s0, n]), ident)
                    nc.tensor.matmul(acc[:, 2 + bank, 2 * P:2 * P + 64], v_wide[:, s0], ident2,
                                     skip_group_check=True).then_inc(m_mm, 1)
                if on1:
                    pair, t0 = at(g, k1)
                    pe.wait_ge(m_done, g + k1 + 1)
                    pe.wait_ge(kbv_done, g + k1 + 1)
                    if not isinstance(g, int) or g + k1 >= 1:
                        pe.wait_ge(x_done, g + k1)
                    o = acc[:, 4, 0:64]
                    nc.tensor.matmul(o, quad_wide[:, s1, SLOT_A], part_state(pair), start=True, stop=False,
                                     skip_group_check=True)
                    nc.tensor.matmul(o, mix_wide[:, s1, 0], kbv_rows[:, s1, 2 * P:2 * P + 64], start=False, stop=True,
                                     skip_group_check=True).then_inc(x_mm, 1)
                if on2:
                    pe.wait_ge(x_done, g + k2 + 1)
                    if not isinstance(g, int) or g + k2 >= 1:
                        pe.wait_ge(u_done, g + k2)
                    nc.tensor.matmul(acc[:, 5, 0:64], inv_wide[:, s2], x_stack[:, s2],
                                     skip_group_check=True).then_inc(u_mm, 1)
                if on3:
                    pair, t0 = at(g, k3)
                    pe.wait_ge(u_done, g + k3 + 1)
                    if not isinstance(g, int) or g + k3 >= 1:
                        pe.wait_ge(y_taken, g + k3)
                    o = acc[:, 6, 0:64]
                    nc.tensor.matmul(o, quad_wide[:, s3, SLOT_R], part_state(pair), start=True, stop=False,
                                     skip_group_check=True)
                    nc.tensor.matmul(o, mix_wide[:, s3, 1], kbv_rows[:, s3, 2 * P:2 * P + 64], start=False, stop=False,
                                     skip_group_check=True)
                    nc.tensor.matmul(o, mix_wide[:, s3, 2], u_stack[:, s3], start=False, stop=True,
                                     skip_group_check=True).then_inc(y_mm, 1)
                    if not isinstance(g, int) or g + k3 >= 1:
                        pe.wait_ge(s_done, g + k3)
                    o = acc[:, 7, 0:64]
                    nc.tensor.matmul(o, kbv_rows[:, s3, 0:P], kbv_rows[:, s3, 2 * P:2 * P + 64], start=True, stop=False,
                                     skip_group_check=True)
                    nc.tensor.matmul(o, kbv_rows[:, s3, P:2 * P], u_stack[:, s3], start=False, stop=True,
                                     skip_group_check=True).then_inc(s_mm, 1)

            turns(pe, step)

        def part_state(pair):
            return state[:, pair, :] if isinstance(pair, int) else flat(state[:, bass.ds(pair, 1), :])

        def scan_act(act):
            def step(g, k, least):
                (k0, s0, on0), (k1, s1, on1), (k2, s2, on2), (k3, s3, on3) = scan_parts(g, k, least)
                if on0:
                    act.wait_ge(m_mm, g + k0 + 1)
                    if least >= 4:
                        act.wait_ge(s_mm, g + k0 - 3)
                    nc.scalar.activation(kbv_rows[:, s0], acc[:, 2 + s0 % 2, 0:2 * P + 64], ACT.Copy).then_inc(kbv_done, 1)
                if on2:
                    pair, t0 = at(g, k2)
                    act.wait_ge(u_mm, g + k2 + 1)
                    nc.scalar.activation(u_stack[:, s2], acc[:, 5, 0:64], ACT.Copy).then_inc(u_done, 1)
                    if isinstance(pair, int):
                        dec = chunk_decay[:, pair, t0 // CHUNK:t0 // CHUNK + 1]
                    else:
                        dec = flat(chunk_decay[:, bass.ds(pair, 1), bass.ds((g + k2) // PAIRS, 1)])
                    nc.scalar.activation(state_dec[:, s2], part_state(pair), ACT.Copy, scale=dec).then_inc(dec_done, 1)
                if on3:
                    pair, t0 = at(g, k3)
                    act.wait_ge(y_mm, g + k3 + 1)
                    if isinstance(pair, int):
                        o = y_all[:, pair, t0 // CHUNK, :]
                    else:
                        o = y_all[:, bass.ds(pair, 1), bass.ds((g + k3) // PAIRS, 1), :].rearrange("p a b t -> p (a b t)")
                    nc.scalar.activation(o, acc[:, 6, 0:64], ACT.Copy).then_inc(y_taken, 1)

            act.wait_ge(state_zero, 1)
            turns(act, step)

        def scan_dve(dve):
            masks = const("chunk_mask").rearrange("p (q h t) -> p q h t", q=2, h=2)

            def step(g, k, least):
                (k0, s0, on0), (k1, s1, on1), (k2, s2, on2), (k3, s3, on3) = scan_parts(g, k, least)
                if on0:
                    dve.wait_ge(m_mm, g + k0 + 1)
                    if least >= 4:
                        dve.wait_ge(s_mm, g + k0 - 3)
                    m1 = acc[:, s0 % 2, 0:P].rearrange("p (q a t) -> p q a t", q=2, a=1).to_broadcast([P, 2, 2, 64])
                    nc.vector.tensor_tensor(mix_wide[:, s0, 0:2], m1, masks, ALU.mult)
                    m2 = acc[:, s0 % 2, P + 64:T].rearrange("p (a t) -> p a t", a=1).to_broadcast([P, 2, 64])
                    nc.vector.tensor_tensor(mix_wide[:, s0, 2], m2, masks[:, 1], ALU.mult).then_inc(m_done, 1)
                if on1:
                    dve.wait_ge(x_mm, g + k1 + 1)
                    nc.vector.tensor_copy(x_stack[:, s1], acc[:, 4, 0:64]).then_inc(x_done, 1)
                if on3:
                    pair, t0 = at(g, k3)
                    dve.wait_ge(s_mm, g + k3 + 1)
                    dve.wait_ge(dec_done, g + k3 + 1)
                    if isinstance(pair, int):
                        dec = chunk_decay[:, pair, t0 // CHUNK:t0 // CHUNK + 1]
                    else:
                        dec = flat(chunk_decay[:, bass.ds(pair, 1), bass.ds((g + k3) // PAIRS, 1)])
                    nc.vector.scalar_tensor_tensor(out=part_state(pair), in0=acc[:, 7, 0:64], scalar=dec,
                                                   in1=state_dec[:, s3], op0=ALU.mult, op1=ALU.add).then_inc(s_done, 1)

            turns(dve, step)

        def finish_dve(dve):
            dve.wait_ge(y_taken, GROUPS)
            dve.wait_ge(bonus_loaded, 16)
            dve.wait_ge(s_mm, GROUPS)
            pm = const("pair_mask")
            step = 0

            def then(ins):
                nonlocal step
                step += 1
                ins.then_inc(ln_step, 1)
                dve.wait_ge(ln_step, step)

            for j in range(4):
                y = y_all[:, 4 * j:4 * j + 4].rearrange("p a c v -> p (a c) v")
                st = slice(16 * j, 16 * j + 16)
                then(nc.vector.tensor_reduce(y_mean[:, st], y, AX_X, ALU.add))
                then(nc.vector.tensor_scalar(y_mean[:, st], y_mean[:, st], 1.0 / RW_HEAD, None, ALU.mult))
                mean = y_mean[:, st].rearrange("p (g a) -> p g a", a=1).to_broadcast([P, 16, 64])
                then(nc.vector.tensor_tensor(y, y, mean, ALU.subtract))
                dve.wait_ge(ln_sq, j + 1)
                sq = work[:, 0].rearrange("p a t -> p (a t)").rearrange("p (g v) -> p g v", v=64)
                then(nc.vector.tensor_reduce(y_inv[:, st], sq, AX_X, ALU.add))
                then(nc.vector.tensor_scalar(y_inv[:, st], y_inv[:, st], 1.0 / RW_HEAD, RW_GN_EPS, ALU.mult, ALU.add))
                then(nc.vector.reciprocal(y_inv[:, st], y_inv[:, st]))
                dve.wait_ge(ln_root, j + 1)
                inv = y_inv[:, st].rearrange("p (g a) -> p g a", a=1).to_broadcast([P, 16, 2])
                then(nc.vector.tensor_tensor(y_scale[:, st], inv,
                                             pm.rearrange("p (a h) -> p a h", a=1).to_broadcast([P, 16, 2]), ALU.mult))
                for q in range(4):
                    p = 4 * j + q
                    if p >= 2:
                        dve.wait_ge(yt_mm, p - 1)
                    src = y_all[:, p].rearrange("p c (a v) -> p c a v", a=1).to_broadcast([P, NC, 2, 64])
                    scale = y_scale[:, NC * p:NC * p + NC].rearrange("p c (h a) -> p c h a", a=1).to_broadcast([P, NC, 2, 64])
                    nc.vector.tensor_tensor(y_wide[:, p % 2], src, scale, ALU.mult).then_inc(y_wide_done, 1)
                if j >= 1:
                    dve.wait_ge(att_lo_done, j)
                dve.wait_ge(yt_mm, 4 * j + 4)
                for q in range(4):
                    p = 4 * j + q
                    last = nc.vector.tensor_scalar(work[:, 1, q], bank_tile(2 * (j % 2), q), param("rw_ln_w", p),
                                                   param("rw_ln_b", p), ALU.mult, ALU.add)
                then(last)
                then(nc.vector.tensor_tensor(work[:, 1], work[:, 1], bonus[:, 4 * j:4 * j + 4], ALU.add))
                nc.vector.tensor_tensor(work[:, 1], work[:, 1], out_gate[:, 4 * j:4 * j + 4],
                                        ALU.mult).then_inc(att_ready, 1)
                dve.wait_ge(att_hi_done, j + 1)
                nc.vector.tensor_tensor(att_lo[:, 4 * j:4 * j + 4], work[:, 1],
                                        att_hi[:, 4 * j:4 * j + 4].bitcast(F32), ALU.subtract).then_inc(att_lo_done, 1)

        LN_STEPS = 9

        def finish_act(act):
            for j in range(4):
                y = y_all[:, 4 * j:4 * j + 4].rearrange("p a c v -> p (a c v)")
                act.wait_ge(ln_step, LN_STEPS * j + 3)
                nc.scalar.activation(flat(work[:, 0]), y, ACT.Square).then_inc(ln_sq, 1)
                act.wait_ge(ln_step, LN_STEPS * j + 6)
                nc.scalar.activation(y_inv[:, 16 * j:16 * j + 16], y_inv[:, 16 * j:16 * j + 16],
                                     ACT.Sqrt).then_inc(ln_root, 1)
                act.wait_ge(att_ready, j + 1)
                nc.scalar.activation(att_hi[:, 4 * j:4 * j + 4], work[:, 1], ACT.Copy).then_inc(att_hi_done, 1)

        def finish_pe(pe):
            for p in range(PAIRS):
                pe.wait_ge(y_wide_done, p + 1)
                if p >= 8 and p % 4 == 0:
                    pe.wait_ge(att_ready, p // 4 - 1)
                for c in range(NC):
                    o = bank_tile(2 * (p // 4 % 2), p % 4)
                    mm = nc.tensor.matmul(o[:, 64 * c:64 * c + 64], y_wide[:, p % 2, c], const("ident2"),
                                          skip_group_check=True)
                mm.then_inc(yt_mm, 1)

        def rwkv_pool(pool):
            tri_pool(pool)
            solve_pool(pool)
            scan_pool(pool)

        def rwkv_pe(pe):
            norm_pe(pe, norm_of["rwkv"])
            lora_pe(pe, "decay", n_dec, 0)
            lora_pe(pe, "rate", n_rate, 1)
            pe.wait_ge(sig_done, 8)
            blocks_pe(pe, "key")
            blocks_pe(pe, "rec", lambda i: prep_pe(pe, i))
            tri_pe(pe)
            pe.wait_ge(tri_masked, PAIRS)

            n0 = units["val"]

            def val_block(i, behind):
                pe.wait_ge(block_free, BLOCKS_BEFORE["val"] + i)
                for u in range(4):
                    pe.wait_ge(hn_lo, 4 * fill_of["val"] + u + 1)
                    bank = (i % 2) * 2
                    unit_product(pe, n0 + u, (4, 512), x_tiles(4 * u), lambda f: bank_tile(bank, f), u == 0, u == 3,
                                 off=4 * i)
                    if u == 2 and behind:
                        rk_pe(pe, i - 1)

            val_block(0, False)
            with pe.Fori(1, 4) as i:
                val_block(i, True)
            rk_pe(pe, 3)
            for u in range(2):
                pe.wait_ge(hn_lo, 4 * fill_of["gate"] + 2 * u + 2)
                if u == 0:
                    pe.wait_ge(block_free, 13)
                    pe.wait_ge(bonus_done, 4)
                unit_product(pe, n_gate + u, (8, GLORA), x_tiles(8 * u), lambda f: bank_tile(0, f), u == 0, u == 1)
            pe.wait_ge(lora_lo_done, 3)
            for u in range(2):
                unit_product(pe, n_gate + 2 + u, (1, D), lambda k: (glora_hi[:, u, :], glora_lo[:, u, :]),
                             lambda f: bank_tile(0, f), u == 0, u == 1)
            scan_pe(pe)
            finish_pe(pe)

            def before_block(b):
                if b == 0:
                    pe.wait_ge(att_lo_done, 3)
                else:
                    pe.wait_ge(att_lo_done, 4)

            out_pe(pe, "rw_out", att_hi, att_lo, DT, before_block, lambda: pe.wait_ge(att_lo_done, 4))

        def rwkv_act(act):
            act.sem_inc(block_free, 1)
            norm_act(act, norm_of["rwkv"])
            mixed_act(act, "decay", 0)
            lora_act_stage(act, n_dec, 0, ACT.Tanh, "rw_w0", SLOT_A)
            mixed_act(act, "rate", n_dec + 1)
            lora_act_stage(act, n_rate, 1, ACT.Copy, "rw_a0", SLOT_B)
            mixed_act(act, "key", n_rate + 1)

            def take_block(name, i, dst, done):
                act.wait_ge(unit_used, units[name] + 4 + 4 * i)
                nc.scalar.activation(two_banks(dst), block_banks(i), ACT.Copy).then_inc(done, 1)

            def key_block(i, behind):
                split_hi(act, units["key"], 4 * i)
                split_hi(act, units["key"] + 1, 4 * i)
                if behind:
                    take_block("key", i - 1, quad[:, SLOT_K, bass.ds(4 * i - 4, 4), :], block_free)
                split_hi(act, units["key"] + 2, 4 * i)
                split_hi(act, units["key"] + 3, 4 * i)

            key_block(0, False)
            with act.Fori(1, 4) as i:
                key_block(i, True)
            take_block("key", 3, quad[:, SLOT_K, 12:16, :], block_free)

            mixed_act(act, "rec", units["rec"])
            with act.Fori(0, 4) as i:
                split_hi(act, units["rec"], 4 * i)
                split_hi(act, units["rec"] + 1, 4 * i)
                prep_act(act, i, 0)
                split_hi(act, units["rec"] + 2, 4 * i)
                split_hi(act, units["rec"] + 3, 4 * i)
                prep_act(act, i, 1)
                prep_act(act, i, 2)

            mixed_act(act, "val", units["val"])

            def take_values(i):
                act.wait_ge(unit_used, units["val"] + 4 + 4 * i)
                act.wait_ge(bonus_stored, 16 * i)
                nc.scalar.activation(two_banks(work[:, 0]), block_banks(i), ACT.Copy).then_inc(val_out, 1)
                act.wait_ge(val_out, 1 + i)
                act.sem_inc(block_free, 1)
                act.dma_start(v_dram[:, bass.ds(4 * i, 4), :], work[:, 0]).then_inc(val_stored, 16)

            def store_bonus(i):
                act.wait_ge(bonus_done, 1 + i)
                act.dma_start(bonus_dram[:, bass.ds(4 * i, 4), :], work[:, 1]).then_inc(bonus_stored, 16)

            def val_block(i, behind):
                n0 = units["val"]
                split_hi(act, n0, 4 * i)
                split_hi(act, n0 + 1, 4 * i)
                if behind:
                    take_values(i - 1)
                split_hi(act, n0 + 2, 4 * i)
                split_hi(act, n0 + 3, 4 * i)
                if behind:
                    store_bonus(i - 1)

            val_block(0, False)
            with act.Fori(1, 4) as i:
                val_block(i, True)
            take_values(3)
            store_bonus(3)

            mixed_act(act, "gate", n_gate)
            for u in range(4):
                if u == 2:
                    act.wait_ge(unit_used, n_gate + 2)
                    nc.scalar.activation(flat(work[:, 1, 0:2]), acc[:, 0, :], ACT.Sigmoid).then_inc(lora_act, 1)
                    lora_split_act(act, glora_hi[:], work[:, 1, 0:2], 2)
                split_hi(act, n_gate + u)
            act.wait_ge(unit_used, n_gate + 4)
            act.dma_start(v_feat[:], v_dram).then_inc(v_loaded, 16)
            nc.scalar.activation(out_gate[:, 0:8].rearrange("p a t -> p (a t)").rearrange("p (b s) -> p b s", b=4),
                                 acc[:, 0:4], ACT.Copy).then_inc(gate_out, 1)
            scan_act(act)
            act.wait_ge(s_mm, GROUPS)
            act.dma_start(bonus[:], bonus_dram).then_inc(bonus_loaded, 16)
            finish_act(act)
            out_act(act, "rw_out", DT)

        def rwkv_dve(dve):
            q = norm_of["rwkv"]
            dve.wait_ge(x_turned, 4)
            nc.vector.memset(h_in[:, :, 0:1], 0.0).then_inc(h_zero, 1)
            norm_dve(dve, q)
            for kt in range(DT):
                last = nc.vector.scalar_tensor_tensor(out=h_in[:, kt, 1:T + 1], in0=x_res[:, kt],
                                                      scalar=param("norm_mix", kt), in1=rstd[:], op0=ALU.mult, op1=ALU.mult)
            last.then_inc(h_ready, 1)
            dve.wait_ge(h_ready, 1)
            dve.wait_ge(h_zero, 1)
            mixed_dve(dve, "decay")
            split_lo(dve, n_dec, width=DT * LORA)
            split_lo(dve, n_dec + 1, parts=LORA)
            lora_split_dve(dve, lora_lo[0:LORA], lora_hi[0:LORA], work[0:LORA, 1, 0:1], 0)
            dve.wait_ge(lora_lo_done, 1)
            mixed_dve(dve, "rate")
            split_lo(dve, n_rate, width=DT * LORA)
            split_lo(dve, n_rate + 1, parts=LORA)
            for kt in range(DT):
                if kt % 4 == 0:
                    dve.wait_ge(sig_done, kt // 4 + 1)
                last = nc.vector.tensor_tensor_scan(quad[:, SLOT_R, kt], const("scan_mask"), quad[:, SLOT_A, kt], 0.0,
                                                    ALU.mult, ALU.add)
            last.then_inc(cum_done, 1)
            lora_split_dve(dve, lora_lo[0:LORA], lora_hi[0:LORA], work[0:LORA, 1, 0:1], 1)
            dve.wait_ge(lora_lo_done, 2)
            mixed_dve(dve, "key")
            with dve.Fori(0, 4) as i:
                for u in range(4):
                    split_lo(dve, units["key"] + u, 4 * i)
            mixed_dve(dve, "rec")
            dve.wait_ge(block_free, 5)
            dve.wait_ge(cum_done, 1)
            dve.wait_ge(sig_done, 8)

            def receptance(i):
                dve.wait_ge(unit_used, units["rec"] + 4 + 4 * i)
                r = quad[:, SLOT_R, bass.ds(4 * i, 4), :]
                nc.vector.tensor_tensor(two_banks(r), block_banks(i), two_banks(r), ALU.mult).then_inc(block_free, 1)

            def rec_block(i, behind):
                n0 = units["rec"]
                split_lo(dve, n0, 4 * i)
                split_lo(dve, n0 + 1, 4 * i)
                prep_dve(dve, i, 0)
                if behind:
                    receptance(i - 1)
                split_lo(dve, n0 + 2, 4 * i)
                split_lo(dve, n0 + 3, 4 * i)
                prep_dve(dve, i, 1)
                prep_dve(dve, i, 2)

            rec_block(0, False)
            with dve.Fori(1, 4) as i:
                rec_block(i, True)
            receptance(3)
            tri_dve(dve)
            mixed_dve(dve, "val")

            def rk(i):
                dve.wait_ge(block_free, 8)
                dve.wait_ge(bonus_stored, 16 * i)
                for k in range(4):
                    t = bass.ds(4 * i + k, 1)
                    last = nc.vector.scalar_tensor_tensor(out=work[:, 1, k], in0=flat(quad[:, SLOT_R, t, :]),
                                                          scalar=param4("rw_r_k", i, k), in1=flat(quad[:, SLOT_K, t, :]),
                                                          op0=ALU.mult, op1=ALU.mult)
                last.then_inc(rk_done, 1)

            def make_bonus(i):
                dve.wait_ge(rk_sum, 1 + i)
                dve.wait_ge(val_out, 1 + i)
                nc.vector.tensor_tensor(two_banks(work[:, 1]), acc[:, 4:6], two_banks(work[:, 0]),
                                        ALU.mult).then_inc(bonus_done, 1)
                dve.wait_ge(val_stored, 16 * i + 16)

            def val_block(i, behind):
                n0 = units["val"]
                split_lo(dve, n0, 4 * i)
                split_lo(dve, n0 + 1, 4 * i)
                if behind:
                    rk(i - 1)
                split_lo(dve, n0 + 2, 4 * i)
                split_lo(dve, n0 + 3, 4 * i)
                if behind:
                    make_bonus(i - 1)

            val_block(0, False)
            with dve.Fori(1, 4) as i:
                val_block(i, True)
            rk(3)
            make_bonus(3)
            dve.wait_ge(bonus_stored, 64)
            mixed_dve(dve, "gate")
            for u in range(4):
                if u == 2:
                    lora_split_dve(dve, glora_lo[:], glora_hi[:], work[:, 1, 0:2], 2)
                split_lo(dve, n_gate + u)
            dve.wait_ge(unit_used, n_gate + 4)
            nc.vector.tensor_copy(out_gate[:, 8:16].rearrange("p a t -> p (a t)").rearrange("p (b s) -> p b s", b=4),
                                  acc[:, 4:8]).then_inc(gate_out, 1)
            nc.vector.memset(state[:], 0.0).then_inc(state_zero, 1)
            scan_dve(dve)
            finish_dve(dve)
            out_dve(dve, "rw_out", DT)

        norms = ["rwkv", "up0", "ret", "up1", "final"]
        norm_of = {name: q for q, name in enumerate(norms)}
        fills = ["decay", "rate", "key", "rec", "val", "gate", "up0", "ret", "up1"]
        fill_of = {name: i for i, name in enumerate(fills)}

        def normed_act(act, name):
            norm_act(act, norm_of[name])
            fill_act(act, fill_of[name])

        def normed_dve(dve, name, gain, gain_tile):
            norm_dve(dve, norm_of[name])
            fill_dve(dve, fill_of[name], lambda j: norm_group(j, gain, gain_tile))

        param_pieces = []
        for name, src in (("norm_mix", norm_mix), ("norm_ffn", norm_ffn), ("norm_final", norm_final),
                          ("rw_mu", rw_mu), ("rw_w0", rw_w0), ("rw_a0", rw_a0), ("rw_k_k", rw_k_k),
                          ("rw_k_a", rw_k_a), ("rw_r_k", rw_r_k), ("rw_ln_w", rw_ln_w), ("rw_ln_b", rw_ln_b),
                          ("ret_gn_w", ret_gn_w)):
            r, n = PARAM_ROWS[name]
            merge = {1: None, 2: "a b -> (a b)", 3: "a b c -> (a b c)"}[len(src.shape)]
            rows = (src.rearrange(merge) if merge else src).rearrange("(r c) -> r c", c=P)
            done = 0
            while done < n:
                first, blk = (r + done) % P, (r + done) // P
                k = min(n - done, P - first)
                param_pieces.append((param_rows[first:first + k, blk, :], rows[done:done + k, :]))
                done += k
        table_loads = 16 * (1 + len(param_pieces))
        rows_of_block = [min(P, PARAM_ROWS["ret_gn_w"][0] + 2 * DT - P * b) for b in range(PARAM_BLOCKS)]

        block = ctx.enter_context(nc.Block())

        @block.sync
        def _(sp):
            sp.dma_start(x_rows[:], x_dram).then_inc(rows_in, 16)
            sp.dma_start(tab[:], table[:, 0:tab_cols]).then_inc(tables_in, 16)
            for dst, src in param_pieces:
                sp.dma_start(dst, src).then_inc(tables_in, 16)
            rwkv_sp(sp)
            for l in range(2):
                up_sp(sp, l)
                out_sp(sp, f"down{l}", w2s[l], FT)
                if l == 0:
                    ret_sp(sp)
                    out_sp(sp, "ret_out", ret_out, 2 * DT)
            for j in range(4):
                sp.wait_ge(out_ready, j + 1)
                sp.dma_start(out_dram[:, :, 512 * j:512 * j + 512],
                             out_rows[:, :, 512 * j:512 * j + 512]).then_inc(out_stored, 16)
            sp.wait_ge(out_stored, 64)

        @block.gpsimd
        def _(pool):
            rwkv_pool(pool)

        @block.scalar
        def _(act):
            rwkv_act(act)
            for l in range(2):
                normed_act(act, f"up{l}")
                up_act(act, l)
                out_act(act, f"down{l}", FT)
                if l == 0:
                    normed_act(act, "ret")
                    rope_act(act)
                    ret_act(act)
                    out_act(act, "ret_out", 2 * DT)
            norm_act(act, norm_of["final"])
            for j in range(4):
                act.wait_ge(out_turned, j + 1)
                nc.scalar.activation(out_rows[:, :, 512 * j:512 * j + 512], acc[:, 2 * (j % 2):2 * (j % 2) + 2],
                                     ACT.Copy).then_inc(out_ready, 1)

        @block.vector
        def _(dve):
            dve.sem_inc(up_free, 1)
            for b in range(PARAM_BLOCKS):
                dve.wait_ge(params_t, PARAM_BLOCKS)
                k = rows_of_block[b]
                nc.vector.tensor_copy(prm[:, P * b:P * b + k], acc[:, 6, P * b:P * b + k]).then_inc(params_ready, 1)
            for j in range(4):
                dve.wait_ge(x_turned, j + 1)
                nc.vector.tensor_copy(two_banks(x_res[:, 4 * j:4 * j + 4]),
                                      acc[:, 2 * (j % 2):2 * (j % 2) + 2]).then_inc(x_ready, 1)
            dve.wait_ge(params_ready, PARAM_BLOCKS)
            rwkv_dve(dve)
            for l in range(2):
                normed_dve(dve, f"up{l}", "norm_ffn", DT * l)
                up_dve(dve, l)
                out_dve(dve, f"down{l}", FT)
                if l == 0:
                    normed_dve(dve, "ret", "norm_mix", DT)
                    rope_dve(dve)
                    ret_dve(dve)
                    out_dve(dve, "ret_out", 2 * DT)
            norm_dve(dve, norm_of["final"])
            for j in range(4):
                if j >= 2:
                    dve.wait_ge(out_turned, j - 1)
                norm_group(j, "norm_final", 0).then_inc(hn_ready, 1)

        @block.tensor
        def _(pe):
            pe.wait_ge(tables_in, table_loads)
            for b in range(PARAM_BLOCKS):
                k = rows_of_block[b]
                mm = nc.tensor.transpose(acc[:, 6, P * b:P * b + k], param_rows[0:k, b, :], ident[0:k, 0:k])
                mm.then_inc(params_t, 1)
            pe.wait_ge(rows_in, 16)
            for j in range(4):
                if j >= 2:
                    pe.wait_ge(x_ready, j - 1)
                for k in range(4):
                    for tt in range(2):
                        mm = nc.tensor.transpose(bank_tile(2 * (j % 2), k)[:, P * tt:P * tt + P],
                                                 x_rows[:, tt, P * (4 * j + k):P * (4 * j + k) + P], ident)
                mm.then_inc(x_turned, 1)
            rwkv_pe(pe)
            for l in range(2):
                norm_pe(pe, norm_of[f"up{l}"])
                up_pe(pe, l, fill_of[f"up{l}"])
                down_pe(pe, l)
                if l == 0:
                    norm_pe(pe, norm_of["ret"])
                    ret_pe(pe, fill_of["ret"])

                    def before_block(b):
                        if b == 0:
                            pe.wait_ge(y_var, RET_HEADS)
                            pe.wait_ge(silu_g_done, RET_HEADS)
                            pe.wait_ge(ret_lo_done, RET_HEADS - 1)
                        else:
                            pe.wait_ge(v_evac, RET_HEADS)

                    out_pe(pe, "ret_out", ret_hi, ret_lo, 2 * DT, before_block,
                           lambda: pe.wait_ge(ret_lo_done, RET_HEADS))
            norm_pe(pe, norm_of["final"])
            for j in range(4):
                pe.wait_ge(hn_ready, 4 * len(fills) + j + 1)
                if j >= 2:
                    pe.wait_ge(out_ready, j - 1)
                for tt in range(2):
                    for k in range(4):
                        mm = nc.tensor.transpose(acc[:, 2 * (j % 2) + tt, P * k:P * k + P],
                                                 work[:, j % 2, k, P * tt:P * tt + P], ident)
                mm.then_inc(out_turned, 1)


_INS = ['x', 'positions', 'norm_mix', 'norm_ffn', 'norm_final', 'rw_mu', 'rw_w_rkv', 'rw_w0', 'rw_w1', 'rw_w2',
        'rw_a0', 'rw_a1', 'rw_a2', 'rw_g1', 'rw_g2', 'rw_k_k', 'rw_k_a', 'rw_r_k', 'rw_ln_w', 'rw_ln_b', 'rw_w_o',
        'ret_w_in', 'ret_gn_w', 'ret_w_out', 'ffn_w1', 'ffn_w3', 'ffn_w2']


def kernel(**inputs):
    import concourse.bacc as _bacc
    from concourse.bass_utils import run_bass_kernel_spmd as _run

    nc = _bacc.Bacc("TRN2", target_bir_lowering=False, num_devices=1)
    arrays, args = {}, []
    for name in _INS:
        a = np.ascontiguousarray(inputs[name])
        arrays[f"in_{name}"] = a
        args.append(nc.dram_tensor(f"in_{name}", a.shape, mybir.dt.from_np(a.dtype), kind="ExternalInput").ap())
    arrays["shape_table"] = shape_table()
    args.append(nc.dram_tensor("shape_table", (P, TABLE_WIDTH), F32, kind="ExternalInput").ap())
    args.append(nc.dram_tensor("out_0", (1, T, D), F32, kind="ExternalOutput").ap())
    trunk_program(nc, *args)
    r = _run(nc, [arrays], core_ids=[0])
    return r.results[0]["out_0"]
```

```python
from contextlib import ExitStack

import numpy as np

import concourse.bass as bass
from concourse import mybir

ALU = mybir.AluOpType
ACT = mybir.ActivationFunctionType
AX_X = mybir.AxisListType.X
F32 = mybir.dt.float32
F32R = mybir.dt.float32r
I32 = mybir.dt.int32

P = 128
T = 256
D = 2048
DT = D // P
F = 5632
FT = F // P
CHUNK = 64
NC = T // CHUNK
LORA = 96
GLORA = 256
RET_HEADS = 8
RET_DK = D // RET_HEADS
RET_DV = 2 * D // RET_HEADS
ROPE_BASE = 10000.0
NORM_EPS = 1e-6
RW_GN_EPS = 64e-5
RW_HEAD = 64
PAIRS = D // P
UNIT = 2048
UP_BLOCKS = F // 512

PARAM_ROWS = {}
_row = 0
for _name, _n in (("norm_mix", 2 * DT), ("norm_ffn", 2 * DT), ("norm_final", DT), ("rw_mu", 6 * DT), ("rw_w0", DT),
                  ("rw_a0", DT), ("rw_k_k", DT), ("rw_k_a", DT), ("rw_r_k", DT), ("rw_ln_w", DT), ("rw_ln_b", DT),
                  ("ret_gn_w", 2 * DT)):
    PARAM_ROWS[_name] = (_row, _n)
    _row += _n
PARAM_BLOCKS = -(-_row // P)
K_A_REST = _row
assert K_A_REST + DT <= PARAM_BLOCKS * P

TABLE_COLS = {}
_col = 0
for _name, _n in (("ident", P), ("ones", P), ("head_ones", P), ("ident2", 64), ("pair_mask", 2), ("strict_mask", 64),
                  ("chunk_mask", 2 * 2 * 64), ("scan_mask", T), ("inv_freq", 1), ("ret_decay", RET_HEADS * T)):
    TABLE_COLS[_name] = (_col, _n)
    _col += _n
TABLE_WIDTH = _col


def shape_table():
    t = np.zeros((P, TABLE_WIDTH), np.float32)

    def put(name, value):
        c, n = TABLE_COLS[name]
        t[:, c:c + n] = np.asarray(value, np.float32).reshape(P, n)

    p = np.arange(P)
    half, s = p // 64, p % 64
    tt = np.arange(64)
    put("ident", np.eye(P))
    put("ones", np.ones((P, P)))
    put("head_ones", half[:, None] == half[None, :])
    put("ident2", s[:, None] == tt[None, :])
    pair = half[:, None] == np.arange(2)[None, :]
    put("pair_mask", pair)
    causal = np.stack([s[:, None] < tt[None, :], s[:, None] <= tt[None, :]], 1)
    put("strict_mask", causal[:, 0])
    put("chunk_mask", causal[:, :, None, :] * pair[:, None, :, None])
    put("scan_mask", np.broadcast_to((np.arange(T) % CHUNK != 0)[None, :], (P, T)))
    put("inv_freq", 1.0 / ROPE_BASE ** (np.arange(P) / (RET_DK // 2 - 1)))
    gamma = 1.0 - 2.0 ** (-5.0 - np.arange(RET_HEADS))
    dist = np.arange(T)[None, :] - p[:, None]
    decay = np.where(dist[:, None, :] >= 0, gamma[None, :, None] ** np.maximum(dist, 0)[:, None, :], 0.0)
    put("ret_decay", decay * RET_DK ** -0.5)
    return t


def trunk_program(nc, x, positions, norm_mix, norm_ffn, norm_final, rw_mu, rw_w_rkv, rw_w0, rw_w1, rw_w2,
                  rw_a0, rw_a1, rw_a2, rw_g1, rw_g2, rw_k_k, rw_k_a, rw_r_k, rw_ln_w, rw_ln_b, rw_w_o,
                  ret_w_in, ret_gn_w, ret_w_out, ffn_w1, ffn_w3, ffn_w2, table, out):
    units = {}
    total = 0
    for name, n in (("decay", 2), ("rate", 2), ("key", 16), ("rec", 16), ("val", 16), ("gate", 4), ("rw_out", DT),
                    ("up0", 8 * UP_BLOCKS), ("down0", FT), ("ret", 12 * RET_HEADS), ("ret_out", 2 * DT),
                    ("up1", 8 * UP_BLOCKS), ("down1", FT)):
        units[name] = total
        total += n

    w1s = [ffn_w1[l].rearrange("(kt p) n -> p kt n", p=P) for l in range(2)]
    w3s = [ffn_w3[l].rearrange("(kt p) n -> p kt n", p=P) for l in range(2)]
    w2s = [ffn_w2[l].rearrange("(kt p) n -> p kt n", p=P) for l in range(2)]
    ret_in = ret_w_in[0].rearrange("(kt p) n -> p kt n", p=P)
    ret_out = ret_w_out[0].rearrange("(kt p) n -> p kt n", p=P)
    x_dram = x[0].rearrange("(tt p) n -> p tt n", p=P)
    out_dram = out[0].rearrange("(tt p) n -> p tt n", p=P)

    base = 16512
    KB = 1024

    def place(name, shape, offset, dtype=F32):
        return nc.alloc_sbuf_tensor_at(name, shape, dtype, offset=base + offset)

    x_res = place("x_res", [P, DT, T], 0)
    raw = place("raw", [P, 2, UNIT], 16 * KB)
    w_hi = place("w_hi", [P, 2, UNIT], 32 * KB, F32R)
    w_lo = place("w_lo", [P, 2, UNIT], 48 * KB, F32R)
    x_hi = place("x_hi", [P, DT, T], 64 * KB, F32R)
    x_lo = place("x_lo", [P, DT, T], 80 * KB, F32R)
    work = place("work", [P, 2, 4, T], 96 * KB)
    small = 104 * KB
    tab_cols = TABLE_COLS["ret_decay"][0]
    tab = place("tab", [P, tab_cols], small)
    small += 4 * tab_cols + 28
    small -= small % 32
    prm = place("prm", [P, PARAM_BLOCKS * P], small)
    small += 4 * PARAM_BLOCKS * P
    rstd = place("rstd", [P, T], small)
    rvar = place("rvar", [P, T], small + KB)
    rvar_at = small + KB
    small += 2 * KB
    zone = small + (-small) % 32
    hid_hi = place("hid_hi", [P, FT, T], zone, F32R)
    hid_lo = place("hid_lo", [P, FT, T], zone + 44 * KB, F32R)
    x_rows = place("x_rows", [P, 2, D], zone)
    param_rows = place("param_rows", [P, PARAM_BLOCKS, P], zone + 16 * KB)
    out_rows = place("out_rows", [P, 2, D], zone)
    ret_hi = place("ret_hi", [P, 2 * DT, T], zone, F32R)
    ret_lo = place("ret_lo", [P, 2 * DT, T], zone + 32 * KB, F32R)
    z = zone + 64 * KB
    ret_decay = place("ret_decay", [P, RET_HEADS, T], z)
    cos = place("cos", [P, T], z + 8 * KB)
    sin = place("sin", [P, T], z + 9 * KB)
    qk_rot = place("qk_rot", [P, 2, 2, T], z + 10 * KB)
    v_rows = place("v_rows", [P, 2, RET_DV], z + 14 * KB)
    probs = place("probs", [P, 3 * P], z + 18 * KB)
    silu_g = place("silu_g", [P, 4, T], z + 20 * KB)
    y_head = place("y_head", [P, 4, T], z + 24 * KB)
    assert base + z + 28 * KB <= nc.sbuf_usable_end and base + zone + 88 * KB <= nc.sbuf_usable_end
    pos_i = place("pos_i", [P, T], z + 14 * KB, I32)
    rot_a, rot_b, rot_c, rot_d = (work[:, k // 2, 2 * (k % 2):2 * (k % 2) + 2] for k in range(4))

    h_in = place("h_in", [P, DT, T + 1], zone)
    out_gate = place("out_gate", [P, DT, T], zone)
    quad_at = zone + 4 * DT * (T + 1)
    quad = place("quad", [P, 4, DT, T], quad_at)
    att_hi = place("att_hi", [P, DT, T], quad_at, F32R)
    att_lo = place("att_lo", [P, DT, T], quad_at + 16 * KB, F32R)
    solve_t = place("solve_t", [P, 1024], quad_at + 32 * KB)
    val_t = place("val_t", [P, 4, T], quad_at + 36 * KB)
    rk_t = place("rk_t", [P, 4, T], quad_at + 40 * KB)
    bonus = place("bonus", [P, DT, T], quad_at + 32 * KB)
    inv_at = quad_at + 64 * KB
    assert base + inv_at + 16 * KB <= nc.sbuf_usable_end
    prep_t = place("prep_t", [P, 4, T], inv_at)
    prep_x = place("prep_x", [P, 2, 4, T], inv_at + 4 * KB)
    b_wide = place("b_wide", [P, 2, NC, 2, 64], inv_at + 4 * KB)
    tri_rows = place("tri_rows", [P, 8, NC, 64], inv_at + 8 * KB)
    tri = place("tri", [P, 64, 64], inv_at)
    inv_t = place("inv_t", [P, PAIRS * NC, 64], inv_at)
    lora_hi = place("lora_hi", [P, 1, T], inv_at + 12 * KB, F32R)
    lora_lo = place("lora_lo", [P, 1, T], inv_at + 13 * KB, F32R)
    lora_mid = place("lora_mid", [P, 1, T], inv_at + 14 * KB)
    glora_hi = place("glora_hi", [P, 2, T], 96 * KB, F32R)
    glora_lo = place("glora_lo", [P, 2, T], 98 * KB, F32R)
    chunk_decay = place("chunk_decay", [P, PAIRS, NC], rvar_at)
    prep_inv = place("prep_inv", [P, 4, T], inv_at + 12 * KB)
    v_feat = place("v_feat", [P, DT, T], 64 * KB)
    y_all = place("y_all", [P, PAIRS, NC, 64], 80 * KB)
    scan_at = 32 * KB
    quad_wide = place("quad_wide", [P, 8, 4, 2, 64], scan_at)
    v_wide = place("v_wide", [P, 4, 2, 64], scan_at + 16 * KB)
    inv_wide = place("inv_wide", [P, 8, 2, 64], scan_at + 18 * KB)
    kbv_rows = place("kbv_rows", [P, 4, 2 * P + 64], scan_at + 22 * KB)
    state = place("state", [P, PAIRS, 64], scan_at + 27 * KB)
    mix_wide = place("mix_wide", [P, 4, 3, 2, 64], 96 * KB)
    x_stack = place("x_stack", [P, 2, 64], 102 * KB)
    u_stack = place("u_stack", [P, 2, 64], 102 * KB + 512)
    state_dec = place("state_dec", [P, 4, 64], 103 * KB)
    y_wide = place("y_wide", [P, 4, NC, 2, 64], inv_at)
    y_mean = place("y_mean", [P, 64], inv_at + 8 * KB)
    y_inv = place("y_inv", [P, 64], inv_at + 9 * KB)
    y_scale = place("y_scale", [P, 64, 2], inv_at + 10 * KB)
    att = place("att", [P, DT, T], 64 * KB)

    def const(name):
        c, n = TABLE_COLS[name]
        return tab[:, c:c + n]

    def param(name, tile):
        r, _ = PARAM_ROWS[name]
        return prm[:, r + tile:r + tile + 1]

    ident, ones = const("ident"), const("ones")

    with ExitStack() as ctx:
        def sem(name):
            return ctx.enter_context(nc.semaphore(name))

        acc = ctx.enter_context(nc.psum_tensor("acc", [P, 8, 512], F32))

        w_loaded = [sem("w_loaded0"), sem("w_loaded1")]
        hi_done = sem("hi_done")
        lo_done = sem("lo_done")
        unit_used = sem("unit_used")
        tables_in = sem("tables_in")
        rows_in = sem("rows_in")
        params_t = sem("params_t")
        params_ready = sem("params_ready")
        k_rest_ready = sem("k_rest_ready")
        x_turned = sem("x_turned")
        x_ready = sem("x_ready")
        norm_sq = sem("norm_sq")
        norm_stat = sem("norm_stat")
        norm_var = sem("norm_var")
        norm_eps_added = sem("norm_eps_added")
        norm_rstd = sem("norm_rstd")
        hn_ready = sem("hn_ready")
        hn_hi = sem("hn_hi")
        hn_lo = sem("hn_lo")
        up_free = sem("up_free")
        silu_done = sem("silu_done")
        hid_hi_done = sem("hid_hi_done")
        hid_lo_done = sem("hid_lo_done")
        out_turned = sem("out_turned")
        out_ready = sem("out_ready")
        out_stored = sem("out_stored")
        pos_in = sem("pos_in")
        decay_in = sem("decay_in")
        rope_step = sem("rope_step")
        rope_sin = sem("rope_sin")
        rope_ready = sem("rope_ready")
        rot_mul = sem("rot_mul")
        rot_done = sem("rot_done")
        v_evac = sem("v_evac")
        silu_g_done = sem("silu_g_done")
        scores_done = sem("scores_done")
        probs_done = sem("probs_done")
        y_done = sem("y_done")
        y_evac = sem("y_evac")
        mean_done = sem("mean_done")
        centred = sem("centred")
        y_sq = sem("y_sq")
        var_done = sem("var_done")
        y_eps_added = sem("y_eps_added")
        y_var = sem("y_var")
        y_rstd = sem("y_rstd")
        y_scaled = sem("y_scaled")
        gated = sem("gated")
        ret_hi_done = sem("ret_hi_done")
        ret_lo_done = sem("ret_lo_done")

        def load_unit(sp, n, src, shape, off=0, parts=P):
            if n >= 2:
                sp.wait_ge(lo_done, n - 1 + off)
            dst = raw[0:parts, n % 2, 0:shape[0] * shape[1]].rearrange("p (k n) -> p k n", k=shape[0])
            sp.dma_start(dst, src).then_inc(w_loaded[n % 2], 16)

        def split_hi(act, n, off=0, parts=P, width=UNIT):
            act.wait_ge(w_loaded[n % 2], 16 * (n // 2 + 1) + 8 * off)
            if n >= 2:
                act.wait_ge(unit_used, n - 1 + off)
            nc.scalar.activation(w_hi[0:parts, n % 2, 0:width], raw[0:parts, n % 2, 0:width],
                                 ACT.Copy).then_inc(hi_done, 1)

        def split_lo(dve, n, off=0, parts=P, width=UNIT):
            dve.wait_ge(hi_done, n + 1 + off)
            nc.vector.tensor_tensor(w_lo[0:parts, n % 2, 0:width], raw[0:parts, n % 2, 0:width],
                                    w_hi[0:parts, n % 2, 0:width].bitcast(F32), ALU.subtract).then_inc(lo_done, 1)

        def unit_product(pe, n, shape, xs, tile_out, first, last, off=0, parts=P):
            pe.wait_ge(lo_done, n + 1 + off)
            rows, cols = shape
            hi = w_hi[0:parts, n % 2, 0:rows * cols].rearrange("p (k n) -> p k n", k=rows)
            lo = w_lo[0:parts, n % 2, 0:rows * cols].rearrange("p (k n) -> p k n", k=rows)
            for k in range(rows):
                a_hi, a_lo = xs(k)
                for f in range(-(-cols // P)):
                    c = slice(f * P, min((f + 1) * P, cols))
                    for m, (w, a) in enumerate(((hi, a_hi), (hi, a_lo), (lo, a_hi))):
                        mm = nc.tensor.matmul(tile_out(f), w[:, k, c], a,
                                              start=(first and k == 0 and m == 0 and f % 2 == 0),
                                              stop=(last and k == rows - 1 and m == 2), skip_group_check=True)
            mm.then_inc(unit_used, 1)

        def x_tiles(k0):
            return lambda k: (x_hi[:, k0 + k, :], x_lo[:, k0 + k, :])

        def bank_tile(b, f):
            if isinstance(b, int):
                return acc[:, b + f // 2, T * (f % 2):T * (f % 2) + T]
            return acc[:, bass.ds(b + f // 2, 1), T * (f % 2):T * (f % 2) + T].rearrange("p a t -> p (a t)")

        def norm_act(act, q, early=None):
            for j in range(4):
                act.wait_ge(x_ready, 4 * q + j + 1)
                if j >= 2:
                    act.wait_ge(norm_stat, 4 * q + j - 1)
                nc.scalar.activation(work[:, j % 2], x_res[:, 4 * j:4 * j + 4], ACT.Square).then_inc(norm_sq, 1)
            if early is not None:
                early(0)
                early(1)
            act.wait_ge(norm_var, q + 1)
            nc.scalar.activation(rstd[:], rvar[:], ACT.Sqrt).then_inc(norm_rstd, 1)

        def norm_pe(pe, q):
            for j in range(4):
                pe.wait_ge(norm_sq, 4 * q + j + 1)
                for k in range(4):
                    mm = nc.tensor.matmul(acc[:, 7, 0:T], ones, work[:, j % 2, k], start=(j == 0 and k == 0),
                                          stop=(j == 3 and k == 3))
                mm.then_inc(norm_stat, 1)

        def norm_dve(dve, q, early=None):
            if early is not None:
                early(0)
                early(1)
            dve.wait_ge(norm_stat, 4 * q + 4)
            nc.vector.tensor_scalar(rvar[:], acc[:, 7, 0:T], 1.0 / D, NORM_EPS, ALU.mult,
                                    ALU.add).then_inc(norm_eps_added, 1)
            dve.wait_ge(norm_eps_added, q + 1)
            nc.vector.reciprocal(rvar[:], rvar[:]).then_inc(norm_var, 1)
            dve.wait_ge(norm_rstd, q + 1)

        def norm_group(j, gain, gain_tile):
            for k in range(4):
                last = nc.vector.scalar_tensor_tensor(out=work[:, j % 2, k], in0=x_res[:, 4 * j + k],
                                                      scalar=param(gain, gain_tile + 4 * j + k), in1=rstd[:],
                                                      op0=ALU.mult, op1=ALU.mult)
            return last

        def fill_act(act, i, before_group=None, after_group=None):
            for j in range(4):
                if before_group is not None:
                    before_group(j)
                act.wait_ge(hn_ready, 4 * i + j + 1)
                nc.scalar.activation(x_hi[:, 4 * j:4 * j + 4], work[:, j % 2], ACT.Copy).then_inc(hn_hi, 1)
                if after_group is not None:
                    after_group(j)

        def fill_dve(dve, i, group, after_group=None):
            def low(j):
                dve.wait_ge(hn_hi, 4 * i + j + 1)
                nc.vector.tensor_tensor(x_lo[:, 4 * j:4 * j + 4], work[:, j % 2],
                                        x_hi[:, 4 * j:4 * j + 4].bitcast(F32), ALU.subtract).then_inc(hn_lo, 1)

            for j in range(4):
                if j >= 2:
                    low(j - 2)
                    dve.wait_ge(hn_lo, 4 * i + j - 1)
                group(j).then_inc(hn_ready, 1)
                if after_group is not None:
                    after_group(j)
            low(2)
            low(3)
            dve.wait_ge(hn_lo, 4 * i + 4)

        def up_sp(sp, l):
            n0 = units[f"up{l}"]
            with sp.Fori(0, UP_BLOCKS) as i:
                for u in range(8):
                    w = (w1s, w3s)[u // 4][l]
                    load_unit(sp, n0 + u, w[:, 4 * (u % 4):4 * (u % 4) + 4, bass.ds(i * 512, 512)], (4, 512), off=8 * i)

        def up_act(act, l):
            n0 = units[f"up{l}"]

            def block(i, behind):
                off = 8 * i
                if behind:
                    split_hi(act, n0, off)
                    split_hi(act, n0 + 1, off)
                    silu(i - 1)
                split_hi(act, n0 + 2, off)
                split_hi(act, n0 + 3, off)
                split_hi(act, n0 + 4, off)
                split_hi(act, n0 + 5, off)
                if behind:
                    hidden_hi(i - 1)
                split_hi(act, n0 + 6, off)
                split_hi(act, n0 + 7, off)

            def silu(i):
                act.wait_ge(unit_used, 8 * i + n0 + 8)
                nc.scalar.activation(work[:, 0].rearrange("p a t -> p (a t)").rearrange("p (b s) -> p b s", b=2),
                                     acc[:, bass.ds((i % 2) * 4, 2), :], ACT.Silu).then_inc(silu_done, 1)

            def hidden_hi(i):
                act.wait_ge(up_free, UP_BLOCKS * l + 2 + i)
                nc.scalar.activation(hid_hi[:, bass.ds(4 * i, 4), :], work[:, 1], ACT.Copy).then_inc(hid_hi_done, 1)

            block(0, False)
            with act.Fori(1, UP_BLOCKS) as i:
                block(i, True)
            silu(UP_BLOCKS - 1)
            hidden_hi(UP_BLOCKS - 1)

        def up_dve(dve, l):
            n0 = units[f"up{l}"]

            def block(i, behind):
                off = 8 * i
                for u in range(0 if behind else 2, 3):
                    split_lo(dve, n0 + u, off)
                if behind:
                    glu(i - 1)
                for u in range(3, 7):
                    split_lo(dve, n0 + u, off)
                if behind:
                    hidden_lo(i - 1)
                split_lo(dve, n0 + 7, off)

            def glu(i):
                dve.wait_ge(silu_done, UP_BLOCKS * l + 1 + i)
                dve.wait_ge(hid_lo_done, UP_BLOCKS * l + i)
                nc.vector.tensor_tensor(work[:, 1].rearrange("p a t -> p (a t)").rearrange("p (b s) -> p b s", b=2),
                                        acc[:, bass.ds((i % 2) * 4 + 2, 2), :],
                                        work[:, 0].rearrange("p a t -> p (a t)").rearrange("p (b s) -> p b s", b=2),
                                        ALU.mult).then_inc(up_free, 1)

            def hidden_lo(i):
                dve.wait_ge(hid_hi_done, UP_BLOCKS * l + 1 + i)
                nc.vector.tensor_tensor(hid_lo[:, bass.ds(4 * i, 4), :], work[:, 1],
                                        hid_hi[:, bass.ds(4 * i, 4), :].bitcast(F32),
                                        ALU.subtract).then_inc(hid_lo_done, 1)

            block(0, False)
            with dve.Fori(1, UP_BLOCKS) as i:
                block(i, True)
            glu(UP_BLOCKS - 1)
            hidden_lo(UP_BLOCKS - 1)

        def up_pe(pe, l, fill):
            n0 = units[f"up{l}"]
            with pe.Fori(0, UP_BLOCKS) as i:
                pe.wait_ge(up_free, UP_BLOCKS * l + i)
                for u in range(8):
                    pe.wait_ge(hn_lo, 4 * fill + u % 4 + 1)
                    bank = (i % 2) * 4 + 2 * (u // 4)
                    unit_product(pe, n0 + u, (4, 512), x_tiles(4 * (u % 4)), lambda f: bank_tile(bank, f),
                                 u % 4 == 0, u % 4 == 3, off=8 * i)

        def out_sp(sp, stage, w, kt):
            for b in range(2):
                n0 = units[stage] + b * kt // 2
                with sp.Fori(0, kt // 4) as j:
                    for u in range(2):
                        load_unit(sp, n0 + u, w[:, bass.ds(4 * j + 2 * u, 2), 1024 * b:1024 * b + 1024], (2, 1024),
                                  off=2 * j)

        def out_act(act, stage, kt, early=False):
            for b in range(2):
                n0 = units[stage] + b * kt // 2
                with act.Fori(1 if early and b == 0 else 0, kt // 4) as j:
                    for u in range(2):
                        split_hi(act, n0 + u, off=2 * j)

        def out_dve(dve, stage, kt, early=False):
            n0 = units[stage]

            def add(b):
                for g in range(2):
                    dve.wait_ge(unit_used, n0 + (b + 1) * kt // 2)
                    o = x_res[:, 8 * b + 4 * g:8 * b + 4 * g + 4].rearrange("p a t -> p (a t)")
                    o = o.rearrange("p (c s) -> p c s", c=2)
                    bank = 4 * (1 - b) + 2 * g
                    nc.vector.tensor_tensor(o, acc[:, bank:bank + 2], o, ALU.add).then_inc(x_ready, 1)

            with dve.Fori(1 if early else 0, kt // 4) as j:
                for u in range(2):
                    split_lo(dve, n0 + u, off=2 * j)
            n1 = n0 + kt // 2
            split_lo(dve, n1)
            split_lo(dve, n1 + 1)
            add(0)
            with dve.Fori(1, kt // 4) as j:
                for u in range(2):
                    split_lo(dve, n1 + u, off=2 * j)
            add(1)

        def out_pe(pe, stage, hi, lo, kt, before_block, before_last):
            for b in range(2):
                n0 = units[stage] + b * kt // 2
                bank = 4 * (1 - b)

                def pair(j, first, last):
                    for u in range(2):
                        def xs(k):
                            if isinstance(j, int):
                                return hi[:, 4 * j + 2 * u + k, :], lo[:, 4 * j + 2 * u + k, :]
                            at = bass.ds(4 * j + 2 * u + k, 1)
                            return (hi[:, at, :].rearrange("p a t -> p (a t)"), lo[:, at, :].rearrange("p a t -> p (a t)"))
                        off, n = (0, n0 + 2 * j + u) if isinstance(j, int) else (2 * j, n0 + u)
                        unit_product(pe, n, (2, 1024), xs, lambda f: bank_tile(bank, f), first and u == 0,
                                     last and u == 1, off=off)

                before_block(b)
                pair(0, True, False)
                with pe.Fori(1, kt // 4 - 1) as j:
                    pair(j, False, False)
                if b == 0:
                    before_last()
                pair(kt // 4 - 1, False, True)

        def down_pe(pe, l):
            def before_block(b):
                pe.wait_ge(up_free, UP_BLOCKS * (l + 1) + b)
                if b == 0:
                    pe.wait_ge(hid_lo_done, UP_BLOCKS * (l + 1) - 1)

            out_pe(pe, f"down{l}", hid_hi, hid_lo, FT, before_block,
                   lambda: pe.wait_ge(hid_lo_done, UP_BLOCKS * (l + 1)))

        TWO_PI = 2.0 * np.pi
        parts_2pi = []
        rest = TWO_PI
        for _ in range(3):
            e = 2.0 ** (7 - int(np.floor(np.log2(rest))))
            parts_2pi.append(float(np.floor(rest * e) / e))
            rest -= parts_2pi[-1]
        parts_2pi.append(float(np.float32(rest)))

        def rope_dve(dve):
            step = 0

            def then(ins):
                nonlocal step
                step += 1
                ins.then_inc(rope_step, 1)
                dve.wait_ge(rope_step, step)

            ang, turns, half = rot_b[:, 0], rot_b[:, 1], rot_c[:, 0]
            dve.wait_ge(pos_in, 16)
            then(nc.vector.tensor_copy(ang, pos_i[:]))
            then(nc.vector.tensor_scalar(ang, ang, const("inv_freq"), None, ALU.mult))
            then(nc.vector.tensor_scalar(turns, ang, 1.0 / TWO_PI, 1.5 * 2.0 ** 23, ALU.mult, ALU.add))
            then(nc.vector.tensor_scalar(turns, turns, 1.5 * 2.0 ** 23, None, ALU.subtract))
            for c in parts_2pi:
                then(nc.vector.scalar_tensor_tensor(out=ang, in0=turns, scalar=-c, in1=ang, op0=ALU.mult, op1=ALU.add))
            pi_below = 3.1415925
            then(nc.vector.tensor_scalar(ang, ang, pi_below, -pi_below, ALU.min, ALU.max))
            dve.wait_ge(rope_sin, 2)
            then(nc.vector.tensor_tensor(half, half, half, ALU.mult))
            nc.vector.tensor_scalar(cos[:], half, -2.0, 1.0, ALU.mult, ALU.add).then_inc(rope_ready, 1)

        rope_steps = 5 + len(parts_2pi)

        def rope_act(act):
            act.wait_ge(x_ready, 4 * (norm_of["ret"] + 1))
            act.dma_start(pos_i[:], positions.to_broadcast([P, T])).then_inc(pos_in, 16)
            c, n = TABLE_COLS["ret_decay"]
            act.dma_start(ret_decay[:], table[:, c:c + n].rearrange("p (h t) -> p h t", h=RET_HEADS)).then_inc(decay_in, 16)
            act.wait_ge(rope_step, rope_steps)
            nc.scalar.activation(sin[:], rot_b[:, 0], ACT.Sin).then_inc(rope_sin, 1)
            nc.scalar.activation(rot_c[:, 0], rot_b[:, 0], ACT.Sin, scale=0.5).then_inc(rope_sin, 1)

        n_ret = units["ret"]

        def ret_sp(sp):
            with sp.Fori(0, RET_HEADS) as h:
                off = 12 * h
                for u in range(4):
                    src = ret_in[:, 8 * (u % 2):8 * (u % 2) + 8, bass.ds(D * (u // 2) + RET_DK * h, RET_DK)]
                    load_unit(sp, n_ret + u, src, (8, RET_DK), off=off)
                for u in range(8):
                    src = ret_in[:, 4 * (u % 4):4 * (u % 4) + 4, bass.ds(2 * D * (1 + u // 4) + RET_DV * h, RET_DV)]
                    load_unit(sp, n_ret + 4 + u, src, (4, RET_DV), off=off)

        def ret_pe(pe, fill):
            def values_unit(u, off):
                n = n_ret + 4 + u
                pe.wait_ge(lo_done, n + 1 + off)
                hi = w_hi[:, n % 2, :].rearrange("p (k n) -> p k n", k=4)
                lo = w_lo[:, n % 2, :].rearrange("p (k n) -> p k n", k=4)
                for k in range(4):
                    for tt in range(2):
                        c = slice(P * tt, P * tt + P)
                        for m, (a, w) in enumerate(((x_hi, hi), (x_lo, hi), (x_hi, lo))):
                            mm = nc.tensor.matmul(acc[:, 2 + tt, :], a[:, 4 * u + k, c], w[:, k, :],
                                                  start=(u == 0 and k == 0 and m == 0),
                                                  stop=(u == 3 and k == 3 and m == 2), skip_group_check=True)
                mm.then_inc(unit_used, 1)

            def outputs(h):
                pe.wait_ge(probs_done, 1 + h)
                pe.wait_ge(v_evac, 1 + h)
                pe.wait_ge(y_var, h)
                for f in range(4):
                    c = slice(P * f, P * f + P)
                    nc.tensor.matmul(bank_tile(6, f), v_rows[:, 0, c], probs[:, 0:T], start=(f % 2 == 0), stop=False,
                                     skip_group_check=True)
                    mm = nc.tensor.matmul(bank_tile(6, f)[:, P:T], v_rows[:, 1, c], probs[:, T:T + P], start=False,
                                          stop=True, skip_group_check=True)
                mm.then_inc(y_done, 1)

            def head_sum(h, ready, src, col, done):
                pe.wait_ge(ready, 1 + h)
                for f in range(4):
                    mm = nc.tensor.matmul(acc[:, 6, col:col + T], ones, src[:, f], start=(f == 0), stop=(f == 3),
                                          skip_group_check=True)
                mm.then_inc(done, 1)

            def scores(h):
                pe.wait_ge(rot_done, 1 + h)
                for jt in range(2):
                    for d in range(2):
                        mm = nc.tensor.matmul(acc[:, 7, T * jt:T + P * jt], qk_rot[:, 1, d, P * jt:P * jt + P],
                                              qk_rot[:, 0, d, P * jt:T], start=(jt == 0 and d == 0), stop=(d == 1),
                                              skip_group_check=True)
                mm.then_inc(scores_done, 1)

            def head(h, behind):
                off = 12 * h
                if behind:
                    pe.wait_ge(rot_done, h)
                for u in range(4):
                    if not behind:
                        pe.wait_ge(hn_lo, 4 * fill + 2 * (u % 2) + 2)
                    unit_product(pe, n_ret + u, (8, RET_DK), x_tiles(8 * (u % 2)), lambda f: bank_tile(u // 2, f),
                                 u % 2 == 0, u % 2 == 1, off=off)
                if behind:
                    outputs(h - 1)
                values_unit(0, off)
                values_unit(1, off)
                if behind:
                    head_sum(h - 1, y_evac, y_head, 0, mean_done)
                values_unit(2, off)
                values_unit(3, off)
                if behind:
                    head_sum(h - 1, y_sq, work[:, 0], T, var_done)
                scores(h)
                if behind:
                    pe.wait_ge(silu_g_done, h)
                for u in range(4):
                    unit_product(pe, n_ret + 8 + u, (4, 512), x_tiles(4 * u), lambda f: bank_tile(4, f), u == 0,
                                 u == 3, off=off)

            head(0, False)
            with pe.Fori(1, RET_HEADS) as h:
                head(h, True)
            h = RET_HEADS - 1
            outputs(h)
            head_sum(h, y_evac, y_head, 0, mean_done)
            head_sum(h, y_sq, work[:, 0], T, var_done)

        def two_banks(ap):
            return ap.rearrange("p a t -> p (a t)").rearrange("p (b s) -> p b s", b=2)

        def ret_act(act):
            def silu(h):
                act.wait_ge(unit_used, n_ret + 12 + 12 * h)
                act.wait_ge(gated, h)
                nc.scalar.activation(two_banks(silu_g[:]), acc[:, 4:6], ACT.Silu).then_inc(silu_g_done, 1)

            def take_y(h):
                act.wait_ge(y_done, 1 + h)
                act.wait_ge(gated, h)
                nc.scalar.activation(two_banks(y_head[:]), acc[:, 6:8], ACT.Copy).then_inc(y_evac, 1)

            def square(h):
                act.wait_ge(centred, 1 + h)
                nc.scalar.activation(work[:, 0], y_head[:], ACT.Square).then_inc(y_sq, 1)

            def root(h):
                act.wait_ge(y_var, 1 + h)
                nc.scalar.activation(rstd[:], rvar[:], ACT.Sqrt).then_inc(y_rstd, 1)

            def take_v(h):
                act.wait_ge(unit_used, n_ret + 8 + 12 * h)
                act.wait_ge(y_done, h)
                nc.scalar.activation(v_rows[:], acc[:, 2:4], ACT.Copy).then_inc(v_evac, 1)

            def high(h):
                act.wait_ge(gated, 1 + h)
                nc.scalar.activation(ret_hi[:, bass.ds(4 * h, 4), :], work[:, 1], ACT.Copy).then_inc(ret_hi_done, 1)

            def head(h, behind):
                off = 12 * h
                if behind:
                    split_hi(act, n_ret, off)
                    split_hi(act, n_ret + 1, off)
                    silu(h - 1)
                split_hi(act, n_ret + 2, off)
                split_hi(act, n_ret + 3, off)
                split_hi(act, n_ret + 4, off)
                split_hi(act, n_ret + 5, off)
                if behind:
                    take_y(h - 1)
                split_hi(act, n_ret + 6, off)
                split_hi(act, n_ret + 7, off)
                if behind:
                    square(h - 1)
                split_hi(act, n_ret + 8, off)
                split_hi(act, n_ret + 9, off)
                if behind:
                    root(h - 1)
                take_v(h)
                split_hi(act, n_ret + 10, off)
                if behind:
                    high(h - 1)
                split_hi(act, n_ret + 11, off)

            head(0, False)
            with act.Fori(1, RET_HEADS) as h:
                head(h, True)
            h = RET_HEADS - 1
            silu(h)
            take_y(h)
            square(h)
            root(h)
            high(h)

        def ret_dve(dve):
            def rotate(h, behind):
                dve.wait_ge(unit_used, n_ret + 4 + 12 * h)
                dve.wait_ge(scores_done, h)
                dve.wait_ge(rot_done, h)
                if behind:
                    dve.wait_ge(ret_lo_done, h - 1)
                first, second = acc[:, 0:2, 0:T], acc[:, 0:2, T:2 * T]
                c2 = cos[:].rearrange("p (a t) -> p a t", a=1).to_broadcast([P, 2, T])
                s2 = sin[:].rearrange("p (a t) -> p a t", a=1).to_broadcast([P, 2, T])
                nc.vector.tensor_tensor(rot_a, first, c2, ALU.mult)
                nc.vector.tensor_tensor(rot_b, second, s2, ALU.mult)
                nc.vector.tensor_tensor(rot_c, first, s2, ALU.mult)
                nc.vector.tensor_tensor(rot_d, second, c2, ALU.mult).then_inc(rot_mul, 1)
                dve.wait_ge(rot_mul, 1 + h)
                nc.vector.tensor_tensor(qk_rot[:, :, 0, :], rot_a, rot_b, ALU.subtract)
                nc.vector.tensor_tensor(qk_rot[:, :, 1, :], rot_c, rot_d, ALU.add).then_inc(rot_done, 1)

            def decay_scores(h):
                dve.wait_ge(scores_done, 1 + h)
                dve.wait_ge(y_done, h)
                d = ret_decay[:, bass.ds(h, 1), :].rearrange("p a t -> p (a t)")
                nc.vector.tensor_tensor(probs[:, 0:T], acc[:, 7, 0:T], d, ALU.mult)
                nc.vector.tensor_tensor(probs[:, T:T + P], acc[:, 7, T:T + P], d[:, 0:P], ALU.mult).then_inc(probs_done, 1)

            def centre(h):
                dve.wait_ge(mean_done, 1 + h)
                mean = acc[:, 6, 0:T]
                for f in range(4):
                    last = nc.vector.scalar_tensor_tensor(out=y_head[:, f], in0=mean, scalar=-1.0 / RET_DV,
                                                          in1=y_head[:, f], op0=ALU.mult, op1=ALU.add)
                last.then_inc(centred, 1)

            def variance(h):
                dve.wait_ge(var_done, 1 + h)
                dve.wait_ge(y_rstd, h)
                nc.vector.tensor_scalar(rvar[:], acc[:, 6, T:2 * T], 1.0 / RET_DV, NORM_EPS, ALU.mult,
                                        ALU.add).then_inc(y_eps_added, 1)
                dve.wait_ge(y_eps_added, 1 + h)
                nc.vector.reciprocal(rvar[:], rvar[:]).then_inc(y_var, 1)

            def gate(h):
                dve.wait_ge(y_rstd, 1 + h)
                r0, _ = PARAM_ROWS["ret_gn_w"]
                for f in range(4):
                    gain = prm[:, r0 + 4 * h + f:r0 + 4 * h + f + 1] if isinstance(h, int) else prm[:, bass.ds(4 * h + (r0 + f), 1)]
                    last = nc.vector.scalar_tensor_tensor(out=y_head[:, f], in0=y_head[:, f], scalar=gain, in1=rstd[:],
                                                          op0=ALU.mult, op1=ALU.mult)
                last.then_inc(y_scaled, 1)
                dve.wait_ge(y_scaled, 1 + h)
                dve.wait_ge(silu_g_done, 1 + h)
                dve.wait_ge(ret_lo_done, h)
                nc.vector.tensor_tensor(work[:, 1], y_head[:], silu_g[:], ALU.mult).then_inc(gated, 1)

            def low(h):
                dve.wait_ge(ret_hi_done, 1 + h)
                nc.vector.tensor_tensor(ret_lo[:, bass.ds(4 * h, 4), :], work[:, 1],
                                        ret_hi[:, bass.ds(4 * h, 4), :].bitcast(F32), ALU.subtract).then_inc(ret_lo_done, 1)

            def head(h, behind):
                off = 12 * h
                for u in range(0 if behind else 2, 6):
                    split_lo(dve, n_ret + u, off)
                rotate(h, behind)
                split_lo(dve, n_ret + 6, off)
                if behind:
                    centre(h - 1)
                split_lo(dve, n_ret + 7, off)
                split_lo(dve, n_ret + 8, off)
                if behind:
                    variance(h - 1)
                split_lo(dve, n_ret + 9, off)
                decay_scores(h)
                if behind:
                    gate(h - 1)
                split_lo(dve, n_ret + 10, off)
                split_lo(dve, n_ret + 11, off)
                if behind:
                    low(h - 1)

            dve.wait_ge(rope_ready, 1)
            dve.wait_ge(decay_in, 16)
            head(0, False)
            with dve.Fori(1, RET_HEADS) as h:
                head(h, True)
            h = RET_HEADS - 1
            centre(h)
            variance(h)
            gate(h)
            low(h)

        SLOT_K, SLOT_B, SLOT_A, SLOT_R = range(4)
        DECAY_SCALE = float(np.exp(-0.5))
        GROUPS = PAIRS * NC
        n_dec, n_rate, n_gate = (units[k] for k in ("decay", "rate", "gate"))
        MU = {"rec": 0, "decay": 1, "key": 2, "val": 3, "rate": 4, "gate": 5}
        BLOCKS_BEFORE = {"key": 0, "rec": 4, "val": 8}
        W_ROW = {"rec": 0, "key": 1, "val": 2}

        h_ready = sem("h_ready")
        h_zero = sem("h_zero")
        mix_diff = sem("mix_diff")
        lora_act = sem("lora_act")
        lora_hi_done = sem("lora_hi_done")
        lora_lo_done = sem("lora_lo_done")
        sig_done = sem("sig_done")
        cum_done = sem("cum_done")
        block_free = sem("block_free")
        kk_raw = sem("kk_raw")
        kk_sq = sem("kk_sq")
        kk_sum = sem("kk_sum")
        kk_root = sem("kk_root")
        kk_step = sem("kk_step")
        cum_gap = sem("cum_gap")
        decayed = sem("decayed")
        prep_step = sem("prep_step")
        prep_done = sem("prep_done")
        b_wide_done = sem("b_wide_done")
        tri_mm = sem("tri_mm")
        tri_masked = sem("tri_masked")
        tri_stored = [sem("tri_stored0"), sem("tri_stored1")]
        tri_loaded = sem("tri_loaded")
        a_stored = sem("a_stored")
        solve_step = sem("solve_step")
        inv_stored = sem("inv_stored")
        inv_loaded = sem("inv_loaded")
        val_out = sem("val_out")
        rk_done = sem("rk_done")
        rk_sum = sem("rk_sum")
        bonus_done = sem("bonus_done")
        val_stored = sem("val_stored")
        bonus_stored = sem("bonus_stored")
        gate_out = sem("gate_out")
        v_loaded = sem("v_loaded")
        bonus_loaded = sem("bonus_loaded")
        wide_done = sem("wide_done")
        state_zero = sem("state_zero")
        m_mm = sem("m_mm")
        m_done = sem("m_done")
        kbv_done = sem("kbv_done")
        x_mm = sem("x_mm")
        x_done = sem("x_done")
        u_mm = sem("u_mm")
        u_done = sem("u_done")
        y_mm = sem("y_mm")
        y_taken = sem("y_taken")
        s_mm = sem("s_mm")
        dec_done = sem("dec_done")
        s_done = sem("s_done")
        ln_step = sem("ln_step")
        ln_centred = sem("ln_centred")
        ln_sq = sem("ln_sq")
        ln_var = sem("ln_var")
        ln_scale = sem("ln_scale")
        att_gain = sem("att_gain")
        att_bonus = sem("att_bonus")
        ln_root = sem("ln_root")
        y_wide_first = sem("y_wide_first")
        y_wide_done = sem("y_wide_done")
        yt_mm = sem("yt_mm")
        att_ready = sem("att_ready")
        att_hi_done = sem("att_hi_done")
        att_lo_done = sem("att_lo_done")

        tri_dram = nc.dram_tensor("tri_dram", (P, 64 * 64), F32, kind="Internal").ap()
        inv_dram = nc.dram_tensor("inv_dram", (P, 64 * 64), F32, kind="Internal").ap()
        a_dram = nc.dram_tensor("a_dram", (P, DT * T), F32, kind="Internal").ap()
        v_dram = nc.dram_tensor("v_dram", (P, DT, T), F32, kind="Internal").ap()
        bonus_dram = nc.dram_tensor("bonus_dram", (P, DT, T), F32, kind="Internal").ap()

        def stacked(dram, g0, n):
            return dram[2 * g0:2 * (g0 + n), :].rearrange("(g h) (s t) -> g (h s) t", h=2, s=64).rearrange("g r t -> r g t")

        def flat(ap):
            return ap.rearrange("p a t -> p (a t)")

        def param4(name, i, k):
            r, _ = PARAM_ROWS[name]
            if isinstance(i, int):
                return prm[:, r + 4 * i + k:r + 4 * i + k + 1]
            return prm[:, bass.ds(4 * i + (r + k), 1)]

        def lora_sp(sp, n, down, up):
            k = down.shape[1]
            load_unit(sp, n, down.rearrange("(kt p) n -> p kt n", p=P), (DT, k))
            load_unit(sp, n + 1, up.rearrange("p (a n) -> p a n", a=1), (1, D), parts=k)

        def rwkv_sp(sp):
            lora_sp(sp, n_dec, rw_w1[0], rw_w2[0])
            lora_sp(sp, n_rate, rw_a1[0], rw_a2[0])
            for name in ("key", "rec", "val"):
                w = rw_w_rkv[0, W_ROW[name]].rearrange("(kt p) n -> p kt n", p=P)
                with sp.Fori(0, 4) as i:
                    for u in range(4):
                        load_unit(sp, units[name] + u, w[:, 4 * u:4 * u + 4, bass.ds(i * 512, 512)], (4, 512), off=4 * i)
            g1 = rw_g1[0].rearrange("(kt p) n -> p kt n", p=P)
            g2 = rw_g2[0].rearrange("(kt p) n -> p kt n", p=P)
            for u in range(2):
                load_unit(sp, n_gate + u, g1[:, 8 * u:8 * u + 8, :], (8, GLORA))
            for u in range(2):
                load_unit(sp, n_gate + 2 + u, g2[:, u:u + 1, :], (1, D))
            out_sp(sp, "rw_out", rw_w_o[0].rearrange("(kt p) n -> p kt n", p=P), DT)

        POOL_DIFFS = ("decay", "rate", "key")

        def diff_pool(pool):
            pool.wait_ge(h_zero, 1)
            for n in range(4 * len(POOL_DIFFS)):
                j = n % 4
                if n < 4:
                    pool.wait_ge(h_ready, n + 1)
                if n >= 2:
                    pool.wait_ge(hn_lo, n - 1)
                nc.gpsimd.tensor_tensor(work[:, j % 2], h_in[:, 4 * j:4 * j + 4, 0:T], h_in[:, 4 * j:4 * j + 4, 1:T + 1],
                                        ALU.subtract).then_inc(mix_diff, 1)

        def mixed_dve(dve, name):
            i, mu = fill_of[name], MU[name]

            def group(j):
                if i == 0:
                    for k in range(4 * j, 4 * j + 4):
                        last = nc.vector.scalar_tensor_tensor(out=h_in[:, k, 1:T + 1], in0=x_res[:, k],
                                                              scalar=param("norm_mix", k), in1=rstd[:], op0=ALU.mult,
                                                              op1=ALU.mult)
                    last.then_inc(h_ready, 1)
                if name not in POOL_DIFFS:
                    nc.vector.tensor_tensor(work[:, j % 2], h_in[:, 4 * j:4 * j + 4, 0:T],
                                            h_in[:, 4 * j:4 * j + 4, 1:T + 1], ALU.subtract).then_inc(mix_diff, 1)
                dve.wait_ge(mix_diff, 4 * i + j + 1)
                for k in range(4):
                    last = nc.vector.scalar_tensor_tensor(out=work[:, j % 2, k], in0=work[:, j % 2, k],
                                                          scalar=param("rw_mu", DT * mu + 4 * j + k),
                                                          in1=h_in[:, 4 * j + k, 1:T + 1], op0=ALU.mult, op1=ALU.add)
                return last

            def after_group(j):
                if j == 1 and name == "rec":
                    prep_dve(dve, 2, 1)
                if j == 2 and name in BLOCKS_BEFORE or j == 2 and name == "gate":
                    split_lo(dve, units[name])

            fill_dve(dve, i, group, after_group)
            if name in BLOCKS_BEFORE or name == "gate":
                split_lo(dve, units[name] + 1)

        def take_block(act, name, i, dst, done):
            act.wait_ge(unit_used, units[name] + 4 + 4 * i)
            nc.scalar.activation(two_banks(dst), block_banks(i), ACT.Copy).then_inc(done, 1)

        def mixed_act(act, name):
            def before_group(j):
                act.wait_ge(unit_used, units[name] - 3 + j)

            def after_group(j):
                if j == 1:
                    split_hi(act, units[name])
                if j == 2 and name == "rec":
                    take_block(act, "key", 3, quad[:, SLOT_K, 12:16, :], block_free)
                if j == 3:
                    split_hi(act, units[name] + 1)

            fill_act(act, fill_of[name], before_group, after_group)

        def lora_pe(pe, name, n, which):
            pe.wait_ge(hn_lo, 4 * fill_of[name] + 4)
            if which:
                pe.wait_ge(sig_done, 2)
            unit_product(pe, n, (DT, LORA), x_tiles(0), lambda f: acc[0:LORA, 0, 0:T], True, True)
            if which:
                pe.wait_ge(sig_done, 4 * which)
            pe.wait_ge(lora_lo_done, which + 1)
            unit_product(pe, n + 1, (1, D), lambda k: (lora_hi[0:LORA, 0, :], lora_lo[0:LORA, 0, :]),
                         lambda f: bank_tile(0, f), True, True, parts=LORA)

        def lora_split_act(act, dst, src, which):
            act.wait_ge(lora_act, which + 1)
            nc.scalar.activation(dst, src, ACT.Copy).then_inc(lora_hi_done, 1)

        def lora_mid_act(act, n, which, func):
            act.wait_ge(unit_used, n + 1)
            src = lora_mid[0:LORA]
            nc.scalar.activation(flat(src), acc[0:LORA, 0, 0:T], func).then_inc(lora_act, 1)
            lora_split_act(act, lora_hi[0:LORA], src, which)

        def sigmoids(act, n, bias_name, slot, j):
            act.wait_ge(unit_used, n + 2)
            for kt in range(4 * j, 4 * j + 4):
                ins = nc.scalar.activation(quad[:, slot, kt, :], bank_tile(0, kt), ACT.Sigmoid, bias=param(bias_name, kt))
            ins.then_inc(sig_done, 1)

        def lora_split_dve(dve, lo, hi, src, which):
            dve.wait_ge(lora_hi_done, which + 1)
            nc.vector.tensor_tensor(lo, src, hi.bitcast(F32), ALU.subtract).then_inc(lora_lo_done, 1)

        def block_pe(pe, name, i, after=None, inside=None):
            pe.wait_ge(block_free, BLOCKS_BEFORE[name] + i)
            for u in range(4):
                pe.wait_ge(hn_lo, 4 * fill_of[name] + u + 1)
                bank = (i % 2) * 2
                unit_product(pe, units[name] + u, (4, 512), x_tiles(4 * u), lambda f: bank_tile(bank, f), u == 0,
                             u == 3, off=4 * i)
                if u == after:
                    inside()

        def block_banks(i):
            return acc[:, bass.ds((i % 2) * 2, 2), :]

        def prep_act(act, i, part):
            tiles = bass.ds(4 * i, 4)
            if part == 0:
                act.wait_ge(kk_raw, 1 + i)
                nc.scalar.activation(prep_x[:, 1], prep_x[:, 0], ACT.Square).then_inc(kk_sq, 1)
            elif part == 1:
                act.wait_ge(kk_step, 3 * i + 1)
                nc.scalar.activation(prep_x[:, 1], prep_x[:, 1], ACT.Ln).then_inc(kk_root, 1)
                act.wait_ge(kk_root, 2 * i + 1)
                nc.scalar.activation(prep_x[:, 1], prep_x[:, 1], ACT.Exp, scale=-0.5).then_inc(kk_root, 1)
                act.wait_ge(prep_done, i)
                nc.scalar.activation(prep_inv[:], quad[:, SLOT_R, tiles, :], ACT.Exp,
                                     scale=DECAY_SCALE).then_inc(decayed, 1)
            else:
                act.wait_ge(cum_gap, 1 + i)
                act.wait_ge(decayed, 3 * i + 1)
                nc.scalar.activation(quad[:, SLOT_A, tiles, :], quad[:, SLOT_A, tiles, :], ACT.Exp,
                                     scale=-DECAY_SCALE).then_inc(decayed, 1)
                nc.scalar.activation(quad[:, SLOT_R, tiles, :], quad[:, SLOT_R, tiles, :], ACT.Exp,
                                     scale=-DECAY_SCALE).then_inc(decayed, 1)

        def prep_pe(pe, i):
            pe.wait_ge(kk_sq, 1 + i)
            pe.wait_ge(kk_root, 2 * i)
            for b in range(2):
                mm = nc.tensor.matmul(acc[:, 4 + b, :], const("head_ones"), flat(prep_x[:, 1, 2 * b:2 * b + 2]))
            mm.then_inc(kk_sum, 1)

        def prep_dve(dve, i, part):
            tiles = bass.ds(4 * i, 4)
            if part == 0:
                dve.wait_ge(kk_sum, 1 + i)
                nc.vector.tensor_scalar(two_banks(prep_x[:, 1]), acc[:, 4:6], 1e-24, None, ALU.max).then_inc(kk_step, 1)
            else:
                dve.wait_ge(kk_root, 2 * i + 2)
                nc.vector.tensor_tensor(prep_x[:, 0], prep_x[:, 0], prep_x[:, 1], ALU.mult).then_inc(kk_step, 1)
                dve.wait_ge(decayed, 3 * i + 2)
                dve.wait_ge(kk_step, 3 * i + 2)
                nc.vector.scalar_tensor_tensor(out=quad[:, SLOT_A, tiles, :], in0=prep_x[:, 0], scalar=-1.0,
                                               in1=quad[:, SLOT_A, tiles, :], op0=ALU.mult,
                                               op1=ALU.mult).then_inc(kk_step, 1)

        def prep_pool(pool):
            pool.wait_ge(sig_done, 8)
            pool.wait_ge(cum_done, 1)
            pool.wait_ge(k_rest_ready, 1)
            for i in range(4):
                tiles = slice(4 * i, 4 * i + 4)
                k_t, b_t, a_t, p_t = (quad[:, s, tiles, :] for s in (SLOT_K, SLOT_B, SLOT_A, SLOT_R))
                pool.wait_ge(block_free, 2 + i)
                for k in range(4):
                    last = nc.gpsimd.tensor_scalar(prep_x[:, 0, k], flat(quad[:, SLOT_K, 4 * i + k:4 * i + k + 1, :]),
                                                   param4("rw_k_k", i, k), None, ALU.mult)
                last.then_inc(kk_raw, 1)
                nc.gpsimd.tensor_tensor(a_t, p_t, a_t, ALU.subtract).then_inc(cum_gap, 1)
                for k in range(4):
                    rest = K_A_REST + 4 * i + k
                    last = nc.gpsimd.tensor_scalar(prep_t[:, k], quad[:, SLOT_B, 4 * i + k, :], param4("rw_k_a", i, k),
                                                   prm[:, rest:rest + 1], ALU.mult, ALU.add)
                last.then_inc(prep_step, 1)
                pool.wait_ge(prep_step, 4 * i + 1)
                nc.gpsimd.tensor_tensor(prep_t[:], prep_t[:], k_t, ALU.mult).then_inc(prep_step, 1)
                pool.wait_ge(kk_step, 3 * i + 3)
                nc.gpsimd.tensor_tensor(prep_x[:, 0], prep_x[:, 0], b_t, ALU.mult).then_inc(prep_step, 1)
                pool.wait_ge(decayed, 3 * i + 3)
                nc.gpsimd.tensor_copy(chunk_decay[:, tiles, :], quad[:, SLOT_R, tiles, CHUNK - 1:T:CHUNK])
                pool.wait_ge(prep_step, 4 * i + 3)
                nc.gpsimd.tensor_tensor(b_t, prep_x[:, 0], prep_inv[:], ALU.mult)
                nc.gpsimd.tensor_tensor(k_t, prep_t[:], prep_inv[:], ALU.mult).then_inc(prep_step, 1)
                pool.wait_ge(prep_step, 4 * i + 4)
                pool.sem_inc(prep_done, 1)

        def rk_pe(pe, i):
            pe.wait_ge(rk_done, 1 + i)
            for b in range(2):
                mm = nc.tensor.matmul(acc[:, 4 + b, :], const("head_ones"), flat(rk_t[:, 2 * b:2 * b + 2]))
            mm.then_inc(rk_sum, 1)

        def tri_pool(pool):
            pool.wait_ge(tables_in, table_loads)
            mask = const("pair_mask").rearrange("p (a h b) -> p a h b", a=1, b=1).to_broadcast([P, NC, 2, 64])
            pool.wait_ge(prep_done, 4)
            pool.dma_start(a_dram, flat(quad[:, SLOT_A])).then_inc(a_stored, 16)
            for p in range(PAIRS):
                if p >= 2:
                    pool.wait_ge(tri_mm, p - 1)
                src = quad[:, SLOT_B, p, :].rearrange("p (c a t) -> p c a t", c=NC, a=1).to_broadcast([P, NC, 2, 64])
                nc.gpsimd.tensor_tensor(b_wide[:, p % 2], src, mask, ALU.mult).then_inc(b_wide_done, 1)

        def tri_act(act):
            for q in range(PAIRS // 4):
                act.wait_ge(tri_masked, 4 * q + 4)
                rows = tri_rows[:, 4 * (q % 2):4 * (q % 2) + 4].rearrange("p a c t -> p (a c) t")
                act.dma_start(stacked(tri_dram, 4 * NC * q, 4 * NC), rows).then_inc(tri_stored[q % 2], 16)

        def tri_pe(pe):
            pe.wait_ge(kk_root, 8)
            for p in range(PAIRS):
                pe.wait_ge(b_wide_done, p + 1)
                if p >= 2:
                    pe.wait_ge(tri_masked, p - 1)
                for c in range(NC):
                    mm = nc.tensor.matmul(acc[:, 4 + p % 2, 64 * c:64 * c + 64], b_wide[:, p % 2, c],
                                          quad[:, SLOT_A, p, 64 * c:64 * c + 64])
                mm.then_inc(tri_mm, 1)

        def tri_dve(dve):
            mask = const("strict_mask").rearrange("p (a t) -> p a t", a=1).to_broadcast([P, NC, 64])
            for p in range(PAIRS):
                dve.wait_ge(tri_mm, p + 1)
                if p >= 8 and p % 4 == 0:
                    dve.wait_ge(tri_stored[p // 4 % 2], 16 * (p // 8))
                nc.vector.tensor_tensor(tri_rows[:, p % 8],
                                        acc[:, 4 + p % 2, 0:NC * 64].rearrange("p (c t) -> p c t", c=NC), mask,
                                        ALU.mult).then_inc(tri_masked, 1)

        def solve_pool(pool):
            for stored in tri_stored:
                pool.wait_ge(stored, 2 * PAIRS)
            pool.dma_start(flat(tri[:]), tri_dram).then_inc(tri_loaded, 16)
            pool.wait_ge(a_stored, 16)
            pool.wait_ge(tri_loaded, 16)
            step = 0
            for u in range(1, 63):
                w = 63 - u
                t = solve_t[:, 0:u * w].rearrange("p (a b) -> p a b", a=u)
                nc.gpsimd.tensor_tensor(t, tri[:, 0:u, u:u + 1].to_broadcast([P, u, w]),
                                        tri[:, u:u + 1, u + 1:64].to_broadcast([P, u, w]), ALU.mult).then_inc(solve_step, 1)
                pool.wait_ge(solve_step, step + 1)
                nc.gpsimd.tensor_tensor(tri[:, 0:u, u + 1:64], tri[:, 0:u, u + 1:64], t, ALU.add).then_inc(solve_step, 1)
                step += 2
                pool.wait_ge(solve_step, step)
            nc.gpsimd.memset(flat(tri[:])[:, 0:4096:65], 1.0).then_inc(solve_step, 1)
            pool.wait_ge(solve_step, step + 1)
            pool.dma_start(inv_dram, flat(tri[:])).then_inc(inv_stored, 16)
            pool.dma_start(flat(quad[:, SLOT_A, 0:4]), a_dram[:, 0:4 * T]).then_inc(inv_loaded, 16)
            pool.wait_ge(inv_stored, 16)
            pool.dma_start(inv_t[:], stacked(inv_dram, 0, GROUPS)).then_inc(inv_loaded, 16)
            pool.wait_ge(inv_loaded, 32)

        def at(g, k):
            if isinstance(g, int):
                return (g + k) % PAIRS, (g + k) // PAIRS * CHUNK
            return (g + (PAIRS + k)) % PAIRS, (g + k) // PAIRS * CHUNK

        def part(ap3, pair, t0, n=CHUNK):
            if isinstance(pair, int):
                return ap3[:, pair, t0:t0 + n]
            return flat(ap3[:, bass.ds(pair, 1), bass.ds(t0, n)])

        def turns(eng, step):
            for g in range(8):
                step(g, 0, g)
            with eng.Fori(1, GROUPS // 8) as it:
                for k in range(8):
                    step(8 * it, k, 8)
            for k in range(3):
                step(GROUPS, k, GROUPS + k)

        def scan_pool(pool):
            pool.wait_ge(v_loaded, 32)
            pool.wait_ge(gate_out, 2)
            four = const("pair_mask").rearrange("p (a h b) -> p a h b", a=1, b=1).to_broadcast([P, 4, 2, 64])
            one = const("pair_mask").rearrange("p (h b) -> p h b", b=1).to_broadcast([P, 2, 64])

            def step(g, k, least):
                if isinstance(g, int) and g + k >= GROUPS:
                    return
                pair, t0 = at(g, k)
                slot = k if not isinstance(g, int) else (g + k) % 8
                if least >= 4:
                    pool.wait_ge(m_mm, g + (k - 3))
                if least >= 8:
                    pool.wait_ge(s_mm, g + (k - 7))
                if isinstance(pair, int):
                    src = quad[:, :, pair, t0:t0 + CHUNK].rearrange("p q (a t) -> p q a t", a=1)
                    v_src, i_src = v_feat[:, pair, t0:t0 + CHUNK], inv_t[:, pair * NC + t0 // CHUNK, :]
                else:
                    src = quad[:, :, bass.ds(pair, 1), bass.ds(t0, CHUNK)]
                    v_src = part(v_feat, pair, t0)
                    i_src = flat(inv_t[:, bass.ds(pair * NC + (g + k) // PAIRS, 1), :])
                nc.gpsimd.tensor_tensor(quad_wide[:, slot], src.to_broadcast([P, 4, 2, 64]), four, ALU.mult)
                nc.gpsimd.tensor_tensor(v_wide[:, slot % 4], v_src.rearrange("p (a t) -> p a t", a=1).to_broadcast([P, 2, 64]),
                                        one, ALU.mult)
                nc.gpsimd.tensor_tensor(inv_wide[:, slot], i_src.rearrange("p (a t) -> p a t", a=1).to_broadcast([P, 2, 64]),
                                        one, ALU.mult).then_inc(wide_done, 1)

            turns(pool, step)

        def scan_parts(g, k, least):
            out = []
            for lag in range(4):
                if isinstance(g, int):
                    here = 0 <= g + k - lag < GROUPS
                    out.append((k - lag, (g + k - lag) % 8, here))
                else:
                    out.append((k - lag, (k - lag) % 8, True))
            return out

        def scan_pe(pe):
            pe.wait_ge(state_zero, 1)
            pe.wait_ge(gate_out, 2)
            ident2 = const("ident2")

            def step(g, k, least):
                (k0, s0, on0), (k1, s1, on1), (k2, s2, on2), (k3, s3, on3) = scan_parts(g, k, least)
                if on0:
                    pair, t0 = at(g, k0)
                    bank = s0 % 2
                    pe.wait_ge(wide_done, g + k0 + 1)
                    if least >= 2:
                        pe.wait_ge(m_done, g + k0 - 1)
                        pe.wait_ge(kbv_done, g + k0 - 1)
                    if isinstance(pair, int):
                        ar = quad[:, SLOT_A:SLOT_R + 1, pair, t0:t0 + CHUNK]
                    else:
                        ar = quad[:, SLOT_A:SLOT_R + 1, bass.ds(pair, 1), bass.ds(t0, CHUNK)].rearrange("p q a t -> p q (a t)")
                    for n in (SLOT_K, SLOT_B):
                        nc.tensor.matmul(acc[:, bank, P * n:P * n + P].rearrange("p (q t) -> p q t", q=2),
                                         quad_wide[:, s0, n], ar, skip_group_check=True)
                    for n in (SLOT_K, SLOT_B):
                        nc.tensor.transpose(acc[:, 2 + bank, P * n:P * n + P], flat(quad_wide[:, s0, n]), ident)
                    nc.tensor.matmul(acc[:, 2 + bank, 2 * P:2 * P + 64], v_wide[:, s0 % 4], ident2,
                                     skip_group_check=True).then_inc(m_mm, 1)
                if on1:
                    pair, t0 = at(g, k1)
                    pe.wait_ge(m_done, g + k1 + 1)
                    pe.wait_ge(kbv_done, g + k1 + 1)
                    if not isinstance(g, int) or g + k1 >= 1:
                        pe.wait_ge(x_done, g + k1)
                    o = acc[:, 4, 0:64]
                    nc.tensor.matmul(o, quad_wide[:, s1, SLOT_A], part_state(pair), start=True, stop=False,
                                     skip_group_check=True)
                    nc.tensor.matmul(o, mix_wide[:, s1 % 4, 0], kbv_rows[:, s1 % 4, 2 * P:2 * P + 64], start=False, stop=True,
                                     skip_group_check=True).then_inc(x_mm, 1)
                if on2:
                    pe.wait_ge(x_done, g + k2 + 1)
                    if not isinstance(g, int) or g + k2 >= 1:
                        pe.wait_ge(u_done, g + k2)
                    nc.tensor.matmul(acc[:, 5, 0:64], inv_wide[:, s2], x_stack[:, s2 % 2],
                                     skip_group_check=True).then_inc(u_mm, 1)
                if on3:
                    pair, t0 = at(g, k3)
                    pe.wait_ge(u_done, g + k3 + 1)
                    if not isinstance(g, int) or g + k3 >= 1:
                        pe.wait_ge(y_taken, g + k3)
                    o = acc[:, 6, 0:64]
                    nc.tensor.matmul(o, quad_wide[:, s3, SLOT_R], part_state(pair), start=True, stop=False,
                                     skip_group_check=True)
                    nc.tensor.matmul(o, mix_wide[:, s3 % 4, 1], kbv_rows[:, s3 % 4, 2 * P:2 * P + 64], start=False, stop=False,
                                     skip_group_check=True)
                    nc.tensor.matmul(o, mix_wide[:, s3 % 4, 2], u_stack[:, s3 % 2], start=False, stop=True,
                                     skip_group_check=True).then_inc(y_mm, 1)
                    if not isinstance(g, int) or g + k3 >= 1:
                        pe.wait_ge(s_done, g + k3)
                    o = acc[:, 7, 0:64]
                    nc.tensor.matmul(o, kbv_rows[:, s3 % 4, 0:P], kbv_rows[:, s3 % 4, 2 * P:2 * P + 64], start=True, stop=False,
                                     skip_group_check=True)
                    nc.tensor.matmul(o, kbv_rows[:, s3 % 4, P:2 * P], u_stack[:, s3 % 2], start=False, stop=True,
                                     skip_group_check=True).then_inc(s_mm, 1)

            turns(pe, step)

        def part_state(pair):
            return state[:, pair, :] if isinstance(pair, int) else flat(state[:, bass.ds(pair, 1), :])

        def scan_act(act):
            def step(g, k, least):
                (k0, s0, on0), (k1, s1, on1), (k2, s2, on2), (k3, s3, on3) = scan_parts(g, k, least)
                if on0:
                    act.wait_ge(m_mm, g + k0 + 1)
                    if least >= 4:
                        act.wait_ge(s_mm, g + k0 - 3)
                    nc.scalar.activation(kbv_rows[:, s0 % 4], acc[:, 2 + s0 % 2, 0:2 * P + 64], ACT.Copy).then_inc(kbv_done, 1)
                if on2:
                    pair, t0 = at(g, k2)
                    act.wait_ge(u_mm, g + k2 + 1)
                    nc.scalar.activation(u_stack[:, s2 % 2], acc[:, 5, 0:64], ACT.Copy).then_inc(u_done, 1)
                    if isinstance(pair, int):
                        dec = chunk_decay[:, pair, t0 // CHUNK:t0 // CHUNK + 1]
                    else:
                        dec = flat(chunk_decay[:, bass.ds(pair, 1), bass.ds((g + k2) // PAIRS, 1)])
                    nc.scalar.activation(state_dec[:, s2 % 4], part_state(pair), ACT.Copy, scale=dec).then_inc(dec_done, 1)
                if on3:
                    pair, t0 = at(g, k3)
                    act.wait_ge(y_mm, g + k3 + 1)
                    if isinstance(pair, int):
                        o = y_all[:, pair, t0 // CHUNK, :]
                    else:
                        o = y_all[:, bass.ds(pair, 1), bass.ds((g + k3) // PAIRS, 1), :].rearrange("p a b t -> p (a b t)")
                    nc.scalar.activation(o, acc[:, 6, 0:64], ACT.Copy).then_inc(y_taken, 1)

            act.wait_ge(state_zero, 1)
            turns(act, step)

        def scan_dve(dve):
            masks = const("chunk_mask").rearrange("p (q h t) -> p q h t", q=2, h=2)

            def step(g, k, least):
                (k0, s0, on0), (k1, s1, on1), (k2, s2, on2), (k3, s3, on3) = scan_parts(g, k, least)
                if on0:
                    dve.wait_ge(m_mm, g + k0 + 1)
                    if least >= 4:
                        dve.wait_ge(s_mm, g + k0 - 3)
                    m1 = acc[:, s0 % 2, 0:P].rearrange("p (q a t) -> p q a t", q=2, a=1).to_broadcast([P, 2, 2, 64])
                    nc.vector.tensor_tensor(mix_wide[:, s0 % 4, 0:2], m1, masks, ALU.mult)
                    m2 = acc[:, s0 % 2, P + 64:T].rearrange("p (a t) -> p a t", a=1).to_broadcast([P, 2, 64])
                    nc.vector.tensor_tensor(mix_wide[:, s0 % 4, 2], m2, masks[:, 1], ALU.mult).then_inc(m_done, 1)
                if on1:
                    dve.wait_ge(x_mm, g + k1 + 1)
                    nc.vector.tensor_copy(x_stack[:, s1 % 2], acc[:, 4, 0:64]).then_inc(x_done, 1)
                if on3:
                    pair, t0 = at(g, k3)
                    dve.wait_ge(s_mm, g + k3 + 1)
                    dve.wait_ge(dec_done, g + k3 + 1)
                    if isinstance(pair, int):
                        dec = chunk_decay[:, pair, t0 // CHUNK:t0 // CHUNK + 1]
                    else:
                        dec = flat(chunk_decay[:, bass.ds(pair, 1), bass.ds((g + k3) // PAIRS, 1)])
                    nc.vector.scalar_tensor_tensor(out=part_state(pair), in0=acc[:, 7, 0:64], scalar=dec,
                                                   in1=state_dec[:, s3 % 4], op0=ALU.mult, op1=ALU.add).then_inc(s_done, 1)

            turns(dve, step)

        def y_groups(j):
            return y_all[:, 4 * j:4 * j + 4].rearrange("p a c v -> p (a c) v"), slice(16 * j, 16 * j + 16)

        def y_out(engine, p):
            src = y_all[:, p].rearrange("p c (a v) -> p c a v", a=1).to_broadcast([P, NC, 2, 64])
            factor = y_scale[:, NC * p:NC * p + NC].rearrange("p c (h a) -> p c h a", a=1)
            return engine.tensor_tensor(y_wide[:, p % 4], src, factor.to_broadcast([P, NC, 2, 64]), ALU.mult)

        def finish_dve(dve):
            dve.wait_ge(y_taken, GROUPS)
            pm = const("pair_mask")
            step = 0

            def then(ins):
                nonlocal step
                step += 1
                ins.then_inc(ln_step, 1)
                dve.wait_ge(ln_step, step)

            def centre(j):
                y, st = y_groups(j)
                then(nc.vector.tensor_reduce(y_mean[:, st], y, AX_X, ALU.add))
                then(nc.vector.tensor_scalar(y_mean[:, st], y_mean[:, st], 1.0 / RW_HEAD, None, ALU.mult))
                mean = y_mean[:, st].rearrange("p (g a) -> p g a", a=1).to_broadcast([P, 16, 64])
                nc.vector.tensor_tensor(y, y, mean, ALU.subtract).then_inc(ln_centred, 1)

            def variance(j):
                st = y_groups(j)[1]
                dve.wait_ge(ln_sq, j + 1)
                sq = work[:, j % 2].rearrange("p a t -> p (a t)").rearrange("p (g v) -> p g v", v=64)
                then(nc.vector.tensor_reduce(y_inv[:, st], sq, AX_X, ALU.add))
                then(nc.vector.tensor_scalar(y_inv[:, st], y_inv[:, st], 1.0 / RW_HEAD, RW_GN_EPS, ALU.mult, ALU.add))
                nc.vector.reciprocal(y_inv[:, st], y_inv[:, st]).then_inc(ln_var, 1)

            def scale(j):
                st = y_groups(j)[1]
                dve.wait_ge(ln_root, j + 1)
                inv = y_inv[:, st].rearrange("p (g a) -> p g a", a=1).to_broadcast([P, 16, 2])
                nc.vector.tensor_tensor(y_scale[:, st], inv, pm.rearrange("p (a h) -> p a h", a=1).to_broadcast([P, 16, 2]),
                                        ALU.mult).then_inc(ln_scale, 1)

            def wide(j):
                for p in range(4 * j, 4 * j + 2):
                    if p >= 4:
                        dve.wait_ge(yt_mm, p - 3)
                    dve.wait_ge(ln_scale, j + 1)
                    y_out(nc.vector, p).then_inc(y_wide_first, 1)

            def gain(j):
                dve.wait_ge(yt_mm, 4 * j + 4)
                for q in range(4):
                    p = 4 * j + q
                    last = nc.vector.tensor_scalar(att[:, p], bank_tile(2 * (j % 2), q), param("rw_ln_w", p),
                                                   param("rw_ln_b", p), ALU.mult, ALU.add)
                last.then_inc(att_gain, 1)

            def low(j):
                dve.wait_ge(att_hi_done, j + 1)
                nc.vector.tensor_tensor(att_lo[:, 4 * j:4 * j + 4], att[:, 4 * j:4 * j + 4],
                                        att_hi[:, 4 * j:4 * j + 4].bitcast(F32), ALU.subtract).then_inc(att_lo_done, 1)

            steps = (centre, variance, scale, wide, gain, low)
            for turn in range(4 + len(steps)):
                for lag, do in zip((0, 1, 2, 2, 3, 4), steps):
                    if 0 <= turn - lag < 4:
                        do(turn - lag)

        def finish_pool(pool):
            def wide(j):
                pool.wait_ge(ln_scale, j + 1)
                for p in range(4 * j + 2, 4 * j + 4):
                    if p >= 4:
                        pool.wait_ge(yt_mm, p - 3)
                    y_out(nc.gpsimd, p).then_inc(y_wide_done, 1)

            def gate(j):
                pool.wait_ge(att_gain, j + 1)
                t = slice(4 * j, 4 * j + 4)
                nc.gpsimd.tensor_tensor(att[:, t], att[:, t], bonus[:, t], ALU.add).then_inc(att_bonus, 1)
                pool.wait_ge(att_bonus, j + 1)
                nc.gpsimd.tensor_tensor(att[:, t], att[:, t], out_gate[:, t], ALU.mult).then_inc(att_ready, 1)

            pool.wait_ge(s_mm, GROUPS)
            pool.wait_ge(bonus_loaded, 16)
            for j in range(4):
                wide(j)
                if j >= 1:
                    gate(j - 1)
            gate(3)

        def finish_act(act):
            def root(j):
                act.wait_ge(ln_var, j + 1)
                nc.scalar.activation(y_inv[:, 16 * j:16 * j + 16], y_inv[:, 16 * j:16 * j + 16],
                                     ACT.Sqrt).then_inc(ln_root, 1)

            for j in range(4):
                act.wait_ge(ln_centred, j + 1)
                if j >= 2:
                    act.wait_ge(ln_var, j - 1)
                nc.scalar.activation(flat(work[:, j % 2]), y_all[:, 4 * j:4 * j + 4].rearrange("p a c v -> p (a c v)"),
                                     ACT.Square).then_inc(ln_sq, 1)
                if j >= 1:
                    root(j - 1)
            root(3)
            for j in range(4):
                act.wait_ge(att_ready, j + 1)
                nc.scalar.activation(att_hi[:, 4 * j:4 * j + 4], att[:, 4 * j:4 * j + 4], ACT.Copy).then_inc(att_hi_done, 1)

        def finish_pe(pe):
            for p in range(PAIRS):
                if p % 4 < 2:
                    pe.wait_ge(y_wide_first, 2 * (p // 4) + p % 4 + 1)
                else:
                    pe.wait_ge(y_wide_done, 2 * (p // 4) + p % 4 - 1)
                if p >= 8 and p % 4 == 0:
                    pe.wait_ge(att_gain, p // 4 - 1)
                for c in range(NC):
                    o = bank_tile(2 * (p // 4 % 2), p % 4)
                    mm = nc.tensor.matmul(o[:, 64 * c:64 * c + 64], y_wide[:, p % 4, c], const("ident2"),
                                          skip_group_check=True)
                mm.then_inc(yt_mm, 1)

        def rwkv_pool(pool):
            diff_pool(pool)
            prep_pool(pool)
            tri_pool(pool)
            solve_pool(pool)
            scan_pool(pool)
            finish_pool(pool)

        def rwkv_pe(pe):
            norm_pe(pe, norm_of["rwkv"])
            lora_pe(pe, "decay", n_dec, 0)
            lora_pe(pe, "rate", n_rate, 1)
            pe.wait_ge(sig_done, 5)
            block_pe(pe, "key", 0)
            pe.wait_ge(sig_done, 8)
            with pe.Fori(1, 4) as i:
                block_pe(pe, "key", i, 1, lambda: prep_pe(pe, i - 1))
            block_pe(pe, "rec", 0, 0, lambda: prep_pe(pe, 3))
            tri_pe(pe)
            with pe.Fori(1, 4) as i:
                block_pe(pe, "rec", i)
            pe.wait_ge(tri_masked, PAIRS)
            block_pe(pe, "val", 0)
            with pe.Fori(1, 4) as i:
                block_pe(pe, "val", i, 1, lambda: rk_pe(pe, i - 1))
            for u in range(2):
                pe.wait_ge(hn_lo, 4 * fill_of["gate"] + 2 * u + 2)
                if u == 0:
                    pe.wait_ge(block_free, 12)
                unit_product(pe, n_gate + u, (8, GLORA), x_tiles(8 * u), lambda f: bank_tile(0, f), u == 0, u == 1)
            rk_pe(pe, 3)
            pe.wait_ge(block_free, 13)
            pe.wait_ge(bonus_done, 4)
            pe.wait_ge(lora_lo_done, 3)
            for u in range(2):
                unit_product(pe, n_gate + 2 + u, (1, D), lambda k: (glora_hi[:, u, :], glora_lo[:, u, :]),
                             lambda f: bank_tile(0, f), u == 0, u == 1)
            pe.wait_ge(gate_out, 2)
            pe.wait_ge(inv_stored, 16)
            for _ in range(14):
                nc.tensor.matmul(acc[:, 7, :], ident, tab[:, 0:512])
            scan_pe(pe)
            finish_pe(pe)

            def before_block(b):
                if b == 0:
                    pe.wait_ge(att_lo_done, 3)
                else:
                    pe.wait_ge(att_lo_done, 4)

            out_pe(pe, "rw_out", att_hi, att_lo, DT, before_block, lambda: pe.wait_ge(att_lo_done, 4))

        def rwkv_act(act):
            act.sem_inc(block_free, 1)
            def early(u):
                if u == 0:
                    split_hi(act, n_dec, width=DT * LORA)
                else:
                    split_hi(act, n_dec + 1, parts=LORA)

            norm_act(act, norm_of["rwkv"], early)
            fill_act(act, fill_of["decay"])
            lora_mid_act(act, n_dec, 0, ACT.Tanh)

            def before_rate(j):
                act.wait_ge(unit_used, n_dec + 1)
                if j >= 2:
                    sigmoids(act, n_dec, "rw_w0", SLOT_A, 2 * j - 4)
                    sigmoids(act, n_dec, "rw_w0", SLOT_A, 2 * j - 3)

            fill_act(act, fill_of["rate"], before_rate)
            split_hi(act, n_rate, width=DT * LORA)
            split_hi(act, n_rate + 1, parts=LORA)
            lora_mid_act(act, n_rate, 1, ACT.Copy)

            def after_key(j):
                if j == 1:
                    split_hi(act, units["key"])

            fill_act(act, fill_of["key"], lambda j: act.wait_ge(unit_used, n_rate + 1), after_key)
            sigmoids(act, n_rate, "rw_a0", SLOT_B, 0)
            split_hi(act, units["key"] + 1)
            for j in range(1, 4):
                sigmoids(act, n_rate, "rw_a0", SLOT_B, j)

            def block(name, i, prep=None, take=False):
                n0 = units[name]
                if not isinstance(i, int):
                    split_hi(act, n0, 4 * i)
                    split_hi(act, n0 + 1, 4 * i)
                if take:
                    take_block(act, "key", i - 1, quad[:, SLOT_K, bass.ds(4 * i - 4, 4), :], block_free)
                split_hi(act, n0 + 2, 4 * i)
                if prep is not None:
                    prep_act(act, prep, 0)
                split_hi(act, n0 + 3, 4 * i)
                if prep is not None:
                    prep_act(act, prep, 1)
                    prep_act(act, prep, 2)

            block("key", 0)
            with act.Fori(1, 4) as i:
                block("key", i, i - 1, True)
            mixed_act(act, "rec")
            block("rec", 0, 3)
            tri_act(act)
            with act.Fori(1, 4) as i:
                block("rec", i)
            mixed_act(act, "val")

            def take_values(i):
                act.wait_ge(unit_used, units["val"] + 4 + 4 * i)
                act.wait_ge(val_stored, 16 * i)
                act.wait_ge(bonus_done, i)
                nc.scalar.activation(two_banks(val_t[:]), block_banks(i), ACT.Copy).then_inc(val_out, 1)
                act.wait_ge(val_out, 1 + i)
                act.sem_inc(block_free, 1)
                act.dma_start(v_dram[:, bass.ds(4 * i, 4), :], val_t[:]).then_inc(val_stored, 16)

            def store_bonus(i):
                act.wait_ge(bonus_done, 1 + i)
                act.dma_start(bonus_dram[:, bass.ds(4 * i, 4), :], rk_t[:]).then_inc(bonus_stored, 16)

            def val_block(i, behind):
                n0 = units["val"]
                if behind:
                    split_hi(act, n0, 4 * i)
                    split_hi(act, n0 + 1, 4 * i)
                    take_values(i - 1)
                split_hi(act, n0 + 2, 4 * i)
                split_hi(act, n0 + 3, 4 * i)
                if behind:
                    store_bonus(i - 1)

            val_block(0, False)
            act.wait_ge(a_stored, 16)
            with act.Fori(1, 4) as i:
                val_block(i, True)
            mixed_act(act, "gate")
            take_values(3)
            act.wait_ge(unit_used, n_gate + 2)
            nc.scalar.activation(flat(work[:, 1, 0:2]), acc[:, 0, :], ACT.Sigmoid).then_inc(lora_act, 1)
            lora_split_act(act, glora_hi[:], work[:, 1, 0:2], 2)
            split_hi(act, n_gate + 2)
            split_hi(act, n_gate + 3)
            store_bonus(3)
            act.wait_ge(val_stored, 64)
            act.dma_start(v_feat[:], v_dram).then_inc(v_loaded, 16)
            act.wait_ge(bonus_stored, 64)
            act.dma_start(flat(quad[:, SLOT_A, 4:DT]), a_dram[:, 4 * T:]).then_inc(v_loaded, 16)
            act.wait_ge(unit_used, n_gate + 4)
            nc.scalar.activation(out_gate[:, 0:8].rearrange("p a t -> p (a t)").rearrange("p (b s) -> p b s", b=4),
                                 acc[:, 0:4], ACT.Copy).then_inc(gate_out, 1)
            scan_act(act)
            act.wait_ge(s_mm, GROUPS)
            act.dma_start(bonus[:], bonus_dram).then_inc(bonus_loaded, 16)
            split_hi(act, units["rw_out"])
            split_hi(act, units["rw_out"] + 1)
            finish_act(act)
            out_act(act, "rw_out", DT, early=True)

        def rwkv_dve(dve):
            q = norm_of["rwkv"]
            dve.wait_ge(x_turned, 4)
            nc.vector.memset(h_in[:, :, 0:1], 0.0).then_inc(h_zero, 1)
            def early(u):
                if u == 0:
                    split_lo(dve, n_dec, width=DT * LORA)
                else:
                    split_lo(dve, n_dec + 1, parts=LORA)

            norm_dve(dve, q, early)
            dve.wait_ge(h_zero, 1)
            mixed_dve(dve, "decay")
            lora_split_dve(dve, lora_lo[0:LORA], lora_hi[0:LORA], lora_mid[0:LORA], 0)
            mixed_dve(dve, "rate")
            split_lo(dve, n_rate, width=DT * LORA)
            split_lo(dve, n_rate + 1, parts=LORA)
            lora_split_dve(dve, lora_lo[0:LORA], lora_hi[0:LORA], lora_mid[0:LORA], 1)
            mixed_dve(dve, "key")
            dve.wait_ge(sig_done, 4)
            for kt in range(DT):
                last = nc.vector.tensor_tensor_scan(quad[:, SLOT_R, kt], const("scan_mask"), quad[:, SLOT_A, kt], 0.0,
                                                    ALU.mult, ALU.add)
            last.then_inc(cum_done, 1)

            def block(name, i, prep=None, take=False):
                n0 = units[name]
                if not (isinstance(i, int) and i == 0):
                    split_lo(dve, n0, 4 * i)
                    split_lo(dve, n0 + 1, 4 * i)
                if take:
                    receptance(i - 1)
                split_lo(dve, n0 + 2, 4 * i)
                if prep is not None:
                    prep_dve(dve, prep, 0)
                split_lo(dve, n0 + 3, 4 * i)

            def receptance(i):
                dve.wait_ge(unit_used, units["rec"] + 4 + 4 * i)
                r = quad[:, SLOT_R, bass.ds(4 * i, 4), :]
                nc.vector.tensor_tensor(two_banks(r), block_banks(i), two_banks(r), ALU.mult).then_inc(block_free, 1)

            block("key", 0)
            with dve.Fori(1, 3) as i:
                block("key", i, i - 1)
                prep_dve(dve, i - 1, 1)
            block("key", 3, 2)
            mixed_dve(dve, "rec")
            block("rec", 0, 3)
            prep_dve(dve, 3, 1)
            dve.wait_ge(prep_done, 4)
            tri_dve(dve)
            with dve.Fori(1, 4) as i:
                block("rec", i, None, True)
            mixed_dve(dve, "val")
            receptance(3)

            def rk(i):
                dve.wait_ge(block_free, 8)
                dve.wait_ge(bonus_stored, 16 * i)
                for k in range(4):
                    t = bass.ds(4 * i + k, 1)
                    last = nc.vector.scalar_tensor_tensor(out=rk_t[:, k], in0=flat(quad[:, SLOT_R, t, :]),
                                                          scalar=param4("rw_r_k", i, k), in1=flat(quad[:, SLOT_K, t, :]),
                                                          op0=ALU.mult, op1=ALU.mult)
                last.then_inc(rk_done, 1)

            def make_bonus(i):
                dve.wait_ge(rk_sum, 1 + i)
                dve.wait_ge(val_out, 1 + i)
                nc.vector.tensor_tensor(two_banks(rk_t[:]), acc[:, 4:6], two_banks(val_t[:]),
                                        ALU.mult).then_inc(bonus_done, 1)

            def val_block(i, behind):
                n0 = units["val"]
                if behind:
                    split_lo(dve, n0, 4 * i)
                    split_lo(dve, n0 + 1, 4 * i)
                    rk(i - 1)
                split_lo(dve, n0 + 2, 4 * i)
                split_lo(dve, n0 + 3, 4 * i)
                if behind:
                    make_bonus(i - 1)

            val_block(0, False)
            dve.wait_ge(a_stored, 16)
            with dve.Fori(1, 4) as i:
                val_block(i, True)
            mixed_dve(dve, "gate")
            rk(3)
            lora_split_dve(dve, glora_lo[:], glora_hi[:], work[:, 1, 0:2], 2)
            split_lo(dve, n_gate + 2)
            split_lo(dve, n_gate + 3)
            make_bonus(3)
            dve.wait_ge(unit_used, n_gate + 4)
            nc.vector.tensor_copy(out_gate[:, 8:16].rearrange("p a t -> p (a t)").rearrange("p (b s) -> p b s", b=4),
                                  acc[:, 4:8]).then_inc(gate_out, 1)
            nc.vector.memset(state[:], 0.0).then_inc(state_zero, 1)
            scan_dve(dve)
            dve.wait_ge(s_done, GROUPS)
            split_lo(dve, units["rw_out"])
            split_lo(dve, units["rw_out"] + 1)
            finish_dve(dve)
            out_dve(dve, "rw_out", DT, early=True)

        norms = ["rwkv", "up0", "ret", "up1", "final"]
        norm_of = {name: q for q, name in enumerate(norms)}
        fills = ["decay", "rate", "key", "rec", "val", "gate", "up0", "ret", "up1"]
        fill_of = {name: i for i, name in enumerate(fills)}

        def normed_act(act, name):
            norm_act(act, norm_of[name], lambda u: split_hi(act, units[name] + u))
            fill_act(act, fill_of[name])

        def normed_dve(dve, name, gain, gain_tile):
            norm_dve(dve, norm_of[name], lambda u: split_lo(dve, units[name] + u))
            fill_dve(dve, fill_of[name], lambda j: norm_group(j, gain, gain_tile))

        param_pieces = []
        for name, src in (("norm_mix", norm_mix), ("norm_ffn", norm_ffn), ("norm_final", norm_final),
                          ("rw_mu", rw_mu), ("rw_w0", rw_w0), ("rw_a0", rw_a0), ("rw_k_k", rw_k_k),
                          ("rw_k_a", rw_k_a), ("rw_r_k", rw_r_k), ("rw_ln_w", rw_ln_w), ("rw_ln_b", rw_ln_b),
                          ("ret_gn_w", ret_gn_w)):
            r, n = PARAM_ROWS[name]
            merge = {1: None, 2: "a b -> (a b)", 3: "a b c -> (a b c)"}[len(src.shape)]
            rows = (src.rearrange(merge) if merge else src).rearrange("(r c) -> r c", c=P)
            done = 0
            while done < n:
                first, blk = (r + done) % P, (r + done) // P
                k = min(n - done, P - first)
                param_pieces.append((param_rows[first:first + k, blk, :], rows[done:done + k, :]))
                done += k
        table_loads = 16 * (1 + len(param_pieces))
        rows_of_block = [min(P, PARAM_ROWS["ret_gn_w"][0] + 2 * DT - P * b) for b in range(PARAM_BLOCKS)]

        block = ctx.enter_context(nc.Block())

        @block.sync
        def _(sp):
            sp.dma_start(x_rows[:], x_dram).then_inc(rows_in, 16)
            sp.dma_start(tab[:], table[:, 0:tab_cols]).then_inc(tables_in, 16)
            for dst, src in param_pieces:
                sp.dma_start(dst, src).then_inc(tables_in, 16)
            rwkv_sp(sp)
            for l in range(2):
                up_sp(sp, l)
                out_sp(sp, f"down{l}", w2s[l], FT)
                if l == 0:
                    ret_sp(sp)
                    out_sp(sp, "ret_out", ret_out, 2 * DT)
            for j in range(4):
                sp.wait_ge(out_ready, j + 1)
                sp.dma_start(out_dram[:, :, 512 * j:512 * j + 512],
                             out_rows[:, :, 512 * j:512 * j + 512]).then_inc(out_stored, 16)
            sp.wait_ge(out_stored, 64)

        @block.gpsimd
        def _(pool):
            rwkv_pool(pool)

        @block.scalar
        def _(act):
            rwkv_act(act)
            for l in range(2):
                normed_act(act, f"up{l}")
                up_act(act, l)
                out_act(act, f"down{l}", FT)
                if l == 0:
                    normed_act(act, "ret")
                    rope_act(act)
                    ret_act(act)
                    out_act(act, "ret_out", 2 * DT)
            norm_act(act, norm_of["final"])
            for j in range(4):
                act.wait_ge(out_turned, j + 1)
                nc.scalar.activation(out_rows[:, :, 512 * j:512 * j + 512], acc[:, 2 * (j % 2):2 * (j % 2) + 2],
                                     ACT.Copy).then_inc(out_ready, 1)

        @block.vector
        def _(dve):
            dve.sem_inc(up_free, 1)
            for b in range(PARAM_BLOCKS):
                dve.wait_ge(params_t, PARAM_BLOCKS)
                k = rows_of_block[b]
                nc.vector.tensor_copy(prm[:, P * b:P * b + k], acc[:, 6, P * b:P * b + k]).then_inc(params_ready, 1)
            for j in range(4):
                dve.wait_ge(x_turned, j + 1)
                nc.vector.tensor_copy(two_banks(x_res[:, 4 * j:4 * j + 4]),
                                      acc[:, 2 * (j % 2):2 * (j % 2) + 2]).then_inc(x_ready, 1)
            dve.wait_ge(params_ready, PARAM_BLOCKS)
            k_a, _ = PARAM_ROWS["rw_k_a"]
            nc.vector.tensor_scalar(prm[:, K_A_REST:K_A_REST + DT], prm[:, k_a:k_a + DT], -1.0, 1.0, ALU.mult,
                                    ALU.add).then_inc(k_rest_ready, 1)
            rwkv_dve(dve)
            for l in range(2):
                normed_dve(dve, f"up{l}", "norm_ffn", DT * l)
                up_dve(dve, l)
                out_dve(dve, f"down{l}", FT)
                if l == 0:
                    normed_dve(dve, "ret", "norm_mix", DT)
                    rope_dve(dve)
                    ret_dve(dve)
                    out_dve(dve, "ret_out", 2 * DT)
            norm_dve(dve, norm_of["final"])
            for j in range(4):
                if j >= 2:
                    dve.wait_ge(out_turned, j - 1)
                norm_group(j, "norm_final", 0).then_inc(hn_ready, 1)

        @block.tensor
        def _(pe):
            pe.wait_ge(tables_in, table_loads)
            for b in range(PARAM_BLOCKS):
                k = rows_of_block[b]
                mm = nc.tensor.transpose(acc[:, 6, P * b:P * b + k], param_rows[0:k, b, :], ident[0:k, 0:k])
                mm.then_inc(params_t, 1)
            pe.wait_ge(rows_in, 16)
            for j in range(4):
                if j >= 2:
                    pe.wait_ge(x_ready, j - 1)
                for k in range(4):
                    for tt in range(2):
                        mm = nc.tensor.transpose(bank_tile(2 * (j % 2), k)[:, P * tt:P * tt + P],
                                                 x_rows[:, tt, P * (4 * j + k):P * (4 * j + k) + P], ident)
                mm.then_inc(x_turned, 1)
            rwkv_pe(pe)
            for l in range(2):
                norm_pe(pe, norm_of[f"up{l}"])
                up_pe(pe, l, fill_of[f"up{l}"])
                down_pe(pe, l)
                if l == 0:
                    norm_pe(pe, norm_of["ret"])
                    ret_pe(pe, fill_of["ret"])

                    def before_block(b):
                        if b == 0:
                            pe.wait_ge(y_var, RET_HEADS)
                            pe.wait_ge(silu_g_done, RET_HEADS)
                            pe.wait_ge(ret_lo_done, RET_HEADS - 1)
                        else:
                            pe.wait_ge(v_evac, RET_HEADS)

                    out_pe(pe, "ret_out", ret_hi, ret_lo, 2 * DT, before_block,
                           lambda: pe.wait_ge(ret_lo_done, RET_HEADS))
            norm_pe(pe, norm_of["final"])
            for j in range(4):
                pe.wait_ge(hn_ready, 4 * len(fills) + j + 1)
                if j >= 2:
                    pe.wait_ge(out_ready, j - 1)
                for tt in range(2):
                    for k in range(4):
                        mm = nc.tensor.transpose(acc[:, 2 * (j % 2) + tt, P * k:P * k + P],
                                                 work[:, j % 2, k, P * tt:P * tt + P], ident)
                mm.then_inc(out_turned, 1)


_INS = ['x', 'positions', 'norm_mix', 'norm_ffn', 'norm_final', 'rw_mu', 'rw_w_rkv', 'rw_w0', 'rw_w1', 'rw_w2',
        'rw_a0', 'rw_a1', 'rw_a2', 'rw_g1', 'rw_g2', 'rw_k_k', 'rw_k_a', 'rw_r_k', 'rw_ln_w', 'rw_ln_b', 'rw_w_o',
        'ret_w_in', 'ret_gn_w', 'ret_w_out', 'ffn_w1', 'ffn_w3', 'ffn_w2']


def kernel(**inputs):
    import concourse.bacc as _bacc
    from concourse.bass_utils import run_bass_kernel_spmd as _run

    nc = _bacc.Bacc("TRN2", target_bir_lowering=False, num_devices=1)
    arrays, args = {}, []
    for name in _INS:
        a = np.ascontiguousarray(inputs[name])
        arrays[f"in_{name}"] = a
        args.append(nc.dram_tensor(f"in_{name}", a.shape, mybir.dt.from_np(a.dtype), kind="ExternalInput").ap())
    arrays["shape_table"] = shape_table()
    args.append(nc.dram_tensor("shape_table", (P, TABLE_WIDTH), F32, kind="ExternalInput").ap())
    args.append(nc.dram_tensor("out_0", (1, T, D), F32, kind="ExternalOutput").ap())
    trunk_program(nc, *args)
    r = _run(nc, [arrays], core_ids=[0])
    return r.results[0]["out_0"]
```

```python
from contextlib import ExitStack

import numpy as np

import concourse.bass as bass
from concourse import mybir

ALU = mybir.AluOpType
ACT = mybir.ActivationFunctionType
AX_X = mybir.AxisListType.X
F32 = mybir.dt.float32
F32R = mybir.dt.float32r
I32 = mybir.dt.int32

P = 128
T = 256
D = 2048
DT = D // P
F = 5632
FT = F // P
CHUNK = 64
NC = T // CHUNK
LORA = 96
GLORA = 256
RET_HEADS = 8
RET_DK = D // RET_HEADS
RET_DV = 2 * D // RET_HEADS
ROPE_BASE = 10000.0
NORM_EPS = 1e-6
RW_GN_EPS = 64e-5
RW_HEAD = 64
PAIRS = D // P
UNIT = 2048
UP_BLOCKS = F // 512

PARAM_ROWS = {}
_row = 0
for _name, _n in (("norm_mix", 2 * DT), ("norm_ffn", 2 * DT), ("norm_final", DT), ("rw_mu", 6 * DT), ("rw_w0", DT),
                  ("rw_a0", DT), ("rw_k_k", DT), ("rw_k_a", DT), ("rw_r_k", DT), ("rw_ln_w", DT), ("rw_ln_b", DT),
                  ("ret_gn_w", 2 * DT)):
    PARAM_ROWS[_name] = (_row, _n)
    _row += _n
PARAM_BLOCKS = -(-_row // P)
K_A_REST = _row
assert K_A_REST + DT <= PARAM_BLOCKS * P

TABLE_COLS = {}
_col = 0
for _name, _n in (("ident", P), ("ones", P), ("head_ones", P), ("ident2", 64), ("pair_mask", 2), ("strict_mask", 64),
                  ("chunk_mask", 2 * 2 * 64), ("scan_mask", T), ("inv_freq", 1), ("ret_decay", RET_HEADS * T)):
    TABLE_COLS[_name] = (_col, _n)
    _col += _n
TABLE_WIDTH = _col


def shape_table():
    t = np.zeros((P, TABLE_WIDTH), np.float32)

    def put(name, value):
        c, n = TABLE_COLS[name]
        t[:, c:c + n] = np.asarray(value, np.float32).reshape(P, n)

    p = np.arange(P)
    half, s = p // 64, p % 64
    tt = np.arange(64)
    put("ident", np.eye(P))
    put("ones", np.ones((P, P)))
    put("head_ones", half[:, None] == half[None, :])
    put("ident2", s[:, None] == tt[None, :])
    pair = half[:, None] == np.arange(2)[None, :]
    put("pair_mask", pair)
    causal = np.stack([s[:, None] < tt[None, :], s[:, None] <= tt[None, :]], 1)
    put("strict_mask", causal[:, 0])
    put("chunk_mask", causal[:, :, None, :] * pair[:, None, :, None])
    put("scan_mask", np.broadcast_to((np.arange(T) % CHUNK != 0)[None, :], (P, T)))
    put("inv_freq", 1.0 / ROPE_BASE ** (np.arange(P) / (RET_DK // 2 - 1)))
    gamma = 1.0 - 2.0 ** (-5.0 - np.arange(RET_HEADS))
    dist = np.arange(T)[None, :] - p[:, None]
    decay = np.where(dist[:, None, :] >= 0, gamma[None, :, None] ** np.maximum(dist, 0)[:, None, :], 0.0)
    put("ret_decay", decay * RET_DK ** -0.5)
    return t


def trunk_program(nc, x, positions, norm_mix, norm_ffn, norm_final, rw_mu, rw_w_rkv, rw_w0, rw_w1, rw_w2,
                  rw_a0, rw_a1, rw_a2, rw_g1, rw_g2, rw_k_k, rw_k_a, rw_r_k, rw_ln_w, rw_ln_b, rw_w_o,
                  ret_w_in, ret_gn_w, ret_w_out, ffn_w1, ffn_w3, ffn_w2, table, out):
    units = {}
    total = 0
    for name, n in (("decay", 2), ("rate", 2), ("key", 16), ("rec", 16), ("val", 16), ("gate", 4), ("rw_out", DT),
                    ("up0", 8 * UP_BLOCKS), ("down0", FT), ("ret", 12 * RET_HEADS), ("ret_out", 2 * DT),
                    ("up1", 8 * UP_BLOCKS), ("down1", FT)):
        units[name] = total
        total += n

    w1s = [ffn_w1[l].rearrange("(kt p) n -> p kt n", p=P) for l in range(2)]
    w3s = [ffn_w3[l].rearrange("(kt p) n -> p kt n", p=P) for l in range(2)]
    w2s = [ffn_w2[l].rearrange("(kt p) n -> p kt n", p=P) for l in range(2)]
    ret_in = ret_w_in[0].rearrange("(kt p) n -> p kt n", p=P)
    ret_out = ret_w_out[0].rearrange("(kt p) n -> p kt n", p=P)
    x_dram = x[0].rearrange("(tt p) n -> p tt n", p=P)
    out_dram = out[0].rearrange("(tt p) n -> p tt n", p=P)

    base = 16512
    KB = 1024

    def place(name, shape, offset, dtype=F32):
        return nc.alloc_sbuf_tensor_at(name, shape, dtype, offset=base + offset)

    x_res = place("x_res", [P, DT, T], 0)
    raw = place("raw", [P, 2, UNIT], 16 * KB)
    w_hi = place("w_hi", [P, 2, UNIT], 32 * KB, F32R)
    w_lo = place("w_lo", [P, 2, UNIT], 48 * KB, F32R)
    x_hi = place("x_hi", [P, DT, T], 64 * KB, F32R)
    x_lo = place("x_lo", [P, DT, T], 80 * KB, F32R)
    work = place("work", [P, 2, 4, T], 96 * KB)
    small = 104 * KB
    tab_cols = TABLE_COLS["ret_decay"][0]
    tab = place("tab", [P, tab_cols], small)
    small += 4 * tab_cols + 28
    small -= small % 32
    prm = place("prm", [P, PARAM_BLOCKS * P], small)
    small += 4 * PARAM_BLOCKS * P
    rstd = place("rstd", [P, T], small)
    rvar = place("rvar", [P, T], small + KB)
    rvar_at = small + KB
    small += 2 * KB
    zone = small + (-small) % 32
    hid_hi = place("hid_hi", [P, FT, T], zone, F32R)
    hid_lo = place("hid_lo", [P, FT, T], zone + 44 * KB, F32R)
    squares = place("squares", [P, 2, 4, T], zone)
    x_rows = place("x_rows", [P, 2, D], zone)
    param_rows = place("param_rows", [P, PARAM_BLOCKS, P], zone + 16 * KB)
    out_rows = place("out_rows", [P, 2, D], zone)
    ret_hi = place("ret_hi", [P, 2 * DT, T], zone, F32R)
    ret_lo = place("ret_lo", [P, 2 * DT, T], zone + 32 * KB, F32R)
    z = zone + 64 * KB
    ret_decay = place("ret_decay", [P, RET_HEADS, T], z)
    cos = place("cos", [P, T], z + 8 * KB)
    sin = place("sin", [P, T], z + 9 * KB)
    qk_rot = place("qk_rot", [P, 2, 2, T], z + 10 * KB)
    v_rows = place("v_rows", [P, 2, RET_DV], z + 14 * KB)
    probs = place("probs", [P, 3 * P], z + 18 * KB)
    silu_g = place("silu_g", [P, 4, T], z + 20 * KB)
    y_head = place("y_head", [P, 4, T], z + 24 * KB)
    assert base + z + 28 * KB <= nc.sbuf_usable_end and base + zone + 88 * KB <= nc.sbuf_usable_end
    pos_i = place("pos_i", [P, T], z + 14 * KB, I32)
    rot_a, rot_b, rot_c, rot_d = (work[:, k // 2, 2 * (k % 2):2 * (k % 2) + 2] for k in range(4))

    h_in = place("h_in", [P, DT, T + 1], zone)
    out_gate = place("out_gate", [P, DT, T], zone)
    quad_at = zone + 4 * DT * (T + 1)
    quad = place("quad", [P, 4, DT, T], quad_at)
    att_hi = place("att_hi", [P, DT, T], quad_at, F32R)
    att_lo = place("att_lo", [P, DT, T], quad_at + 16 * KB, F32R)
    solve_t = place("solve_t", [P, 1024], quad_at + 32 * KB)
    val_t = place("val_t", [P, 4, T], quad_at + 36 * KB)
    rk_t = place("rk_t", [P, 4, T], quad_at + 40 * KB)
    bonus = place("bonus", [P, DT, T], quad_at + 32 * KB)
    inv_at = quad_at + 64 * KB
    assert base + inv_at + 16 * KB <= nc.sbuf_usable_end
    prep_t = place("prep_t", [P, 4, T], inv_at)
    prep_x = place("prep_x", [P, 2, 4, T], inv_at + 4 * KB)
    b_wide = place("b_wide", [P, 2, NC, 2, 64], inv_at + 4 * KB)
    tri_rows = place("tri_rows", [P, 8, NC, 64], inv_at + 8 * KB)
    tri = place("tri", [P, 64, 64], inv_at)
    inv_t = place("inv_t", [P, PAIRS * NC, 64], inv_at)
    lora_hi = place("lora_hi", [P, 1, T], inv_at + 12 * KB, F32R)
    lora_lo = place("lora_lo", [P, 1, T], inv_at + 13 * KB, F32R)
    lora_mid = place("lora_mid", [P, 1, T], inv_at + 14 * KB)
    glora_hi = place("glora_hi", [P, 2, T], 96 * KB, F32R)
    glora_lo = place("glora_lo", [P, 2, T], 98 * KB, F32R)
    chunk_decay = place("chunk_decay", [P, PAIRS, NC], rvar_at)
    prep_inv = place("prep_inv", [P, 4, T], inv_at + 12 * KB)
    v_feat = place("v_feat", [P, DT, T], 64 * KB)
    y_all = place("y_all", [P, PAIRS, NC, 64], 80 * KB)
    scan_at = 32 * KB
    quad_wide = place("quad_wide", [P, 8, 4, 2, 64], scan_at)
    v_wide = place("v_wide", [P, 4, 2, 64], scan_at + 16 * KB)
    inv_wide = place("inv_wide", [P, 8, 2, 64], scan_at + 18 * KB)
    kbv_rows = place("kbv_rows", [P, 4, 2 * P + 64], scan_at + 22 * KB)
    state = place("state", [P, PAIRS, 64], scan_at + 27 * KB)
    mix_wide = place("mix_wide", [P, 4, 3, 2, 64], 96 * KB)
    x_stack = place("x_stack", [P, 2, 64], 102 * KB)
    u_stack = place("u_stack", [P, 2, 64], 102 * KB + 512)
    state_dec = place("state_dec", [P, 4, 64], 103 * KB)
    y_wide = place("y_wide", [P, 4, NC, 2, 64], inv_at)
    y_mean = place("y_mean", [P, 64], rvar_at - KB)
    y_inv = place("y_inv", [P, 64], rvar_at - KB + 256)
    y_scale = place("y_scale", [P, 64, 2], rvar_at - KB + 512)
    att = place("att", [P, DT, T], 64 * KB)

    def const(name):
        c, n = TABLE_COLS[name]
        return tab[:, c:c + n]

    def param(name, tile):
        r, _ = PARAM_ROWS[name]
        return prm[:, r + tile:r + tile + 1]

    ident, ones = const("ident"), const("ones")

    with ExitStack() as ctx:
        def sem(name):
            return ctx.enter_context(nc.semaphore(name))

        acc = ctx.enter_context(nc.psum_tensor("acc", [P, 8, 512], F32))

        w_loaded = [[sem(f"w_loaded{slot}{half}") for half in range(2)] for slot in range(2)]
        hi_done = sem("hi_done")
        lo_done = sem("lo_done")
        unit_used = sem("unit_used")
        tables_in = sem("tables_in")
        rows_in = sem("rows_in")
        params_t = sem("params_t")
        params_ready = sem("params_ready")
        k_rest_ready = sem("k_rest_ready")
        x_turned = sem("x_turned")
        x_ready = sem("x_ready")
        norm_sq = sem("norm_sq")
        norm_stat = sem("norm_stat")
        norm_var = sem("norm_var")
        norm_eps_added = sem("norm_eps_added")
        norm_rstd = sem("norm_rstd")
        hn_ready = sem("hn_ready")
        hn_hi = sem("hn_hi")
        hn_lo = sem("hn_lo")
        up_free = sem("up_free")
        gate_scaled = sem("gate_scaled")
        glu_done = sem("glu_done")
        silu_done = sem("silu_done")
        hid_hi_done = sem("hid_hi_done")
        hid_lo_done = sem("hid_lo_done")
        out_turned = sem("out_turned")
        out_ready = sem("out_ready")
        out_stored = sem("out_stored")
        pos_in = sem("pos_in")
        decay_in = sem("decay_in")
        rope_step = sem("rope_step")
        rope_sin = sem("rope_sin")
        rope_ready = sem("rope_ready")
        rot_mul = sem("rot_mul")
        rot_done = sem("rot_done")
        v_evac = sem("v_evac")
        silu_g_done = sem("silu_g_done")
        scores_done = sem("scores_done")
        probs_done = sem("probs_done")
        y_done = sem("y_done")
        y_evac = sem("y_evac")
        mean_done = sem("mean_done")
        centred = sem("centred")
        y_sq = sem("y_sq")
        var_done = sem("var_done")
        y_eps_added = sem("y_eps_added")
        y_var = sem("y_var")
        y_rstd = sem("y_rstd")
        y_scaled = sem("y_scaled")
        gated = sem("gated")
        ret_hi_done = sem("ret_hi_done")
        ret_lo_done = sem("ret_lo_done")

        def load_unit(sp, n, src, shape, off=0, parts=P, after_short=False):
            rows, cols = shape
            for half in range(2):
                if rows > 1:
                    r, c = slice(half * rows // 2, (half + 1) * rows // 2), slice(0, cols)
                else:
                    r, c = slice(0, 1), slice(half * cols // 2, (half + 1) * cols // 2)
                if n >= 2:
                    sp.wait_ge(lo_done, 2 * (n - 2) + (2 if after_short else half + 1) + 2 * off)
                dst = raw[0:parts, n % 2, 0:rows * cols].rearrange("p (k n) -> p k n", k=rows)
                sp.dma_start(dst[:, r, c], src[:, r, c]).then_inc(w_loaded[n % 2][half], 16)

        def split_hi(act, n, off=0, parts=P, width=UNIT):
            if n >= 2:
                act.wait_ge(unit_used, n - 1 + off)
            for half in range(2):
                act.wait_ge(w_loaded[n % 2][half], 16 * (n // 2 + 1) + 8 * off)
                c = slice(half * width // 2, (half + 1) * width // 2)
                nc.scalar.activation(w_hi[0:parts, n % 2, c], raw[0:parts, n % 2, c], ACT.Copy).then_inc(hi_done, 1)

        def split_lo(dve, n, off=0, parts=P, width=UNIT):
            for half in range(2):
                dve.wait_ge(hi_done, 2 * n + half + 1 + 2 * off)
                c = slice(half * width // 2, (half + 1) * width // 2)
                nc.vector.tensor_tensor(w_lo[0:parts, n % 2, c], raw[0:parts, n % 2, c],
                                        w_hi[0:parts, n % 2, c].bitcast(F32), ALU.subtract).then_inc(lo_done, 1)

        def unit_product(pe, n, shape, xs, tile_out, first, last, off=0, parts=P):
            pe.wait_ge(lo_done, 2 * (n + 1) + 2 * off)
            rows, cols = shape
            hi = w_hi[0:parts, n % 2, 0:rows * cols].rearrange("p (k n) -> p k n", k=rows)
            lo = w_lo[0:parts, n % 2, 0:rows * cols].rearrange("p (k n) -> p k n", k=rows)
            for k in range(rows):
                a_hi, a_lo = xs(k)
                for f in range(-(-cols // P)):
                    c = slice(f * P, min((f + 1) * P, cols))
                    for m, (w, a) in enumerate(((hi, a_hi), (hi, a_lo), (lo, a_hi))):
                        mm = nc.tensor.matmul(tile_out(f), w[:, k, c], a,
                                              start=(first and k == 0 and m == 0 and f % 2 == 0),
                                              stop=(last and k == rows - 1 and m == 2), skip_group_check=True)
            mm.then_inc(unit_used, 1)

        def x_tiles(k0, pe=None, fill=None):
            def xs(k):
                if pe is not None and (k0 + k) % 4 == 0:
                    pe.wait_ge(hn_lo, 4 * fill + (k0 + k) // 4 + 1)
                return x_hi[:, k0 + k, :], x_lo[:, k0 + k, :]
            return xs

        def bank_tile(b, f):
            if isinstance(b, int):
                return acc[:, b + f // 2, T * (f % 2):T * (f % 2) + T]
            return acc[:, bass.ds(b + f // 2, 1), T * (f % 2):T * (f % 2) + T].rearrange("p a t -> p (a t)")

        def norm_act(act, q, early=None):
            for j in range(4):
                act.wait_ge(x_ready, 4 * q + j + 1)
                if j >= 2:
                    act.wait_ge(norm_stat, 4 * q + j - 1)
                nc.scalar.activation(work[:, j % 2], x_res[:, 4 * j:4 * j + 4], ACT.Square).then_inc(norm_sq, 1)
            if early is not None:
                early(0)
                early(1)
            act.wait_ge(norm_var, q + 1)
            nc.scalar.activation(rstd[:], rvar[:], ACT.Sqrt).then_inc(norm_rstd, 1)

        def norm_pe(pe, q, src=work):
            for j in range(4):
                pe.wait_ge(norm_sq, 4 * q + j + 1)
                for k in range(4):
                    mm = nc.tensor.matmul(acc[:, 7, 0:T], ones, src[:, j % 2, k], start=(j == 0 and k == 0),
                                          stop=(j == 3 and k == 3))
                mm.then_inc(norm_stat, 1)

        def late_square(act, q, j):
            act.wait_ge(x_ready, 4 * q + 4)
            if j >= 2:
                act.wait_ge(norm_stat, 4 * q + j - 1)
            nc.scalar.activation(squares[:, j % 2], x_res[:, 4 * j:4 * j + 4], ACT.Square).then_inc(norm_sq, 1)

        def late_root(act, q):
            act.wait_ge(norm_var, q + 1)
            nc.scalar.activation(rstd[:], rvar[:], ACT.Sqrt).then_inc(norm_rstd, 1)

        def norm_dve(dve, q, early=None):
            if early is not None:
                early(0)
                early(1)
            dve.wait_ge(norm_stat, 4 * q + 4)
            nc.vector.tensor_scalar(rvar[:], acc[:, 7, 0:T], 1.0 / D, NORM_EPS, ALU.mult,
                                    ALU.add).then_inc(norm_eps_added, 1)
            dve.wait_ge(norm_eps_added, q + 1)
            nc.vector.reciprocal(rvar[:], rvar[:]).then_inc(norm_var, 1)
            dve.wait_ge(norm_rstd, q + 1)

        def norm_group(j, gain, gain_tile):
            for k in range(4):
                last = nc.vector.scalar_tensor_tensor(out=work[:, j % 2, k], in0=x_res[:, 4 * j + k],
                                                      scalar=param(gain, gain_tile + 4 * j + k), in1=rstd[:],
                                                      op0=ALU.mult, op1=ALU.mult)
            return last

        def fill_act(act, i, before_group=None, after_group=None):
            for j in range(4):
                if before_group is not None:
                    before_group(j)
                act.wait_ge(hn_ready, 4 * i + j + 1)
                nc.scalar.activation(x_hi[:, 4 * j:4 * j + 4], work[:, j % 2], ACT.Copy).then_inc(hn_hi, 1)
                if after_group is not None:
                    after_group(j)

        def fill_dve(dve, i, group, after_group=None):
            def low(j):
                dve.wait_ge(hn_hi, 4 * i + j + 1)
                nc.vector.tensor_tensor(x_lo[:, 4 * j:4 * j + 4], work[:, j % 2],
                                        x_hi[:, 4 * j:4 * j + 4].bitcast(F32), ALU.subtract).then_inc(hn_lo, 1)

            for j in range(4):
                if j >= 2:
                    low(j - 2)
                    dve.wait_ge(hn_lo, 4 * i + j - 1)
                group(j).then_inc(hn_ready, 1)
                if after_group is not None:
                    after_group(j)
            low(2)
            low(3)
            dve.wait_ge(hn_lo, 4 * i + 4)

        def late_group(l, j):
            for k in range(4):
                last = nc.vector.tensor_scalar(work[:, j % 2, k], x_res[:, 4 * j + k],
                                               param("norm_ffn", DT * l + 4 * j + k), None, ALU.mult)
            last.then_inc(hn_ready, 1)

        def late_low(dve, i, j):
            dve.wait_ge(hn_hi, 4 * i + j + 1)
            nc.vector.tensor_tensor(x_lo[:, 4 * j:4 * j + 4], work[:, j % 2], x_hi[:, 4 * j:4 * j + 4].bitcast(F32),
                                    ALU.subtract).then_inc(hn_lo, 1)

        def late_high(act, i, j):
            act.wait_ge(hn_ready, 4 * i + j + 1)
            nc.scalar.activation(x_hi[:, 4 * j:4 * j + 4], work[:, j % 2], ACT.Copy).then_inc(hn_hi, 1)

        def before_up_dve(dve, l, q):
            dve.wait_ge(x_ready, 4 * q + 2)
            for j in range(2):
                late_group(l, j)

        def up_sp(sp, l):
            n0 = units[f"up{l}"]
            with sp.Fori(0, UP_BLOCKS) as i:
                for u in range(8):
                    w = (w1s, w3s)[u // 4][l]
                    load_unit(sp, n0 + u, w[:, 4 * (u % 4):4 * (u % 4) + 4, bass.ds(i * 512, 512)], (4, 512), off=8 * i)

        def up_act(act, l):
            n0, fill, q = units[f"up{l}"], fill_of[f"up{l}"], norm_of[f"up{l}"]

            def silu(i):
                act.wait_ge(gate_scaled, UP_BLOCKS * l + 1 + i)
                nc.scalar.activation(work[:, 0], work[:, 0], ACT.Silu).then_inc(silu_done, 1)

            def hidden_hi(i):
                act.wait_ge(glu_done, UP_BLOCKS * l + 2 + i)
                nc.scalar.activation(hid_hi[:, bass.ds(4 * i, 4), :], work[:, 1], ACT.Copy).then_inc(hid_hi_done, 1)

            for j in range(2):
                late_high(act, fill, j)
            split_hi(act, n0)
            split_hi(act, n0 + 1)
            late_square(act, q, 0)
            late_square(act, q, 1)
            late_high(act, fill, 2)
            late_high(act, fill, 3)
            split_hi(act, n0 + 2)
            split_hi(act, n0 + 3)
            late_square(act, q, 2)
            late_square(act, q, 3)
            split_hi(act, n0 + 4)
            late_root(act, q)
            for u in range(5, 8):
                split_hi(act, n0 + u)
            with act.Fori(1, UP_BLOCKS) as i:
                off = 8 * i
                split_hi(act, n0, off)
                split_hi(act, n0 + 1, off)
                silu(i - 1)
                for u in range(2, 6):
                    split_hi(act, n0 + u, off)
                hidden_hi(i - 1)
                split_hi(act, n0 + 6, off)
                split_hi(act, n0 + 7, off)
            split_hi(act, units[f"down{l}"])
            silu(UP_BLOCKS - 1)
            split_hi(act, units[f"down{l}"] + 1)
            hidden_hi(UP_BLOCKS - 1)

        def up_dve(dve, l):
            n0, fill, q = units[f"up{l}"], fill_of[f"up{l}"], norm_of[f"up{l}"]

            def scaled(i, half):
                src = acc[:, bass.ds((i % 2) * 4 + 2 * half, 2), :].rearrange("p b (a t) -> p (b a) t", a=2)
                factor = rstd[:].rearrange("p (a t) -> p a t", a=1).to_broadcast([P, 4, T])
                return nc.vector.tensor_tensor(work[:, half], src, factor, ALU.mult)

            def gate_half(i):
                dve.wait_ge(unit_used, 8 * i + n0 + 8)
                dve.wait_ge(glu_done, 1 + UP_BLOCKS * l + i)
                scaled(i, 0).then_inc(gate_scaled, 1)

            def glu(i):
                dve.wait_ge(hid_lo_done, 1 + UP_BLOCKS * l + i)
                scaled(i, 1).then_inc(up_free, 1)
                dve.wait_ge(up_free, UP_BLOCKS * l + 3 + i)
                dve.wait_ge(silu_done, UP_BLOCKS * l + 1 + i)
                nc.vector.tensor_tensor(work[:, 1], work[:, 1], work[:, 0], ALU.mult).then_inc(glu_done, 1)

            def hidden_lo(i):
                dve.wait_ge(hid_hi_done, UP_BLOCKS * l + 1 + i)
                nc.vector.tensor_tensor(hid_lo[:, bass.ds(4 * i, 4), :], work[:, 1],
                                        hid_hi[:, bass.ds(4 * i, 4), :].bitcast(F32),
                                        ALU.subtract).then_inc(hid_lo_done, 1)

            split_lo(dve, n0 + 1)
            dve.wait_ge(x_ready, 4 * q + 4)
            for j in range(2, 4):
                dve.wait_ge(hn_lo, 4 * fill + j - 1)
                late_group(l, j)
            late_low(dve, fill, 2)
            late_low(dve, fill, 3)
            dve.wait_ge(hn_lo, 4 * fill + 4)
            split_lo(dve, n0 + 2)
            split_lo(dve, n0 + 3)
            norm_dve(dve, q, lambda u: split_lo(dve, n0 + 4) if u == 0 else None)
            for u in range(5, 8):
                split_lo(dve, n0 + u)
            with dve.Fori(1, UP_BLOCKS) as i:
                off = 8 * i
                split_lo(dve, n0, off)
                gate_half(i - 1)
                split_lo(dve, n0 + 1, off)
                split_lo(dve, n0 + 2, off)
                glu(i - 1)
                for u in range(3, 7):
                    split_lo(dve, n0 + u, off)
                hidden_lo(i - 1)
                split_lo(dve, n0 + 7, off)
            split_lo(dve, units[f"down{l}"])
            gate_half(UP_BLOCKS - 1)
            glu(UP_BLOCKS - 1)
            split_lo(dve, units[f"down{l}"] + 1)
            hidden_lo(UP_BLOCKS - 1)

        def up_pe(pe, l, fill):
            n0, q = units[f"up{l}"], norm_of[f"up{l}"]

            def block(i):
                pe.wait_ge(up_free, 1 + UP_BLOCKS * l + i)
                for u in range(8):
                    pe.wait_ge(hn_lo, 4 * fill + u % 4 + 1)
                    bank = (i % 2) * 4 + 2 * (u // 4)
                    unit_product(pe, n0 + u, (4, 512), x_tiles(4 * (u % 4)), lambda f: bank_tile(bank, f),
                                 u % 4 == 0, u % 4 == 3, off=8 * i)
                    if isinstance(i, int) and u == 2:
                        norm_pe(pe, q, squares)

            block(0)
            pe.wait_ge(norm_eps_added, q + 1)
            with pe.Fori(1, UP_BLOCKS) as i:
                block(i)

        def out_sp(sp, stage, w, kt):
            for b in range(2):
                n0 = units[stage] + b * kt // 2
                with sp.Fori(0, kt // 4) as j:
                    for u in range(2):
                        load_unit(sp, n0 + u, w[:, bass.ds(4 * j + 2 * u, 2), 1024 * b:1024 * b + 1024], (2, 1024),
                                  off=2 * j)

        def out_act(act, stage, kt, early):
            for b in range(2):
                n0 = units[stage] + b * kt // 2
                with act.Fori(early if b == 0 else 0, kt // 4) as j:
                    for u in range(2):
                        split_hi(act, n0 + u, off=2 * j)

        def out_dve(dve, stage, kt, early, banks=(4, 0), between=None, before_last=None):
            n0 = units[stage]

            def add(b):
                for g in range(2):
                    dve.wait_ge(unit_used, n0 + (b + 1) * kt // 2)
                    o = x_res[:, 8 * b + 4 * g:8 * b + 4 * g + 4].rearrange("p a t -> p (a t)")
                    o = o.rearrange("p (c s) -> p c s", c=2)
                    bank = banks[b] + 2 * g
                    nc.vector.tensor_tensor(o, acc[:, bank:bank + 2], o, ALU.add).then_inc(x_ready, 1)

            with dve.Fori(early, kt // 4) as j:
                for u in range(2):
                    split_lo(dve, n0 + u, off=2 * j)
            n1 = n0 + kt // 2
            split_lo(dve, n1)
            split_lo(dve, n1 + 1)
            add(0)
            if between is not None:
                between()
            with dve.Fori(1, kt // 4) as j:
                for u in range(2):
                    split_lo(dve, n1 + u, off=2 * j)
            if before_last is not None:
                before_last()
            add(1)

        def out_pe(pe, stage, hi, lo, kt, before_block, before_last, banks=(4, 0), after_pair=()):
            for b in range(2):
                n0 = units[stage] + b * kt // 2
                bank = banks[b]

                def pair(j, first, last):
                    for u in range(2):
                        def xs(k):
                            if isinstance(j, int):
                                return hi[:, 4 * j + 2 * u + k, :], lo[:, 4 * j + 2 * u + k, :]
                            at = bass.ds(4 * j + 2 * u + k, 1)
                            return (hi[:, at, :].rearrange("p a t -> p (a t)"), lo[:, at, :].rearrange("p a t -> p (a t)"))
                        off, n = (0, n0 + 2 * j + u) if isinstance(j, int) else (2 * j, n0 + u)
                        unit_product(pe, n, (2, 1024), xs, lambda f: bank_tile(bank, f), first and u == 0,
                                     last and u == 1, off=off)

                before_block(b)
                pair(0, True, False)
                done = 1
                for k, inside in enumerate(after_pair if b == 0 else ()):
                    if k > 0:
                        pair(k, False, False)
                        done += 1
                    inside()
                with pe.Fori(done, kt // 4 - 1) as j:
                    pair(j, False, False)
                if b == 0:
                    before_last()
                pair(kt // 4 - 1, False, True)

        def down_pe(pe, l):
            def before_block(b):
                pe.wait_ge(up_free, 1 + UP_BLOCKS * (l + 1) + b)
                if b == 0:
                    pe.wait_ge(hid_lo_done, 1 + UP_BLOCKS * (l + 1) - 1)

            out_pe(pe, f"down{l}", hid_hi, hid_lo, FT, before_block,
                   lambda: pe.wait_ge(hid_lo_done, 1 + UP_BLOCKS * (l + 1)))

        def out_dve_then_up(dve, stage, kt, early, l):
            def before_last():
                for j in range(2):
                    late_low(dve, fill_of[f"up{l}"], j)
                split_lo(dve, units[f"up{l}"])

            out_dve(dve, stage, kt, early, (0, 4), lambda: before_up_dve(dve, l, norm_of[f"up{l}"]), before_last)

        TWO_PI = 2.0 * np.pi
        parts_2pi = []
        rest = TWO_PI
        for _ in range(3):
            e = 2.0 ** (7 - int(np.floor(np.log2(rest))))
            parts_2pi.append(float(np.floor(rest * e) / e))
            rest -= parts_2pi[-1]
        parts_2pi.append(float(np.float32(rest)))

        def rope_dve(dve):
            step = 0

            def then(ins):
                nonlocal step
                step += 1
                ins.then_inc(rope_step, 1)
                dve.wait_ge(rope_step, step)

            ang, turns, half = rot_b[:, 0], rot_b[:, 1], rot_c[:, 0]
            dve.wait_ge(pos_in, 16)
            then(nc.vector.tensor_copy(ang, pos_i[:]))
            then(nc.vector.tensor_scalar(ang, ang, const("inv_freq"), None, ALU.mult))
            then(nc.vector.tensor_scalar(turns, ang, 1.0 / TWO_PI, 1.5 * 2.0 ** 23, ALU.mult, ALU.add))
            then(nc.vector.tensor_scalar(turns, turns, 1.5 * 2.0 ** 23, None, ALU.subtract))
            for c in parts_2pi:
                then(nc.vector.scalar_tensor_tensor(out=ang, in0=turns, scalar=-c, in1=ang, op0=ALU.mult, op1=ALU.add))
            pi_below = 3.1415925
            then(nc.vector.tensor_scalar(ang, ang, pi_below, -pi_below, ALU.min, ALU.max))
            dve.wait_ge(rope_sin, 2)
            then(nc.vector.tensor_tensor(half, half, half, ALU.mult))
            nc.vector.tensor_scalar(cos[:], half, -2.0, 1.0, ALU.mult, ALU.add).then_inc(rope_ready, 1)

        rope_steps = 5 + len(parts_2pi)

        def rope_act(act):
            act.wait_ge(x_ready, 4 * (norm_of["ret"] + 1))
            act.dma_start(pos_i[:], positions.to_broadcast([P, T])).then_inc(pos_in, 16)
            c, n = TABLE_COLS["ret_decay"]
            act.dma_start(ret_decay[:], table[:, c:c + n].rearrange("p (h t) -> p h t", h=RET_HEADS)).then_inc(decay_in, 16)
            act.wait_ge(rope_step, rope_steps)
            nc.scalar.activation(sin[:], rot_b[:, 0], ACT.Sin).then_inc(rope_sin, 1)
            nc.scalar.activation(rot_c[:, 0], rot_b[:, 0], ACT.Sin, scale=0.5).then_inc(rope_sin, 1)

        n_ret = units["ret"]

        def ret_sp(sp):
            with sp.Fori(0, RET_HEADS) as h:
                off = 12 * h
                for u in range(4):
                    src = ret_in[:, 8 * (u % 2):8 * (u % 2) + 8, bass.ds(D * (u // 2) + RET_DK * h, RET_DK)]
                    load_unit(sp, n_ret + u, src, (8, RET_DK), off=off)
                for u in range(8):
                    src = ret_in[:, 4 * (u % 4):4 * (u % 4) + 4, bass.ds(2 * D * (1 + u // 4) + RET_DV * h, RET_DV)]
                    load_unit(sp, n_ret + 4 + u, src, (4, RET_DV), off=off)

        def ret_pe(pe, fill):
            def values_unit(u, off):
                n = n_ret + 4 + u
                pe.wait_ge(lo_done, 2 * (n + 1) + 2 * off)
                hi = w_hi[:, n % 2, :].rearrange("p (k n) -> p k n", k=4)
                lo = w_lo[:, n % 2, :].rearrange("p (k n) -> p k n", k=4)
                for k in range(4):
                    for tt in range(2):
                        c = slice(P * tt, P * tt + P)
                        for m, (a, w) in enumerate(((x_hi, hi), (x_lo, hi), (x_hi, lo))):
                            mm = nc.tensor.matmul(acc[:, 2 + tt, :], a[:, 4 * u + k, c], w[:, k, :],
                                                  start=(u == 0 and k == 0 and m == 0),
                                                  stop=(u == 3 and k == 3 and m == 2), skip_group_check=True)
                mm.then_inc(unit_used, 1)

            def outputs(h):
                pe.wait_ge(probs_done, 1 + h)
                pe.wait_ge(v_evac, 1 + h)
                pe.wait_ge(y_var, 1 + h)
                for f in range(4):
                    c = slice(P * f, P * f + P)
                    nc.tensor.matmul(bank_tile(6, f), v_rows[:, 0, c], probs[:, 0:T], start=(f % 2 == 0), stop=False,
                                     skip_group_check=True)
                    mm = nc.tensor.matmul(bank_tile(6, f)[:, P:T], v_rows[:, 1, c], probs[:, T:T + P], start=False,
                                          stop=True, skip_group_check=True)
                mm.then_inc(y_done, 1)

            def head_sum(h, ready, src, col, done):
                pe.wait_ge(ready, 1 + h)
                for f in range(4):
                    mm = nc.tensor.matmul(acc[:, 6, col:col + T], ones, src[:, f], start=(f == 0), stop=(f == 3),
                                          skip_group_check=True)
                mm.then_inc(done, 1)

            def scores(h):
                pe.wait_ge(rot_done, 1 + h)
                for jt in range(2):
                    for d in range(2):
                        mm = nc.tensor.matmul(acc[:, 7, T * jt:T + P * jt], qk_rot[:, 1, d, P * jt:P * jt + P],
                                              qk_rot[:, 0, d, P * jt:T], start=(jt == 0 and d == 0), stop=(d == 1),
                                              skip_group_check=True)
                mm.then_inc(scores_done, 1)

            def head(h, behind):
                off = 12 * h
                if behind:
                    pe.wait_ge(rot_done, h)
                for u in range(4):
                    xs = x_tiles(8 * (u % 2)) if behind else x_tiles(8 * (u % 2), pe, fill)
                    unit_product(pe, n_ret + u, (8, RET_DK), xs, lambda f: bank_tile(u // 2, f),
                                 u % 2 == 0, u % 2 == 1, off=off)
                if behind:
                    outputs(h - 1)
                values_unit(0, off)
                values_unit(1, off)
                if behind:
                    head_sum(h - 1, y_evac, y_head, 0, mean_done)
                values_unit(2, off)
                values_unit(3, off)
                if behind:
                    head_sum(h - 1, y_sq, work[:, 0], T, var_done)
                scores(h)
                if behind:
                    pe.wait_ge(silu_g_done, h)
                for u in range(4):
                    unit_product(pe, n_ret + 8 + u, (4, 512), x_tiles(4 * u), lambda f: bank_tile(4, f), u == 0,
                                 u == 3, off=off)

            head(0, False)
            with pe.Fori(1, RET_HEADS) as h:
                head(h, True)
            h = RET_HEADS - 1
            outputs(h)
            return (lambda: head_sum(h, y_evac, y_head, 0, mean_done),
                    lambda: head_sum(h, y_sq, work[:, 0], T, var_done))

        def two_banks(ap):
            return ap.rearrange("p a t -> p (a t)").rearrange("p (b s) -> p b s", b=2)

        def ret_act(act):
            def silu(h):
                act.wait_ge(unit_used, n_ret + 12 + 12 * h)
                act.wait_ge(gated, 1 + h)
                nc.scalar.activation(two_banks(silu_g[:]), acc[:, 4:6], ACT.Silu).then_inc(silu_g_done, 1)

            def take_y(h):
                act.wait_ge(y_done, 1 + h)
                act.wait_ge(gated, 1 + h)
                nc.scalar.activation(two_banks(y_head[:]), acc[:, 6:8], ACT.Copy).then_inc(y_evac, 1)

            def square(h):
                act.wait_ge(centred, 1 + h)
                nc.scalar.activation(work[:, 0], y_head[:], ACT.Square).then_inc(y_sq, 1)

            def root(h):
                act.wait_ge(y_var, 2 + h)
                nc.scalar.activation(rstd[:], rvar[:], ACT.Sqrt).then_inc(y_rstd, 1)

            def take_v(h):
                act.wait_ge(unit_used, n_ret + 8 + 12 * h)
                act.wait_ge(y_done, h)
                nc.scalar.activation(v_rows[:], acc[:, 2:4], ACT.Copy).then_inc(v_evac, 1)

            def high(h):
                act.wait_ge(gated, 2 + h)
                nc.scalar.activation(ret_hi[:, bass.ds(4 * h, 4), :], work[:, 1], ACT.Copy).then_inc(ret_hi_done, 1)

            def head(h, behind):
                off = 12 * h
                if behind:
                    split_hi(act, n_ret, off)
                    split_hi(act, n_ret + 1, off)
                    silu(h - 1)
                split_hi(act, n_ret + 2, off)
                split_hi(act, n_ret + 3, off)
                split_hi(act, n_ret + 4, off)
                split_hi(act, n_ret + 5, off)
                if behind:
                    take_y(h - 1)
                split_hi(act, n_ret + 6, off)
                split_hi(act, n_ret + 7, off)
                if behind:
                    square(h - 1)
                split_hi(act, n_ret + 8, off)
                split_hi(act, n_ret + 9, off)
                if behind:
                    root(h - 1)
                take_v(h)
                split_hi(act, n_ret + 10, off)
                if behind:
                    high(h - 1)
                split_hi(act, n_ret + 11, off)

            head(0, False)
            with act.Fori(1, RET_HEADS) as h:
                head(h, True)
            h = RET_HEADS - 1
            n_out = units["ret_out"]
            split_hi(act, n_out)
            silu(h)
            take_y(h)
            split_hi(act, n_out + 1)
            split_hi(act, n_out + 2)
            square(h)
            split_hi(act, n_out + 3)
            split_hi(act, n_out + 4)
            root(h)
            split_hi(act, n_out + 5)
            high(h)

        def ret_dve(dve):
            def rotate(h, behind):
                dve.wait_ge(unit_used, n_ret + 4 + 12 * h)
                dve.wait_ge(scores_done, h)
                dve.wait_ge(rot_done, h)
                if behind:
                    dve.wait_ge(ret_lo_done, 1 + h - 1)
                first, second = acc[:, 0:2, 0:T], acc[:, 0:2, T:2 * T]
                c2 = cos[:].rearrange("p (a t) -> p a t", a=1).to_broadcast([P, 2, T])
                s2 = sin[:].rearrange("p (a t) -> p a t", a=1).to_broadcast([P, 2, T])
                nc.vector.tensor_tensor(rot_a, first, c2, ALU.mult)
                nc.vector.tensor_tensor(rot_b, second, s2, ALU.mult)
                nc.vector.tensor_tensor(rot_c, first, s2, ALU.mult)
                nc.vector.tensor_tensor(rot_d, second, c2, ALU.mult).then_inc(rot_mul, 1)
                dve.wait_ge(rot_mul, 1 + h)
                nc.vector.tensor_tensor(qk_rot[:, :, 0, :], rot_a, rot_b, ALU.subtract)
                nc.vector.tensor_tensor(qk_rot[:, :, 1, :], rot_c, rot_d, ALU.add).then_inc(rot_done, 1)

            def decay_scores(h):
                dve.wait_ge(scores_done, 1 + h)
                dve.wait_ge(y_done, h)
                d = ret_decay[:, bass.ds(h, 1), :].rearrange("p a t -> p (a t)")
                nc.vector.tensor_tensor(probs[:, 0:T], acc[:, 7, 0:T], d, ALU.mult)
                nc.vector.tensor_tensor(probs[:, T:T + P], acc[:, 7, T:T + P], d[:, 0:P], ALU.mult).then_inc(probs_done, 1)

            def centre(h):
                dve.wait_ge(mean_done, 1 + h)
                mean = acc[:, 6, 0:T]
                for f in range(4):
                    last = nc.vector.scalar_tensor_tensor(out=y_head[:, f], in0=mean, scalar=-1.0 / RET_DV,
                                                          in1=y_head[:, f], op0=ALU.mult, op1=ALU.add)
                last.then_inc(centred, 1)

            def variance(h):
                dve.wait_ge(var_done, 1 + h)
                dve.wait_ge(y_rstd, 1 + h)
                nc.vector.tensor_scalar(rvar[:], acc[:, 6, T:2 * T], 1.0 / RET_DV, NORM_EPS, ALU.mult,
                                        ALU.add).then_inc(y_eps_added, 1)
                dve.wait_ge(y_eps_added, 1 + h)
                nc.vector.reciprocal(rvar[:], rvar[:]).then_inc(y_var, 1)

            def gate(h):
                dve.wait_ge(y_rstd, 2 + h)
                r0, _ = PARAM_ROWS["ret_gn_w"]
                for f in range(4):
                    gain = prm[:, bass.ds(4 * h + (r0 + f), 1)]
                    last = nc.vector.scalar_tensor_tensor(out=y_head[:, f], in0=y_head[:, f], scalar=gain, in1=rstd[:],
                                                          op0=ALU.mult, op1=ALU.mult)
                last.then_inc(y_scaled, 1)
                dve.wait_ge(y_scaled, 1 + h)
                dve.wait_ge(silu_g_done, 1 + h)
                dve.wait_ge(ret_lo_done, 1 + h)
                nc.vector.tensor_tensor(work[:, 1], y_head[:], silu_g[:], ALU.mult).then_inc(gated, 1)

            def low(h):
                dve.wait_ge(ret_hi_done, 1 + h)
                nc.vector.tensor_tensor(ret_lo[:, bass.ds(4 * h, 4), :], work[:, 1],
                                        ret_hi[:, bass.ds(4 * h, 4), :].bitcast(F32), ALU.subtract).then_inc(ret_lo_done, 1)

            def head(h, behind):
                off = 12 * h
                for u in range(0 if behind else 2, 6):
                    split_lo(dve, n_ret + u, off)
                rotate(h, behind)
                split_lo(dve, n_ret + 6, off)
                if behind:
                    centre(h - 1)
                split_lo(dve, n_ret + 7, off)
                split_lo(dve, n_ret + 8, off)
                if behind:
                    variance(h - 1)
                split_lo(dve, n_ret + 9, off)
                decay_scores(h)
                if behind:
                    gate(h - 1)
                split_lo(dve, n_ret + 10, off)
                split_lo(dve, n_ret + 11, off)
                if behind:
                    low(h - 1)

            dve.wait_ge(rope_ready, 1)
            dve.wait_ge(decay_in, 16)
            head(0, False)
            with dve.Fori(1, RET_HEADS) as h:
                head(h, True)
            h = RET_HEADS - 1
            n_out = units["ret_out"]
            split_lo(dve, n_out)
            split_lo(dve, n_out + 1)
            split_lo(dve, n_out + 2)
            centre(h)
            split_lo(dve, n_out + 3)
            split_lo(dve, n_out + 4)
            variance(h)
            split_lo(dve, n_out + 5)
            gate(h)
            low(h)

        SLOT_K, SLOT_B, SLOT_A, SLOT_R = range(4)
        DECAY_SCALE = float(np.exp(-0.5))
        GROUPS = PAIRS * NC
        n_dec, n_rate, n_gate = (units[k] for k in ("decay", "rate", "gate"))
        MU = {"rec": 0, "decay": 1, "key": 2, "val": 3, "rate": 4, "gate": 5}
        BLOCKS_BEFORE = {"key": 0, "rec": 4, "val": 8}
        W_ROW = {"rec": 0, "key": 1, "val": 2}

        h_ready = sem("h_ready")
        h_zero = sem("h_zero")
        mix_diff = sem("mix_diff")
        lora_act = sem("lora_act")
        lora_hi_done = sem("lora_hi_done")
        lora_lo_done = sem("lora_lo_done")
        sig_done = sem("sig_done")
        cum_done = sem("cum_done")
        block_free = sem("block_free")
        kk_raw = sem("kk_raw")
        kk_sq = sem("kk_sq")
        kk_sum = sem("kk_sum")
        kk_root = sem("kk_root")
        kk_step = sem("kk_step")
        cum_gap = sem("cum_gap")
        decayed = sem("decayed")
        prep_step = sem("prep_step")
        prep_done = sem("prep_done")
        b_wide_done = sem("b_wide_done")
        tri_mm = sem("tri_mm")
        tri_masked = sem("tri_masked")
        tri_stored = [sem("tri_stored0"), sem("tri_stored1")]
        tri_loaded = sem("tri_loaded")
        a_stored = sem("a_stored")
        solve_step = sem("solve_step")
        inv_stored = sem("inv_stored")
        inv_loaded = sem("inv_loaded")
        val_out = sem("val_out")
        rk_done = sem("rk_done")
        rk_sum = sem("rk_sum")
        bonus_done = sem("bonus_done")
        val_stored = sem("val_stored")
        bonus_stored = sem("bonus_stored")
        gate_out = sem("gate_out")
        v_loaded = sem("v_loaded")
        bonus_loaded = sem("bonus_loaded")
        wide_done = sem("wide_done")
        state_zero = sem("state_zero")
        m_mm = sem("m_mm")
        m_done = sem("m_done")
        kbv_done = sem("kbv_done")
        x_mm = sem("x_mm")
        x_done = sem("x_done")
        u_mm = sem("u_mm")
        u_done = sem("u_done")
        y_mm = sem("y_mm")
        y_taken = sem("y_taken")
        s_mm = sem("s_mm")
        dec_done = sem("dec_done")
        s_done = sem("s_done")
        ln_step = sem("ln_step")
        ln_centred = sem("ln_centred")
        ln_sq = sem("ln_sq")
        ln_var = sem("ln_var")
        ln_scale = sem("ln_scale")
        att_gain = sem("att_gain")
        att_bonus = sem("att_bonus")
        ln_root = sem("ln_root")
        y_wide_first = sem("y_wide_first")
        y_wide_done = sem("y_wide_done")
        yt_mm = sem("yt_mm")
        att_ready = sem("att_ready")
        att_hi_done = sem("att_hi_done")
        att_lo_done = sem("att_lo_done")

        tri_dram = nc.dram_tensor("tri_dram", (P, 64 * 64), F32, kind="Internal").ap()
        inv_dram = nc.dram_tensor("inv_dram", (P, 64 * 64), F32, kind="Internal").ap()
        a_dram = nc.dram_tensor("a_dram", (P, DT * T), F32, kind="Internal").ap()
        v_dram = nc.dram_tensor("v_dram", (P, DT, T), F32, kind="Internal").ap()
        bonus_dram = nc.dram_tensor("bonus_dram", (P, DT, T), F32, kind="Internal").ap()

        def stacked(dram, g0, n):
            return dram[2 * g0:2 * (g0 + n), :].rearrange("(g h) (s t) -> g (h s) t", h=2, s=64).rearrange("g r t -> r g t")

        def flat(ap):
            return ap.rearrange("p a t -> p (a t)")

        def param4(name, i, k):
            r, _ = PARAM_ROWS[name]
            if isinstance(i, int):
                return prm[:, r + 4 * i + k:r + 4 * i + k + 1]
            return prm[:, bass.ds(4 * i + (r + k), 1)]

        def lora_sp(sp, n, down, up):
            k = down.shape[1]
            load_unit(sp, n, down.rearrange("(kt p) n -> p kt n", p=P), (DT, k), after_short=True)
            load_unit(sp, n + 1, up.rearrange("p (a n) -> p a n", a=1), (1, D), parts=k, after_short=True)

        def rwkv_sp(sp):
            lora_sp(sp, n_dec, rw_w1[0], rw_w2[0])
            lora_sp(sp, n_rate, rw_a1[0], rw_a2[0])
            for name in ("key", "rec", "val"):
                w = rw_w_rkv[0, W_ROW[name]].rearrange("(kt p) n -> p kt n", p=P)
                with sp.Fori(0, 4) as i:
                    for u in range(4):
                        load_unit(sp, units[name] + u, w[:, 4 * u:4 * u + 4, bass.ds(i * 512, 512)], (4, 512), off=4 * i,
                                  after_short=name == "key")
            g1 = rw_g1[0].rearrange("(kt p) n -> p kt n", p=P)
            g2 = rw_g2[0].rearrange("(kt p) n -> p kt n", p=P)
            for u in range(2):
                load_unit(sp, n_gate + u, g1[:, 8 * u:8 * u + 8, :], (8, GLORA))
            for u in range(2):
                load_unit(sp, n_gate + 2 + u, g2[:, u:u + 1, :], (1, D))
            out_sp(sp, "rw_out", rw_w_o[0].rearrange("(kt p) n -> p kt n", p=P), DT)

        POOL_DIFFS = ("rate", "key")

        def diff_pool(pool):
            pool.wait_ge(h_ready, 4)
            for n in (4, 5, 8, 9):
                j = n % 4
                pool.wait_ge(hn_lo, n - 1)
                nc.gpsimd.tensor_tensor(work[:, j % 2], h_in[:, 4 * j:4 * j + 4, 0:T], h_in[:, 4 * j:4 * j + 4, 1:T + 1],
                                        ALU.subtract).then_inc(mix_diff, 1)

        def mixed_dve(dve, name):
            i, mu = fill_of[name], MU[name]

            def group(j):
                if i == 0:
                    for k in range(4 * j, 4 * j + 4):
                        last = nc.vector.scalar_tensor_tensor(out=h_in[:, k, 1:T + 1], in0=x_res[:, k],
                                                              scalar=param("norm_mix", k), in1=rstd[:], op0=ALU.mult,
                                                              op1=ALU.mult)
                    last.then_inc(h_ready, 1)
                    dve.wait_ge(h_ready, j + 1)
                if name not in POOL_DIFFS or j >= 2:
                    nc.vector.tensor_tensor(work[:, j % 2], h_in[:, 4 * j:4 * j + 4, 0:T],
                                            h_in[:, 4 * j:4 * j + 4, 1:T + 1], ALU.subtract).then_inc(mix_diff, 1)
                dve.wait_ge(mix_diff, 4 * i + j + 1)
                for k in range(4):
                    last = nc.vector.scalar_tensor_tensor(out=work[:, j % 2, k], in0=work[:, j % 2, k],
                                                          scalar=param("rw_mu", DT * mu + 4 * j + k),
                                                          in1=h_in[:, 4 * j + k, 1:T + 1], op0=ALU.mult, op1=ALU.add)
                return last

            def after_group(j):
                if j == 1 and name == "rec":
                    prep_dve(dve, 2, 1)
                if j == 1 and name == "rate":
                    split_lo(dve, n_rate, width=DT * LORA)
                if j == 2 and name in ("key", "rec", "val", "gate"):
                    split_lo(dve, units[name])

            fill_dve(dve, i, group, after_group)
            if name in ("key", "rec", "val", "gate"):
                split_lo(dve, units[name] + 1)

        def take_block(act, name, i, dst, done):
            act.wait_ge(unit_used, units[name] + 4 + 4 * i)
            nc.scalar.activation(two_banks(dst), block_banks(i), ACT.Copy).then_inc(done, 1)

        def mixed_act(act, name):
            def before_group(j):
                act.wait_ge(unit_used, units[name] - 3 + j)

            def after_group(j):
                if j == 1:
                    split_hi(act, units[name])
                if j == 2 and name == "rec":
                    take_block(act, "key", 3, quad[:, SLOT_K, 12:16, :], block_free)
                if j == 3:
                    split_hi(act, units[name] + 1)

            fill_act(act, fill_of[name], before_group, after_group)

        def lora_pe(pe, name, n, which):
            if which:
                pe.wait_ge(sig_done, 1)
            unit_product(pe, n, (DT, LORA), x_tiles(0, pe, fill_of[name]), lambda f: acc[0:LORA, 0, 0:T], True, True)
            if which:
                pe.wait_ge(sig_done, 4 * which)
            pe.wait_ge(lora_lo_done, which + 1)
            unit_product(pe, n + 1, (1, D), lambda k: (lora_hi[0:LORA, 0, :], lora_lo[0:LORA, 0, :]),
                         lambda f: bank_tile(0, f), True, True, parts=LORA)

        def lora_split_act(act, dst, src, which):
            act.wait_ge(lora_act, which + 1)
            nc.scalar.activation(dst, src, ACT.Copy).then_inc(lora_hi_done, 1)

        def lora_mid_act(act, n, which, func):
            act.wait_ge(unit_used, n + 1)
            src = lora_mid[0:LORA]
            nc.scalar.activation(flat(src), acc[0:LORA, 0, 0:T], func).then_inc(lora_act, 1)
            lora_split_act(act, lora_hi[0:LORA], src, which)

        def sigmoids(act, n, bias_name, slot, j):
            act.wait_ge(unit_used, n + 2)
            for kt in range(4 * j, 4 * j + 4):
                ins = nc.scalar.activation(quad[:, slot, kt, :], bank_tile(0, kt), ACT.Sigmoid, bias=param(bias_name, kt))
            ins.then_inc(sig_done, 1)

        def lora_split_dve(dve, lo, hi, src, which):
            dve.wait_ge(lora_hi_done, which + 1)
            nc.vector.tensor_tensor(lo, src, hi.bitcast(F32), ALU.subtract).then_inc(lora_lo_done, 1)

        def block_pe(pe, name, i, after=None, inside=None):
            pe.wait_ge(block_free, BLOCKS_BEFORE[name] + i)
            for u in range(4):
                pe.wait_ge(hn_lo, 4 * fill_of[name] + u + 1)
                bank = (i % 2) * 2
                unit_product(pe, units[name] + u, (4, 512), x_tiles(4 * u), lambda f: bank_tile(bank, f), u == 0,
                             u == 3, off=4 * i)
                if u == after:
                    inside()

        def block_banks(i):
            return acc[:, bass.ds((i % 2) * 2, 2), :]

        def prep_act(act, i, part):
            tiles = bass.ds(4 * i, 4)
            if part == 0:
                act.wait_ge(kk_raw, 1 + i)
                nc.scalar.activation(prep_x[:, 1], prep_x[:, 0], ACT.Square).then_inc(kk_sq, 1)
            elif part == 1:
                act.wait_ge(kk_step, 3 * i + 1)
                nc.scalar.activation(prep_x[:, 1], prep_x[:, 1], ACT.Ln).then_inc(kk_root, 1)
                act.wait_ge(kk_root, 2 * i + 2)
                nc.scalar.activation(prep_x[:, 1], prep_x[:, 1], ACT.Exp, scale=-0.5).then_inc(kk_root, 1)
                act.wait_ge(prep_done, 1 + i)
                nc.scalar.activation(prep_inv[:], quad[:, SLOT_R, tiles, :], ACT.Exp,
                                     scale=DECAY_SCALE).then_inc(decayed, 1)
            else:
                act.wait_ge(cum_gap, 1 + i)
                act.wait_ge(decayed, 3 * i + 1)
                nc.scalar.activation(quad[:, SLOT_A, tiles, :], quad[:, SLOT_A, tiles, :], ACT.Exp,
                                     scale=-DECAY_SCALE).then_inc(decayed, 1)
                nc.scalar.activation(quad[:, SLOT_R, tiles, :], quad[:, SLOT_R, tiles, :], ACT.Exp,
                                     scale=-DECAY_SCALE).then_inc(decayed, 1)

        def prep_pe(pe, i):
            pe.wait_ge(kk_sq, 1 + i)
            pe.wait_ge(kk_root, 1 + 2 * i)
            for b in range(2):
                mm = nc.tensor.matmul(acc[:, 4 + b, :], const("head_ones"), flat(prep_x[:, 1, 2 * b:2 * b + 2]))
            mm.then_inc(kk_sum, 1)

        def prep_dve(dve, i, part):
            tiles = bass.ds(4 * i, 4)
            if part == 0:
                dve.wait_ge(kk_sum, 1 + i)
                nc.vector.tensor_scalar(two_banks(prep_x[:, 1]), acc[:, 4:6], 1e-24, None, ALU.max).then_inc(kk_step, 1)
            else:
                dve.wait_ge(kk_root, 2 * i + 3)
                nc.vector.tensor_tensor(prep_x[:, 0], prep_x[:, 0], prep_x[:, 1], ALU.mult).then_inc(kk_step, 1)
                dve.wait_ge(decayed, 3 * i + 2)
                dve.wait_ge(kk_step, 3 * i + 2)
                nc.vector.scalar_tensor_tensor(out=quad[:, SLOT_A, tiles, :], in0=prep_x[:, 0], scalar=-1.0,
                                               in1=quad[:, SLOT_A, tiles, :], op0=ALU.mult,
                                               op1=ALU.mult).then_inc(kk_step, 1)

        def prep_pool(pool):
            pool.wait_ge(sig_done, 8)
            pool.wait_ge(cum_done, 1)
            pool.wait_ge(k_rest_ready, 1)
            for i in range(4):
                tiles = slice(4 * i, 4 * i + 4)
                k_t, b_t, a_t, p_t = (quad[:, s, tiles, :] for s in (SLOT_K, SLOT_B, SLOT_A, SLOT_R))
                pool.wait_ge(block_free, 2 + i)
                for k in range(4):
                    last = nc.gpsimd.tensor_scalar(prep_x[:, 0, k], flat(quad[:, SLOT_K, 4 * i + k:4 * i + k + 1, :]),
                                                   param4("rw_k_k", i, k), None, ALU.mult)
                last.then_inc(kk_raw, 1)
                nc.gpsimd.tensor_tensor(a_t, p_t, a_t, ALU.subtract).then_inc(cum_gap, 1)
                for k in range(4):
                    rest = K_A_REST + 4 * i + k
                    last = nc.gpsimd.tensor_scalar(prep_t[:, k], quad[:, SLOT_B, 4 * i + k, :], param4("rw_k_a", i, k),
                                                   prm[:, rest:rest + 1], ALU.mult, ALU.add)
                last.then_inc(prep_step, 1)
                pool.wait_ge(prep_step, 4 * i + 1)
                nc.gpsimd.tensor_tensor(prep_t[:], prep_t[:], k_t, ALU.mult).then_inc(prep_step, 1)
                pool.wait_ge(kk_step, 3 * i + 3)
                nc.gpsimd.tensor_tensor(prep_x[:, 0], prep_x[:, 0], b_t, ALU.mult).then_inc(prep_step, 1)
                pool.wait_ge(decayed, 3 * i + 3)
                nc.gpsimd.tensor_copy(chunk_decay[:, tiles, :], quad[:, SLOT_R, tiles, CHUNK - 1:T:CHUNK])
                pool.wait_ge(prep_step, 4 * i + 3)
                nc.gpsimd.tensor_tensor(b_t, prep_x[:, 0], prep_inv[:], ALU.mult)
                nc.gpsimd.tensor_tensor(k_t, prep_t[:], prep_inv[:], ALU.mult).then_inc(prep_step, 1)
                pool.wait_ge(prep_step, 4 * i + 4)
                pool.sem_inc(prep_done, 1)

        def rk_pe(pe, i):
            pe.wait_ge(rk_done, 1 + i)
            for b in range(2):
                mm = nc.tensor.matmul(acc[:, 4 + b, :], const("head_ones"), flat(rk_t[:, 2 * b:2 * b + 2]))
            mm.then_inc(rk_sum, 1)

        def tri_pool(pool):
            pool.wait_ge(tables_in, table_loads)
            mask = const("pair_mask").rearrange("p (a h b) -> p a h b", a=1, b=1).to_broadcast([P, NC, 2, 64])
            pool.wait_ge(prep_done, 1 + 4)
            pool.dma_start(a_dram, flat(quad[:, SLOT_A])).then_inc(a_stored, 16)
            for p in range(PAIRS):
                if p >= 2:
                    pool.wait_ge(tri_mm, p - 1)
                src = quad[:, SLOT_B, p, :].rearrange("p (c a t) -> p c a t", c=NC, a=1).to_broadcast([P, NC, 2, 64])
                nc.gpsimd.tensor_tensor(b_wide[:, p % 2], src, mask, ALU.mult).then_inc(b_wide_done, 1)

        def tri_act(act):
            for q in range(PAIRS // 4):
                act.wait_ge(tri_masked, 4 * q + 4)
                rows = tri_rows[:, 4 * (q % 2):4 * (q % 2) + 4].rearrange("p a c t -> p (a c) t")
                act.dma_start(stacked(tri_dram, 4 * NC * q, 4 * NC), rows).then_inc(tri_stored[q % 2], 16)

        def tri_pe(pe):
            pe.wait_ge(kk_root, 1 + 8)
            for p in range(PAIRS):
                pe.wait_ge(b_wide_done, p + 1)
                if p >= 2:
                    pe.wait_ge(tri_masked, p - 1)
                for c in range(NC):
                    mm = nc.tensor.matmul(acc[:, 4 + p % 2, 64 * c:64 * c + 64], b_wide[:, p % 2, c],
                                          quad[:, SLOT_A, p, 64 * c:64 * c + 64])
                mm.then_inc(tri_mm, 1)

        def tri_dve(dve):
            mask = const("strict_mask").rearrange("p (a t) -> p a t", a=1).to_broadcast([P, NC, 64])
            for p in range(PAIRS):
                dve.wait_ge(tri_mm, p + 1)
                if p >= 8 and p % 4 == 0:
                    dve.wait_ge(tri_stored[p // 4 % 2], 16 * (p // 8))
                nc.vector.tensor_tensor(tri_rows[:, p % 8],
                                        acc[:, 4 + p % 2, 0:NC * 64].rearrange("p (c t) -> p c t", c=NC), mask,
                                        ALU.mult).then_inc(tri_masked, 1)

        def solve_pool(pool):
            for stored in tri_stored:
                pool.wait_ge(stored, 2 * PAIRS)
            pool.dma_start(flat(tri[:]), tri_dram).then_inc(tri_loaded, 16)
            pool.wait_ge(a_stored, 16)
            pool.wait_ge(tri_loaded, 16)
            step = 0
            for u in range(1, 63):
                w = 63 - u
                t = solve_t[:, 0:u * w].rearrange("p (a b) -> p a b", a=u)
                nc.gpsimd.tensor_tensor(t, tri[:, 0:u, u:u + 1].to_broadcast([P, u, w]),
                                        tri[:, u:u + 1, u + 1:64].to_broadcast([P, u, w]), ALU.mult).then_inc(solve_step, 1)
                pool.wait_ge(solve_step, step + 1)
                nc.gpsimd.tensor_tensor(tri[:, 0:u, u + 1:64], tri[:, 0:u, u + 1:64], t, ALU.add).then_inc(solve_step, 1)
                step += 2
                pool.wait_ge(solve_step, step)
            nc.gpsimd.memset(flat(tri[:])[:, 0:4096:65], 1.0).then_inc(solve_step, 1)
            pool.wait_ge(solve_step, step + 1)
            pool.dma_start(inv_dram, flat(tri[:])).then_inc(inv_stored, 16)
            pool.dma_start(flat(quad[:, SLOT_A, 0:4]), a_dram[:, 0:4 * T]).then_inc(inv_loaded, 16)
            pool.wait_ge(inv_stored, 16)
            pool.dma_start(inv_t[:], stacked(inv_dram, 0, GROUPS)).then_inc(inv_loaded, 16)
            pool.wait_ge(inv_loaded, 32)

        def at(g, k):
            if isinstance(g, int):
                return (g + k) % PAIRS, (g + k) // PAIRS * CHUNK
            return (g + (PAIRS + k)) % PAIRS, (g + k) // PAIRS * CHUNK

        def part(ap3, pair, t0, n=CHUNK):
            if isinstance(pair, int):
                return ap3[:, pair, t0:t0 + n]
            return flat(ap3[:, bass.ds(pair, 1), bass.ds(t0, n)])

        def turns(eng, step, after=None):
            for g in range(8):
                step(g, 0, g)
            with eng.Fori(1, GROUPS // 8 - (1 if after else 0)) as it:
                for k in range(8):
                    step(8 * it, k, 8)
            if after:
                for g in range(GROUPS - 8, GROUPS):
                    step(g, 0, g)
                    after(g)
            for k in range(3):
                step(GROUPS, k, GROUPS + k)

        def scan_pool(pool):
            pool.wait_ge(v_loaded, 32)
            pool.wait_ge(gate_out, 2)
            four = const("pair_mask").rearrange("p (a h b) -> p a h b", a=1, b=1).to_broadcast([P, 4, 2, 64])
            one = const("pair_mask").rearrange("p (h b) -> p h b", b=1).to_broadcast([P, 2, 64])

            def step(g, k, least):
                if isinstance(g, int) and g + k >= GROUPS:
                    return
                pair, t0 = at(g, k)
                slot = k if not isinstance(g, int) else (g + k) % 8
                if least >= 4:
                    pool.wait_ge(m_mm, g + (k - 3))
                if least >= 8:
                    pool.wait_ge(s_mm, g + (k - 7))
                if isinstance(pair, int):
                    src = quad[:, :, pair, t0:t0 + CHUNK].rearrange("p q (a t) -> p q a t", a=1)
                    v_src, i_src = v_feat[:, pair, t0:t0 + CHUNK], inv_t[:, pair * NC + t0 // CHUNK, :]
                else:
                    src = quad[:, :, bass.ds(pair, 1), bass.ds(t0, CHUNK)]
                    v_src = part(v_feat, pair, t0)
                    i_src = flat(inv_t[:, bass.ds(pair * NC + (g + k) // PAIRS, 1), :])
                nc.gpsimd.tensor_tensor(quad_wide[:, slot], src.to_broadcast([P, 4, 2, 64]), four, ALU.mult)
                nc.gpsimd.tensor_tensor(v_wide[:, slot % 4], v_src.rearrange("p (a t) -> p a t", a=1).to_broadcast([P, 2, 64]),
                                        one, ALU.mult)
                nc.gpsimd.tensor_tensor(inv_wide[:, slot], i_src.rearrange("p (a t) -> p a t", a=1).to_broadcast([P, 2, 64]),
                                        one, ALU.mult).then_inc(wide_done, 1)

            turns(pool, step)

        def scan_parts(g, k, least):
            out = []
            for lag in range(4):
                if isinstance(g, int):
                    here = 0 <= g + k - lag < GROUPS
                    out.append((k - lag, (g + k - lag) % 8, here))
                else:
                    out.append((k - lag, (k - lag) % 8, True))
            return out

        def scan_pe(pe):
            pe.wait_ge(state_zero, 1)
            pe.wait_ge(gate_out, 2)
            ident2 = const("ident2")

            def step(g, k, least):
                (k0, s0, on0), (k1, s1, on1), (k2, s2, on2), (k3, s3, on3) = scan_parts(g, k, least)
                if on0:
                    pair, t0 = at(g, k0)
                    bank = s0 % 2
                    pe.wait_ge(wide_done, g + k0 + 1)
                    if least >= 2:
                        pe.wait_ge(m_done, g + k0 - 1)
                        pe.wait_ge(kbv_done, g + k0 - 1)
                    if isinstance(pair, int):
                        ar = quad[:, SLOT_A:SLOT_R + 1, pair, t0:t0 + CHUNK]
                    else:
                        ar = quad[:, SLOT_A:SLOT_R + 1, bass.ds(pair, 1), bass.ds(t0, CHUNK)].rearrange("p q a t -> p q (a t)")
                    for n in (SLOT_K, SLOT_B):
                        nc.tensor.matmul(acc[:, bank, P * n:P * n + P].rearrange("p (q t) -> p q t", q=2),
                                         quad_wide[:, s0, n], ar, skip_group_check=True)
                    for n in (SLOT_K, SLOT_B):
                        nc.tensor.transpose(acc[:, 2 + bank, P * n:P * n + P], flat(quad_wide[:, s0, n]), ident)
                    nc.tensor.matmul(acc[:, 2 + bank, 2 * P:2 * P + 64], v_wide[:, s0 % 4], ident2,
                                     skip_group_check=True).then_inc(m_mm, 1)
                if on1:
                    pair, t0 = at(g, k1)
                    pe.wait_ge(m_done, g + k1 + 1)
                    pe.wait_ge(kbv_done, g + k1 + 1)
                    if not isinstance(g, int) or g + k1 >= 1:
                        pe.wait_ge(x_done, g + k1)
                    o = acc[:, 4, 0:64]
                    nc.tensor.matmul(o, quad_wide[:, s1, SLOT_A], part_state(pair), start=True, stop=False,
                                     skip_group_check=True)
                    nc.tensor.matmul(o, mix_wide[:, s1 % 4, 0], kbv_rows[:, s1 % 4, 2 * P:2 * P + 64], start=False, stop=True,
                                     skip_group_check=True).then_inc(x_mm, 1)
                if on2:
                    pe.wait_ge(x_done, g + k2 + 1)
                    if not isinstance(g, int) or g + k2 >= 1:
                        pe.wait_ge(u_done, g + k2)
                    nc.tensor.matmul(acc[:, 5, 0:64], inv_wide[:, s2], x_stack[:, s2 % 2],
                                     skip_group_check=True).then_inc(u_mm, 1)
                if on3:
                    pair, t0 = at(g, k3)
                    pe.wait_ge(u_done, g + k3 + 1)
                    if not isinstance(g, int) or g + k3 >= 1:
                        pe.wait_ge(y_taken, g + k3)
                    o = acc[:, 6, 0:64]
                    nc.tensor.matmul(o, quad_wide[:, s3, SLOT_R], part_state(pair), start=True, stop=False,
                                     skip_group_check=True)
                    nc.tensor.matmul(o, mix_wide[:, s3 % 4, 1], kbv_rows[:, s3 % 4, 2 * P:2 * P + 64], start=False, stop=False,
                                     skip_group_check=True)
                    nc.tensor.matmul(o, mix_wide[:, s3 % 4, 2], u_stack[:, s3 % 2], start=False, stop=True,
                                     skip_group_check=True).then_inc(y_mm, 1)
                    if not isinstance(g, int) or g + k3 >= 1:
                        pe.wait_ge(s_done, g + k3)
                    o = acc[:, 7, 0:64]
                    nc.tensor.matmul(o, kbv_rows[:, s3 % 4, 0:P], kbv_rows[:, s3 % 4, 2 * P:2 * P + 64], start=True, stop=False,
                                     skip_group_check=True)
                    nc.tensor.matmul(o, kbv_rows[:, s3 % 4, P:2 * P], u_stack[:, s3 % 2], start=False, stop=True,
                                     skip_group_check=True).then_inc(s_mm, 1)

            turns(pe, step)

        def part_state(pair):
            return state[:, pair, :] if isinstance(pair, int) else flat(state[:, bass.ds(pair, 1), :])

        def scan_act(act, after):
            def step(g, k, least):
                (k0, s0, on0), (k1, s1, on1), (k2, s2, on2), (k3, s3, on3) = scan_parts(g, k, least)
                if on0:
                    act.wait_ge(m_mm, g + k0 + 1)
                    if least >= 4:
                        act.wait_ge(s_mm, g + k0 - 3)
                    nc.scalar.activation(kbv_rows[:, s0 % 4], acc[:, 2 + s0 % 2, 0:2 * P + 64], ACT.Copy).then_inc(kbv_done, 1)
                if on2:
                    pair, t0 = at(g, k2)
                    act.wait_ge(u_mm, g + k2 + 1)
                    nc.scalar.activation(u_stack[:, s2 % 2], acc[:, 5, 0:64], ACT.Copy).then_inc(u_done, 1)
                    if isinstance(pair, int):
                        dec = chunk_decay[:, pair, t0 // CHUNK:t0 // CHUNK + 1]
                    else:
                        dec = flat(chunk_decay[:, bass.ds(pair, 1), bass.ds((g + k2) // PAIRS, 1)])
                    nc.scalar.activation(state_dec[:, s2 % 4], part_state(pair), ACT.Copy, scale=dec).then_inc(dec_done, 1)
                if on3:
                    pair, t0 = at(g, k3)
                    act.wait_ge(y_mm, g + k3 + 1)
                    if isinstance(pair, int):
                        o = y_all[:, pair, t0 // CHUNK, :]
                    else:
                        o = y_all[:, bass.ds(pair, 1), bass.ds((g + k3) // PAIRS, 1), :].rearrange("p a b t -> p (a b t)")
                    nc.scalar.activation(o, acc[:, 6, 0:64], ACT.Copy).then_inc(y_taken, 1)

            act.wait_ge(state_zero, 1)
            turns(act, step, after)

        def scan_dve(dve, after):
            masks = const("chunk_mask").rearrange("p (q h t) -> p q h t", q=2, h=2)

            def step(g, k, least):
                (k0, s0, on0), (k1, s1, on1), (k2, s2, on2), (k3, s3, on3) = scan_parts(g, k, least)
                if on0:
                    dve.wait_ge(m_mm, g + k0 + 1)
                    if least >= 4:
                        dve.wait_ge(s_mm, g + k0 - 3)
                    m1 = acc[:, s0 % 2, 0:P].rearrange("p (q a t) -> p q a t", q=2, a=1).to_broadcast([P, 2, 2, 64])
                    nc.vector.tensor_tensor(mix_wide[:, s0 % 4, 0:2], m1, masks, ALU.mult)
                    m2 = acc[:, s0 % 2, P + 64:T].rearrange("p (a t) -> p a t", a=1).to_broadcast([P, 2, 64])
                    nc.vector.tensor_tensor(mix_wide[:, s0 % 4, 2], m2, masks[:, 1], ALU.mult).then_inc(m_done, 1)
                if on1:
                    dve.wait_ge(x_mm, g + k1 + 1)
                    nc.vector.tensor_copy(x_stack[:, s1 % 2], acc[:, 4, 0:64]).then_inc(x_done, 1)
                if on3:
                    pair, t0 = at(g, k3)
                    dve.wait_ge(s_mm, g + k3 + 1)
                    dve.wait_ge(dec_done, g + k3 + 1)
                    if isinstance(pair, int):
                        dec = chunk_decay[:, pair, t0 // CHUNK:t0 // CHUNK + 1]
                    else:
                        dec = flat(chunk_decay[:, bass.ds(pair, 1), bass.ds((g + k3) // PAIRS, 1)])
                    nc.vector.scalar_tensor_tensor(out=part_state(pair), in0=acc[:, 7, 0:64], scalar=dec,
                                                   in1=state_dec[:, s3 % 4], op0=ALU.mult, op1=ALU.add).then_inc(s_done, 1)

            turns(dve, step, after)

        def y_groups(j):
            return y_all[:, 4 * j:4 * j + 4].rearrange("p a c v -> p (a c) v"), slice(16 * j, 16 * j + 16)

        def y_out(engine, p):
            src = y_all[:, p].rearrange("p c (a v) -> p c a v", a=1).to_broadcast([P, NC, 2, 64])
            factor = y_scale[:, NC * p:NC * p + NC].rearrange("p c (h a) -> p c h a", a=1)
            return engine.tensor_tensor(y_wide[:, p % 4], src, factor.to_broadcast([P, NC, 2, 64]), ALU.mult)

        def scan_finish_dve(dve):
            pm = const("pair_mask")
            step = 0

            def then(ins):
                nonlocal step
                step += 1
                ins.then_inc(ln_step, 1)
                dve.wait_ge(ln_step, step)

            def centre(j):
                dve.wait_ge(y_taken, GROUPS - PAIRS + 4 * j + 4)
                y, st = y_groups(j)
                then(nc.vector.tensor_reduce(y_mean[:, st], y, AX_X, ALU.add))
                then(nc.vector.tensor_scalar(y_mean[:, st], y_mean[:, st], 1.0 / RW_HEAD, None, ALU.mult))
                mean = y_mean[:, st].rearrange("p (g a) -> p g a", a=1).to_broadcast([P, 16, 64])
                nc.vector.tensor_tensor(y, y, mean, ALU.subtract).then_inc(ln_centred, 1)

            def variance(j):
                st = y_groups(j)[1]
                dve.wait_ge(ln_sq, j + 1)
                sq = flat(att[:, 4 * j:4 * j + 4]).rearrange("p (g v) -> p g v", v=64)
                then(nc.vector.tensor_reduce(y_inv[:, st], sq, AX_X, ALU.add))
                then(nc.vector.tensor_scalar(y_inv[:, st], y_inv[:, st], 1.0 / RW_HEAD, RW_GN_EPS, ALU.mult, ALU.add))
                nc.vector.reciprocal(y_inv[:, st], y_inv[:, st]).then_inc(ln_var, 1)

            def scale(j):
                st = y_groups(j)[1]
                dve.wait_ge(ln_root, j + 1)
                inv = y_inv[:, st].rearrange("p (g a) -> p g a", a=1).to_broadcast([P, 16, 2])
                nc.vector.tensor_tensor(y_scale[:, st], inv, pm.rearrange("p (a h) -> p a h", a=1).to_broadcast([P, 16, 2]),
                                        ALU.mult).then_inc(ln_scale, 1)

            def wide(j):
                for p in range(4 * j, 4 * j + 2):
                    if p >= 4:
                        dve.wait_ge(yt_mm, p - 3)
                    dve.wait_ge(ln_scale, j + 1)
                    y_out(nc.vector, p).then_inc(y_wide_first, 1)

            def gain(j):
                dve.wait_ge(yt_mm, 4 * j + 4)
                for q in range(4):
                    p = 4 * j + q
                    last = nc.vector.tensor_scalar(att[:, p], bank_tile(2 * (j % 2), q), param("rw_ln_w", p),
                                                   param("rw_ln_b", p), ALU.mult, ALU.add)
                last.then_inc(att_gain, 1)

            def low(j):
                dve.wait_ge(att_hi_done, j + 1)
                nc.vector.tensor_tensor(att_lo[:, 4 * j:4 * j + 4], att[:, 4 * j:4 * j + 4],
                                        att_hi[:, 4 * j:4 * j + 4].bitcast(F32), ALU.subtract).then_inc(att_lo_done, 1)

            def after(g):
                if g == GROUPS - 7:
                    centre(0)
                if g == GROUPS - 5:
                    centre(1)
                if g == GROUPS - 3:
                    variance(0)
                if g == GROUPS - 1:
                    variance(1)

            scan_dve(dve, after)
            dve.wait_ge(s_done, GROUPS)
            split_lo(dve, units["rw_out"])
            for turn in range(2, 8):
                if turn < 4:
                    centre(turn)
                if 3 <= turn < 5:
                    variance(turn - 1)
                if 2 <= turn < 6:
                    scale(turn - 2)
                    wide(turn - 2)
                if 3 <= turn < 7:
                    gain(turn - 3)
                if turn == 4:
                    split_lo(dve, units["rw_out"] + 1)
                if turn >= 4:
                    low(turn - 4)

        def finish_pool(pool):
            def wide(j):
                pool.wait_ge(ln_scale, j + 1)
                for p in range(4 * j + 2, 4 * j + 4):
                    if p >= 4:
                        pool.wait_ge(yt_mm, p - 3)
                    y_out(nc.gpsimd, p).then_inc(y_wide_done, 1)

            def gate(j):
                pool.wait_ge(att_gain, j + 1)
                t = slice(4 * j, 4 * j + 4)
                nc.gpsimd.tensor_tensor(att[:, t], att[:, t], bonus[:, t], ALU.add).then_inc(att_bonus, 1)
                pool.wait_ge(att_bonus, j + 1)
                nc.gpsimd.tensor_tensor(att[:, t], att[:, t], out_gate[:, t], ALU.mult).then_inc(att_ready, 1)

            pool.wait_ge(s_mm, GROUPS)
            pool.wait_ge(bonus_loaded, 16)
            for j in range(4):
                wide(j)
                if j >= 1:
                    gate(j - 1)
            gate(3)

        def scan_finish_act(act):
            def square(j):
                act.wait_ge(ln_centred, j + 1)
                nc.scalar.activation(flat(att[:, 4 * j:4 * j + 4]),
                                     y_all[:, 4 * j:4 * j + 4].rearrange("p a c v -> p (a c v)"),
                                     ACT.Square).then_inc(ln_sq, 1)

            def root(j):
                act.wait_ge(ln_var, j + 1)
                nc.scalar.activation(y_inv[:, 16 * j:16 * j + 16], y_inv[:, 16 * j:16 * j + 16],
                                     ACT.Sqrt).then_inc(ln_root, 1)

            def after(g):
                if g == GROUPS - 5:
                    square(0)
                if g == GROUPS - 3:
                    square(1)

            scan_act(act, after)
            act.wait_ge(s_mm, GROUPS)
            act.dma_start(bonus[:], bonus_dram).then_inc(bonus_loaded, 16)
            root(0)
            root(1)
            split_hi(act, units["rw_out"])
            square(2)
            root(2)
            square(3)
            split_hi(act, units["rw_out"] + 1)
            root(3)
            for j in range(4):
                act.wait_ge(att_ready, j + 1)
                nc.scalar.activation(att_hi[:, 4 * j:4 * j + 4], att[:, 4 * j:4 * j + 4], ACT.Copy).then_inc(att_hi_done, 1)

        def finish_pe(pe):
            for p in range(PAIRS):
                if p % 4 < 2:
                    pe.wait_ge(y_wide_first, 2 * (p // 4) + p % 4 + 1)
                else:
                    pe.wait_ge(y_wide_done, 2 * (p // 4) + p % 4 - 1)
                if p >= 8 and p % 4 == 0:
                    pe.wait_ge(att_gain, p // 4 - 1)
                for c in range(NC):
                    o = bank_tile(2 * (p // 4 % 2), p % 4)
                    mm = nc.tensor.matmul(o[:, 64 * c:64 * c + 64], y_wide[:, p % 4, c], const("ident2"),
                                          skip_group_check=True)
                mm.then_inc(yt_mm, 1)

        def rwkv_pool(pool):
            diff_pool(pool)
            prep_pool(pool)
            tri_pool(pool)
            solve_pool(pool)
            scan_pool(pool)
            finish_pool(pool)

        def rwkv_pe(pe):
            norm_pe(pe, norm_of["rwkv"])
            lora_pe(pe, "decay", n_dec, 0)
            lora_pe(pe, "rate", n_rate, 1)
            pe.wait_ge(sig_done, 5)
            block_pe(pe, "key", 0)
            pe.wait_ge(sig_done, 8)
            with pe.Fori(1, 4) as i:
                block_pe(pe, "key", i, 1, lambda: prep_pe(pe, i - 1))
            block_pe(pe, "rec", 0, 0, lambda: prep_pe(pe, 3))
            block_pe(pe, "rec", 1, 1, lambda: tri_pe(pe))
            with pe.Fori(2, 4) as i:
                block_pe(pe, "rec", i)
            pe.wait_ge(tri_masked, PAIRS)
            block_pe(pe, "val", 0)
            with pe.Fori(1, 4) as i:
                block_pe(pe, "val", i, 1, lambda: rk_pe(pe, i - 1))
            for u in range(2):
                if u == 0:
                    pe.wait_ge(block_free, 12)
                unit_product(pe, n_gate + u, (8, GLORA), x_tiles(8 * u, pe, fill_of["gate"]), lambda f: bank_tile(0, f),
                             u == 0, u == 1)
            rk_pe(pe, 3)
            pe.wait_ge(block_free, 13)
            pe.wait_ge(bonus_done, 1 + 4)
            pe.wait_ge(lora_lo_done, 3)
            for u in range(2):
                unit_product(pe, n_gate + 2 + u, (1, D), lambda k: (glora_hi[:, u, :], glora_lo[:, u, :]),
                             lambda f: bank_tile(0, f), u == 0, u == 1)
            pe.wait_ge(gate_out, 2)
            pe.wait_ge(inv_stored, 16)
            for _ in range(14):
                nc.tensor.matmul(acc[:, 7, :], ident, tab[:, 0:512])
            scan_pe(pe)
            finish_pe(pe)

            def before_block(b):
                if b == 0:
                    pe.wait_ge(att_lo_done, 3)
                else:
                    pe.wait_ge(att_lo_done, 4)

            out_pe(pe, "rw_out", att_hi, att_lo, DT, before_block, lambda: pe.wait_ge(att_lo_done, 4),
                   banks=(0, 4))

        def rwkv_act(act):
            act.sem_inc(block_free, 1)
            def early(u):
                if u == 0:
                    split_hi(act, n_dec, width=DT * LORA)
                else:
                    split_hi(act, n_dec + 1, parts=LORA)

            norm_act(act, norm_of["rwkv"], early)
            fill_act(act, fill_of["decay"])
            lora_mid_act(act, n_dec, 0, ACT.Tanh)

            def before_rate(j):
                act.wait_ge(unit_used, n_dec + 1)
                if j >= 2:
                    sigmoids(act, n_dec, "rw_w0", SLOT_A, 2 * j - 4)
                    sigmoids(act, n_dec, "rw_w0", SLOT_A, 2 * j - 3)

            split_hi(act, n_rate, width=DT * LORA)
            fill_act(act, fill_of["rate"], before_rate)
            split_hi(act, n_rate + 1, parts=LORA)
            lora_mid_act(act, n_rate, 1, ACT.Copy)

            def after_key(j):
                if j == 1:
                    split_hi(act, units["key"])

            fill_act(act, fill_of["key"], lambda j: act.wait_ge(unit_used, n_rate + 1), after_key)
            sigmoids(act, n_rate, "rw_a0", SLOT_B, 0)
            split_hi(act, units["key"] + 1)
            for j in range(1, 4):
                sigmoids(act, n_rate, "rw_a0", SLOT_B, j)

            def block(name, i, prep=None, take=False, tri=False):
                n0 = units[name]
                if not (isinstance(i, int) and i == 0):
                    split_hi(act, n0, 4 * i)
                    split_hi(act, n0 + 1, 4 * i)
                if take:
                    take_block(act, "key", i - 1, quad[:, SLOT_K, bass.ds(4 * i - 4, 4), :], block_free)
                split_hi(act, n0 + 2, 4 * i)
                if prep is not None:
                    prep_act(act, prep, 0)
                if tri:
                    tri_act(act)
                split_hi(act, n0 + 3, 4 * i)
                if prep is not None:
                    prep_act(act, prep, 1)
                    prep_act(act, prep, 2)

            block("key", 0)
            with act.Fori(1, 4) as i:
                block("key", i, i - 1, True)
            mixed_act(act, "rec")
            block("rec", 0, 3)
            block("rec", 1, tri=True)
            with act.Fori(2, 4) as i:
                block("rec", i)
            mixed_act(act, "val")

            def take_values(i):
                act.wait_ge(unit_used, units["val"] + 4 + 4 * i)
                act.wait_ge(val_stored, 16 + 16 * i)
                act.wait_ge(bonus_done, 1 + i)
                nc.scalar.activation(two_banks(val_t[:]), block_banks(i), ACT.Copy).then_inc(val_out, 1)
                act.wait_ge(val_out, 1 + i)
                act.sem_inc(block_free, 1)
                act.dma_start(v_dram[:, bass.ds(4 * i, 4), :], val_t[:]).then_inc(val_stored, 16)

            def store_bonus(i):
                act.wait_ge(bonus_done, 2 + i)
                act.dma_start(bonus_dram[:, bass.ds(4 * i, 4), :], rk_t[:]).then_inc(bonus_stored, 16)

            def val_block(i, behind):
                n0 = units["val"]
                if behind:
                    split_hi(act, n0, 4 * i)
                    split_hi(act, n0 + 1, 4 * i)
                    take_values(i - 1)
                split_hi(act, n0 + 2, 4 * i)
                split_hi(act, n0 + 3, 4 * i)
                if behind:
                    store_bonus(i - 1)

            val_block(0, False)
            act.wait_ge(a_stored, 16)
            with act.Fori(1, 4) as i:
                val_block(i, True)
            mixed_act(act, "gate")
            take_values(3)
            act.wait_ge(unit_used, n_gate + 2)
            nc.scalar.activation(flat(work[:, 1, 0:2]), acc[:, 0, :], ACT.Sigmoid).then_inc(lora_act, 1)
            lora_split_act(act, glora_hi[:], work[:, 1, 0:2], 2)
            split_hi(act, n_gate + 2)
            split_hi(act, n_gate + 3)
            store_bonus(3)
            act.wait_ge(val_stored, 16 + 64)
            act.dma_start(v_feat[:], v_dram).then_inc(v_loaded, 16)
            act.wait_ge(bonus_stored, 16 + 64)
            act.dma_start(flat(quad[:, SLOT_A, 4:DT]), a_dram[:, 4 * T:]).then_inc(v_loaded, 16)
            act.wait_ge(unit_used, n_gate + 4)
            nc.scalar.activation(out_gate[:, 0:8].rearrange("p a t -> p (a t)").rearrange("p (b s) -> p b s", b=4),
                                 acc[:, 0:4], ACT.Copy).then_inc(gate_out, 1)
            scan_finish_act(act)
            out_act(act, "rw_out", DT, 1)

        def rwkv_dve(dve):
            q = norm_of["rwkv"]
            dve.wait_ge(x_turned, 4)
            nc.vector.memset(h_in[:, :, 0:1], 0.0).then_inc(h_zero, 1)
            def early(u):
                if u == 0:
                    split_lo(dve, n_dec, width=DT * LORA)
                else:
                    split_lo(dve, n_dec + 1, parts=LORA)

            norm_dve(dve, q, early)
            dve.wait_ge(h_zero, 1)
            mixed_dve(dve, "decay")
            lora_split_dve(dve, lora_lo[0:LORA], lora_hi[0:LORA], lora_mid[0:LORA], 0)
            mixed_dve(dve, "rate")
            split_lo(dve, n_rate + 1, parts=LORA)
            lora_split_dve(dve, lora_lo[0:LORA], lora_hi[0:LORA], lora_mid[0:LORA], 1)
            mixed_dve(dve, "key")
            dve.wait_ge(sig_done, 4)
            for kt in range(DT):
                last = nc.vector.tensor_tensor_scan(quad[:, SLOT_R, kt], const("scan_mask"), quad[:, SLOT_A, kt], 0.0,
                                                    ALU.mult, ALU.add)
            last.then_inc(cum_done, 1)

            def block(name, i, prep=None, take=False, tri=False):
                n0 = units[name]
                if not (isinstance(i, int) and i == 0):
                    split_lo(dve, n0, 4 * i)
                    split_lo(dve, n0 + 1, 4 * i)
                if take:
                    receptance(i - 1)
                split_lo(dve, n0 + 2, 4 * i)
                if prep is not None:
                    prep_dve(dve, prep, 0)
                if tri:
                    tri_dve(dve)
                split_lo(dve, n0 + 3, 4 * i)

            def receptance(i):
                dve.wait_ge(unit_used, units["rec"] + 4 + 4 * i)
                dve.wait_ge(prep_done, 1 + 4)
                r = quad[:, SLOT_R, bass.ds(4 * i, 4), :]
                nc.vector.tensor_tensor(two_banks(r), block_banks(i), two_banks(r), ALU.mult).then_inc(block_free, 1)

            block("key", 0)
            with dve.Fori(1, 3) as i:
                block("key", i, i - 1)
                prep_dve(dve, i - 1, 1)
            block("key", 3, 2)
            mixed_dve(dve, "rec")
            block("rec", 0, 3)
            prep_dve(dve, 3, 1)
            block("rec", 1, None, True, tri=True)
            with dve.Fori(2, 4) as i:
                block("rec", i, None, True)
            mixed_dve(dve, "val")
            receptance(3)

            def rk(i):
                dve.wait_ge(block_free, 8)
                dve.wait_ge(bonus_stored, 16 + 16 * i)
                for k in range(4):
                    t = bass.ds(4 * i + k, 1)
                    last = nc.vector.scalar_tensor_tensor(out=rk_t[:, k], in0=flat(quad[:, SLOT_R, t, :]),
                                                          scalar=param4("rw_r_k", i, k), in1=flat(quad[:, SLOT_K, t, :]),
                                                          op0=ALU.mult, op1=ALU.mult)
                last.then_inc(rk_done, 1)

            def make_bonus(i):
                dve.wait_ge(rk_sum, 1 + i)
                dve.wait_ge(val_out, 1 + i)
                nc.vector.tensor_tensor(two_banks(rk_t[:]), acc[:, 4:6], two_banks(val_t[:]),
                                        ALU.mult).then_inc(bonus_done, 1)

            def val_block(i, behind):
                n0 = units["val"]
                if behind:
                    split_lo(dve, n0, 4 * i)
                    split_lo(dve, n0 + 1, 4 * i)
                    rk(i - 1)
                split_lo(dve, n0 + 2, 4 * i)
                split_lo(dve, n0 + 3, 4 * i)
                if behind:
                    make_bonus(i - 1)

            val_block(0, False)
            dve.wait_ge(a_stored, 16)
            with dve.Fori(1, 4) as i:
                val_block(i, True)
            mixed_dve(dve, "gate")
            rk(3)
            lora_split_dve(dve, glora_lo[:], glora_hi[:], work[:, 1, 0:2], 2)
            split_lo(dve, n_gate + 2)
            split_lo(dve, n_gate + 3)
            make_bonus(3)
            dve.wait_ge(unit_used, n_gate + 4)
            nc.vector.tensor_copy(out_gate[:, 8:16].rearrange("p a t -> p (a t)").rearrange("p (b s) -> p b s", b=4),
                                  acc[:, 4:8]).then_inc(gate_out, 1)
            nc.vector.memset(state[:], 0.0).then_inc(state_zero, 1)
            scan_finish_dve(dve)
            out_dve_then_up(dve, "rw_out", DT, 1, 0)

        norms = ["rwkv", "up0", "ret", "up1", "final"]
        norm_of = {name: q for q, name in enumerate(norms)}
        fills = ["decay", "rate", "key", "rec", "val", "gate", "up0", "ret", "up1"]
        fill_of = {name: i for i, name in enumerate(fills)}

        def normed_act(act, name):
            norm_act(act, norm_of[name], lambda u: split_hi(act, units[name] + u))
            fill_act(act, fill_of[name])

        def normed_dve(dve, name, gain, gain_tile):
            norm_dve(dve, norm_of[name], lambda u: split_lo(dve, units[name] + u))
            fill_dve(dve, fill_of[name], lambda j: norm_group(j, gain, gain_tile))

        param_pieces = []
        for name, src in (("norm_mix", norm_mix), ("norm_ffn", norm_ffn), ("norm_final", norm_final),
                          ("rw_mu", rw_mu), ("rw_w0", rw_w0), ("rw_a0", rw_a0), ("rw_k_k", rw_k_k),
                          ("rw_k_a", rw_k_a), ("rw_r_k", rw_r_k), ("rw_ln_w", rw_ln_w), ("rw_ln_b", rw_ln_b),
                          ("ret_gn_w", ret_gn_w)):
            r, n = PARAM_ROWS[name]
            merge = {1: None, 2: "a b -> (a b)", 3: "a b c -> (a b c)"}[len(src.shape)]
            rows = (src.rearrange(merge) if merge else src).rearrange("(r c) -> r c", c=P)
            done = 0
            while done < n:
                first, blk = (r + done) % P, (r + done) // P
                k = min(n - done, P - first)
                param_pieces.append((param_rows[first:first + k, blk, :], rows[done:done + k, :]))
                done += k
        table_loads = 16 * (1 + len(param_pieces))
        rows_of_block = [min(P, PARAM_ROWS["ret_gn_w"][0] + 2 * DT - P * b) for b in range(PARAM_BLOCKS)]

        block = ctx.enter_context(nc.Block())

        @block.sync
        def _(sp):
            sp.dma_start(x_rows[:], x_dram).then_inc(rows_in, 16)
            sp.dma_start(tab[:], table[:, 0:tab_cols]).then_inc(tables_in, 16)
            for dst, src in param_pieces:
                sp.dma_start(dst, src).then_inc(tables_in, 16)
            rwkv_sp(sp)
            for l in range(2):
                up_sp(sp, l)
                out_sp(sp, f"down{l}", w2s[l], FT)
                if l == 0:
                    ret_sp(sp)
                    out_sp(sp, "ret_out", ret_out, 2 * DT)
            for j in range(4):
                sp.wait_ge(out_ready, j + 1)
                sp.dma_start(out_dram[:, :, 512 * j:512 * j + 512],
                             out_rows[:, :, 512 * j:512 * j + 512]).then_inc(out_stored, 16)
            sp.wait_ge(out_stored, 64)

        @block.gpsimd
        def _(pool):
            rwkv_pool(pool)

        @block.scalar
        def _(act):
            rwkv_act(act)
            for l in range(2):
                up_act(act, l)
                out_act(act, f"down{l}", FT, 1)
                if l == 0:
                    normed_act(act, "ret")
                    rope_act(act)
                    ret_act(act)
                    out_act(act, "ret_out", 2 * DT, 3)
            norm_act(act, norm_of["final"])
            for j in range(4):
                act.wait_ge(out_turned, j + 1)
                nc.scalar.activation(out_rows[:, :, 512 * j:512 * j + 512], acc[:, 2 * (j % 2):2 * (j % 2) + 2],
                                     ACT.Copy).then_inc(out_ready, 1)

        @block.vector
        def _(dve):
            for started in (gated, ret_lo_done, y_rstd, y_var, hid_lo_done, kk_root, prep_done, bonus_done,
                            glu_done):
                dve.sem_inc(started, 1)
            dve.sem_inc(val_stored, 16)
            dve.sem_inc(bonus_stored, 16)
            dve.sem_inc(up_free, 2)
            for b in range(PARAM_BLOCKS):
                dve.wait_ge(params_t, PARAM_BLOCKS)
                k = rows_of_block[b]
                nc.vector.tensor_copy(prm[:, P * b:P * b + k], acc[:, 6, P * b:P * b + k]).then_inc(params_ready, 1)
            for j in range(4):
                dve.wait_ge(x_turned, j + 1)
                nc.vector.tensor_copy(two_banks(x_res[:, 4 * j:4 * j + 4]),
                                      acc[:, 2 * (j % 2):2 * (j % 2) + 2]).then_inc(x_ready, 1)
            dve.wait_ge(params_ready, PARAM_BLOCKS)
            k_a, _ = PARAM_ROWS["rw_k_a"]
            nc.vector.tensor_scalar(prm[:, K_A_REST:K_A_REST + DT], prm[:, k_a:k_a + DT], -1.0, 1.0, ALU.mult,
                                    ALU.add).then_inc(k_rest_ready, 1)
            rwkv_dve(dve)
            for l in range(2):
                up_dve(dve, l)
                out_dve(dve, f"down{l}", FT, 1)
                if l == 0:
                    normed_dve(dve, "ret", "norm_mix", DT)
                    rope_dve(dve)
                    ret_dve(dve)
                    out_dve_then_up(dve, "ret_out", 2 * DT, 3, 1)
            norm_dve(dve, norm_of["final"])
            for j in range(4):
                if j >= 2:
                    dve.wait_ge(out_turned, j - 1)
                norm_group(j, "norm_final", 0).then_inc(hn_ready, 1)

        @block.tensor
        def _(pe):
            pe.wait_ge(tables_in, table_loads)
            for b in range(PARAM_BLOCKS):
                k = rows_of_block[b]
                mm = nc.tensor.transpose(acc[:, 6, P * b:P * b + k], param_rows[0:k, b, :], ident[0:k, 0:k])
                mm.then_inc(params_t, 1)
            pe.wait_ge(rows_in, 16)
            for j in range(4):
                if j >= 2:
                    pe.wait_ge(x_ready, j - 1)
                for k in range(4):
                    for tt in range(2):
                        mm = nc.tensor.transpose(bank_tile(2 * (j % 2), k)[:, P * tt:P * tt + P],
                                                 x_rows[:, tt, P * (4 * j + k):P * (4 * j + k) + P], ident)
                mm.then_inc(x_turned, 1)
            rwkv_pe(pe)
            for l in range(2):
                up_pe(pe, l, fill_of[f"up{l}"])
                down_pe(pe, l)
                if l == 0:
                    norm_pe(pe, norm_of["ret"])
                    last_sums = ret_pe(pe, fill_of["ret"])

                    def before_block(b):
                        if b == 0:
                            pe.wait_ge(rot_done, RET_HEADS)
                            pe.wait_ge(v_evac, RET_HEADS)
                            pe.wait_ge(ret_lo_done, 1 + RET_HEADS - 1)
                        else:
                            pe.wait_ge(y_var, 1 + RET_HEADS)
                            pe.wait_ge(silu_g_done, RET_HEADS)

                    out_pe(pe, "ret_out", ret_hi, ret_lo, 2 * DT, before_block,
                           lambda: pe.wait_ge(ret_lo_done, 1 + RET_HEADS), banks=(0, 4), after_pair=last_sums)
            norm_pe(pe, norm_of["final"])
            for j in range(4):
                pe.wait_ge(hn_ready, 4 * len(fills) + j + 1)
                if j >= 2:
                    pe.wait_ge(out_ready, j - 1)
                for tt in range(2):
                    for k in range(4):
                        mm = nc.tensor.transpose(acc[:, 2 * (j % 2) + tt, P * k:P * k + P],
                                                 work[:, j % 2, k, P * tt:P * tt + P], ident)
                mm.then_inc(out_turned, 1)


_INS = ['x', 'positions', 'norm_mix', 'norm_ffn', 'norm_final', 'rw_mu', 'rw_w_rkv', 'rw_w0', 'rw_w1', 'rw_w2',
        'rw_a0', 'rw_a1', 'rw_a2', 'rw_g1', 'rw_g2', 'rw_k_k', 'rw_k_a', 'rw_r_k', 'rw_ln_w', 'rw_ln_b', 'rw_w_o',
        'ret_w_in', 'ret_gn_w', 'ret_w_out', 'ffn_w1', 'ffn_w3', 'ffn_w2']


def kernel(**inputs):
    import concourse.bacc as _bacc
    from concourse.bass_utils import run_bass_kernel_spmd as _run

    nc = _bacc.Bacc("TRN2", target_bir_lowering=False, num_devices=1)
    arrays, args = {}, []
    for name in _INS:
        a = np.ascontiguousarray(inputs[name])
        arrays[f"in_{name}"] = a
        args.append(nc.dram_tensor(f"in_{name}", a.shape, mybir.dt.from_np(a.dtype), kind="ExternalInput").ap())
    arrays["shape_table"] = shape_table()
    args.append(nc.dram_tensor("shape_table", (P, TABLE_WIDTH), F32, kind="ExternalInput").ap())
    args.append(nc.dram_tensor("out_0", (1, T, D), F32, kind="ExternalOutput").ap())
    trunk_program(nc, *args)
    r = _run(nc, [arrays], core_ids=[0])
    return r.results[0]["out_0"]
```
